# Optimizing a Trainium2 kernel written in Bass

```python
import jax, jax.numpy as jnp
from jax import lax
import numpy as np

D_MODEL = 1024
BATCH = 1
SEQ = 256
DEPTH = 2

GRID_W = 64
NA_HEADS = 4
NA_HEAD_DIM = 64
NA_KH = 8
NA_KW = 16
NA_QB = 16
MLA_HEADS = 4
MLA_Q_LORA = 256
MLA_KV_LORA = 128
MLA_NOPE = 64
MLA_ROPE = 32
MLA_V = 64
GQA_HEADS = 8
GQA_KV_HEADS = 2
GQA_HEAD_DIM = 64
N_BRANCHES = 3
FFN_HIDDEN = -(-8 * D_MODEL // (3 * 256)) * 256
Q_BLOCK = 128
ROPE_THETA = 10000.0
AXIAL_THETA = 10000.0
NORM_EPS = 1e-6
N_MOD = 6


def _in_splits():
    return ([NA_HEADS * NA_HEAD_DIM] * 3
            + [MLA_Q_LORA, MLA_KV_LORA, MLA_ROPE]
            + [GQA_HEADS * GQA_HEAD_DIM, GQA_KV_HEADS * GQA_HEAD_DIM, GQA_KV_HEADS * GQA_HEAD_DIM]
            + [D_MODEL] * N_BRANCHES)

def _in_cols():
    return int(sum(_in_splits()))

def rms_norm(x, g):
    xf = x.astype(jnp.float32)
    y = xf * lax.rsqrt(jnp.mean(xf * xf, axis=-1, keepdims=True) + NORM_EPS)
    return (y * g.astype(jnp.float32)).astype(x.dtype)

def rope(x, pos, theta):
    d = x.shape[-1]
    half = d // 2
    inv_freq = 1.0 / (theta ** (jnp.arange(half, dtype=jnp.float32) / half))
    ang = pos[:, None] * inv_freq[None, :]
    ang = ang.reshape((ang.shape[0],) + (1,) * (x.ndim - 3) + (half,))
    cos, sin = jnp.cos(ang), jnp.sin(ang)
    xf = x.astype(jnp.float32)
    x1, x2 = xf[..., :half], xf[..., half:]
    return jnp.concatenate([x1 * cos - x2 * sin, x2 * cos + x1 * sin], axis=-1).astype(x.dtype)

def axial_rope(x, row, col):
    h = x.shape[-1] // 2
    return jnp.concatenate([rope(x[..., :h], row, AXIAL_THETA), rope(x[..., h:], col, AXIAL_THETA)], axis=-1)

def blocked_attention(q, k, v, scale):
    B, S, KVH, G, dk = q.shape
    dv = v.shape[-1]
    nb = S // Q_BLOCK
    qb = jnp.moveaxis(q.reshape(B, nb, Q_BLOCK, KVH, G, dk), 1, 0)

    def one_block(qi):
        s = jnp.einsum('bqkgd,bskd->bkgqs', qi, k, preferred_element_type=jnp.float32) * scale
        p = jax.nn.softmax(s, axis=-1)
        return jnp.einsum('bkgqs,bskd->bqkgd', p.astype(v.dtype), v)

    o = lax.map(one_block, qb)
    return jnp.moveaxis(o, 0, 1).reshape(B, S, KVH * G * dv)

def neighborhood_attention(q, k, v, rpb):
    B, S, H, d = q.shape
    rows = S // GRID_W
    kh = min(NA_KH, rows)
    kw = NA_KW
    n_cb = GRID_W // NA_QB
    band = NA_QB + kw
    scale = d ** -0.5
    qg = q.reshape(B, rows, GRID_W, H, d)
    kg = k.reshape(B, rows, GRID_W, H, d)
    vg = v.reshape(B, rows, GRID_W, H, d)

    cb_start = jnp.clip(jnp.arange(n_cb) * NA_QB - kw // 2, 0, GRID_W - band)
    band_cols = cb_start[:, None] + jnp.arange(band)[None, :]
    q_cols = (jnp.arange(n_cb) * NA_QB)[:, None] + jnp.arange(NA_QB)[None, :]
    win_start = jnp.clip(q_cols - kw // 2, 0, GRID_W - kw)
    bc = band_cols[:, None, :]
    col_valid = (bc >= win_start[..., None]) & (bc < win_start[..., None] + kw)
    col_off = jnp.clip(bc - q_cols[..., None], -(kw - 1), kw - 1) + (kw - 1)
    rpb_cols = rpb[:, :, col_off]

    def one_row(r):
        rs = jnp.clip(r - kh // 2, 0, rows - kh)
        k_rows = lax.dynamic_slice_in_dim(kg, rs, kh, axis=1)
        v_rows = lax.dynamic_slice_in_dim(vg, rs, kh, axis=1)
        k_band = k_rows[:, :, band_cols]
        v_band = v_rows[:, :, band_cols]
        q_row = lax.dynamic_index_in_dim(qg, r, axis=1, keepdims=False).reshape(B, n_cb, NA_QB, H, d)
        s = jnp.einsum('bnqhd,bknjhd->bhnqkj', q_row, k_band, preferred_element_type=jnp.float32) * scale
        row_off = rs + jnp.arange(kh) - r + (NA_KH - 1)
        bias = jnp.transpose(rpb_cols[:, row_off], (0, 2, 3, 1, 4))
        s = s + bias[None].astype(jnp.float32)
        s = jnp.where(col_valid[None, None, :, :, None, :], s, -jnp.inf)
        p = jax.nn.softmax(s.reshape(B, H, n_cb, NA_QB, kh * band), axis=-1)
        p = p.reshape(B, H, n_cb, NA_QB, kh, band)
        o = jnp.einsum('bhnqkj,bknjhd->bnqhd', p.astype(v.dtype), v_band)
        return o.reshape(B, GRID_W, H, d)

    out = lax.map(one_row, jnp.arange(rows))
    return jnp.moveaxis(out, 0, 1).reshape(B, S, H * d)

def hybrid_layer(x, c, ada_w, ada_b, norm_mix_g, norm_ffn_g, w_in, na_rpb,
                 mla_q_norm_g, mla_kv_norm_g, mla_w_uq, mla_w_ukv, gqa_q_norm_g, gqa_k_norm_g,
                 w_br_na, w_br_mla, w_br_gqa, w_out, ffn_w_gate_up, ffn_w_down, pos_t, pos_row, pos_col):
    B, S, D = x.shape
    mod = jax.nn.silu(c) @ ada_w + ada_b
    sh_m, sc_m, g_m, sh_f, sc_f, g_f = [m[:, None, :] for m in jnp.split(mod, N_MOD, axis=-1)]

    h = rms_norm(x, norm_mix_g) * (1 + sc_m) + sh_m
    proj = h @ w_in
    idx = [int(i) for i in np.cumsum(_in_splits())[:-1]]
    (qa, ka, va, cq, ckv, kr, qc, kc, vc, ga, gb, gc) = jnp.split(proj, idx, axis=-1)

    o_na = neighborhood_attention(qa.reshape(B, S, NA_HEADS, NA_HEAD_DIM),
                                  ka.reshape(B, S, NA_HEADS, NA_HEAD_DIM),
                                  va.reshape(B, S, NA_HEADS, NA_HEAD_DIM), na_rpb)

    q_b = (rms_norm(cq, mla_q_norm_g) @ mla_w_uq).reshape(B, S, MLA_HEADS, MLA_NOPE + MLA_ROPE)
    q_nope, q_pe = q_b[..., :MLA_NOPE], rope(q_b[..., MLA_NOPE:], pos_t, ROPE_THETA)
    kv_b = (rms_norm(ckv, mla_kv_norm_g) @ mla_w_ukv).reshape(B, S, MLA_HEADS, MLA_NOPE + MLA_V)
    k_nope, v_b = kv_b[..., :MLA_NOPE], kv_b[..., MLA_NOPE:]
    k_pe = jnp.broadcast_to(rope(kr, pos_t, ROPE_THETA)[:, :, None, :], (B, S, MLA_HEADS, MLA_ROPE))
    q_full = jnp.concatenate([q_nope, q_pe], axis=-1)[:, :, :, None, :]
    k_full = jnp.concatenate([k_nope, k_pe], axis=-1)
    o_mla = blocked_attention(q_full, k_full, v_b, (MLA_NOPE + MLA_ROPE) ** -0.5)

    q_c = axial_rope(rms_norm(qc.reshape(B, S, GQA_HEADS, GQA_HEAD_DIM), gqa_q_norm_g), pos_row, pos_col)
    k_c = axial_rope(rms_norm(kc.reshape(B, S, GQA_KV_HEADS, GQA_HEAD_DIM), gqa_k_norm_g), pos_row, pos_col)
    v_c = vc.reshape(B, S, GQA_KV_HEADS, GQA_HEAD_DIM)
    q_c = q_c.reshape(B, S, GQA_KV_HEADS, GQA_HEADS // GQA_KV_HEADS, GQA_HEAD_DIM)
    o_gqa = blocked_attention(q_c, k_c, v_c, GQA_HEAD_DIM ** -0.5)

    merged = (jax.nn.sigmoid(ga) * (o_na @ w_br_na)
              + jax.nn.sigmoid(gb) * (o_mla @ w_br_mla)
              + jax.nn.sigmoid(gc) * (o_gqa @ w_br_gqa))
    x = x + g_m * (merged @ w_out)

    h = rms_norm(x, norm_ffn_g) * (1 + sc_f) + sh_f
    gate, up = jnp.split(h @ ffn_w_gate_up, 2, axis=-1)
    x = x + g_f * ((jax.nn.silu(gate) * up) @ ffn_w_down)
    return x

def first_inputs(seed: int = 0) -> dict:
    key = jax.random.key(seed)
    ks = jax.random.split(key, 24)
    f32 = jnp.float32

    def w(k, shape, fan_in):
        return jax.random.normal(k, shape, f32) * fan_in ** -0.5

    def gain(k, shape):
        return 1.0 + 0.02 * jax.random.normal(k, shape, f32)

    L, D = DEPTH, D_MODEL
    return {
        "x": jax.random.normal(ks[0], (BATCH, SEQ, D), f32),
        "c": jax.random.normal(ks[1], (BATCH, D), f32),
        "ada_w": w(ks[2], (L, D, N_MOD * D), D),
        "ada_b": 0.02 * jax.random.normal(ks[3], (L, N_MOD * D), f32),
        "norm_mix_g": gain(ks[4], (L, D)),
        "norm_ffn_g": gain(ks[5], (L, D)),
        "w_in": w(ks[6], (L, D, _in_cols()), D),
        "na_rpb": 0.1 * jax.random.normal(ks[7], (L, NA_HEADS, 2 * NA_KH - 1, 2 * NA_KW - 1), f32),
        "mla_q_norm_g": gain(ks[8], (L, MLA_Q_LORA)),
        "mla_kv_norm_g": gain(ks[9], (L, MLA_KV_LORA)),
        "mla_w_uq": w(ks[10], (L, MLA_Q_LORA, MLA_HEADS * (MLA_NOPE + MLA_ROPE)), MLA_Q_LORA),
        "mla_w_ukv": w(ks[11], (L, MLA_KV_LORA, MLA_HEADS * (MLA_NOPE + MLA_V)), MLA_KV_LORA),
        "gqa_q_norm_g": gain(ks[12], (L, GQA_HEAD_DIM)),
        "gqa_k_norm_g": gain(ks[13], (L, GQA_HEAD_DIM)),
        "w_br_na": w(ks[14], (L, NA_HEADS * NA_HEAD_DIM, D), NA_HEADS * NA_HEAD_DIM),
        "w_br_mla": w(ks[15], (L, MLA_HEADS * MLA_V, D), MLA_HEADS * MLA_V),
        "w_br_gqa": w(ks[16], (L, GQA_HEADS * GQA_HEAD_DIM, D), GQA_HEADS * GQA_HEAD_DIM),
        "w_out": w(ks[17], (L, D, D), D),
        "ffn_w_gate_up": w(ks[18], (L, D, 2 * FFN_HIDDEN), D),
        "ffn_w_down": w(ks[19], (L, FFN_HIDDEN, D), FFN_HIDDEN),
        "final_norm_g": gain(ks[20], (D,)),
    }

def first_block(x, c, ada_w, ada_b, norm_mix_g, norm_ffn_g, w_in, na_rpb, mla_q_norm_g, mla_kv_norm_g,
              mla_w_uq, mla_w_ukv, gqa_q_norm_g, gqa_k_norm_g, w_br_na, w_br_mla, w_br_gqa, w_out,
              ffn_w_gate_up, ffn_w_down, final_norm_g):
    S = x.shape[1]
    t = jnp.arange(S, dtype=jnp.int32)
    pos_t = t.astype(jnp.float32)
    pos_row = (t // GRID_W).astype(jnp.float32)
    pos_col = (t % GRID_W).astype(jnp.float32)
    for l in range(DEPTH):
        x = hybrid_layer(x, c, ada_w[l], ada_b[l], norm_mix_g[l], norm_ffn_g[l], w_in[l], na_rpb[l],
                         mla_q_norm_g[l], mla_kv_norm_g[l], mla_w_uq[l], mla_w_ukv[l],
                         gqa_q_norm_g[l], gqa_k_norm_g[l], w_br_na[l], w_br_mla[l], w_br_gqa[l], w_out[l],
                         ffn_w_gate_up[l], ffn_w_down[l], pos_t, pos_row, pos_col)
    return rms_norm(x, final_norm_g)


DEPTH_2 = 1

LRU_WIDTH = 512
LRU_BLOCKS = 8
LRU_BLOCK_DIM = LRU_WIDTH // LRU_BLOCKS
LRU_C = 8.0
CONV_WIDTH = 4
GDN_HEADS = 4
GDN_DK = 128
GDN_DV = 128
GDN_CHUNK = 64
SB_HEADS = 8
SB_DH = 64
SB_BLOCK = 128
GLA_HEADS = 4
GLA_DK = 128
GLA_DV = 128
GLA_GATE_RANK = 16
GLA_TAU = 16.0
GLA_CHUNK = 16
N_BRANCHES_2 = 4
BRANCH_WIDTH = 512
N_EXPERTS = 16
N_GROUPS = 4
EXPERTS_PER_GROUP = N_EXPERTS // N_GROUPS
TOP_K = 2
D_EXPERT = 512
LN_EPS = 1e-5
DN_ALPHA = (2 * DEPTH_2) ** 0.25
DN_BETA = (8 * DEPTH_2) ** -0.25

IN_SPLITS = (
    LRU_WIDTH,
    3 * GDN_HEADS * GDN_DK,
    GDN_HEADS,
    GDN_HEADS,
    GDN_HEADS * GDN_DV,
    3 * SB_HEADS * SB_DH,
    GLA_HEADS * (2 * GLA_DK + GLA_DV),
    GLA_GATE_RANK,
    GLA_HEADS * GLA_DV,
    N_BRANCHES_2 * D_MODEL,
)
D_IN = sum(IN_SPLITS)


def layer_norm(x, g, b):
    xf = x.astype(jnp.float32)
    mu = jnp.mean(xf, -1, keepdims=True)
    var = jnp.mean(jnp.square(xf - mu), -1, keepdims=True)
    y = (xf - mu) * lax.rsqrt(var + LN_EPS) * g.astype(jnp.float32) + b.astype(jnp.float32)
    return y.astype(x.dtype)

def rms_norm_2(x, g):
    xf = x.astype(jnp.float32)
    return xf * lax.rsqrt(jnp.mean(jnp.square(xf), -1, keepdims=True) + NORM_EPS) * g.astype(jnp.float32)

def l2_normalize(x):
    return x * lax.rsqrt(jnp.sum(jnp.square(x), -1, keepdims=True) + NORM_EPS)

def causal_depthwise_conv(x, w):
    return lax.conv_general_dilated(
        x, w[:, None, :].astype(x.dtype), window_strides=(1,),
        padding=((w.shape[0] - 1, 0),), dimension_numbers=("NWC", "WIO", "NWC"),
        feature_group_count=x.shape[-1])

def _to_chunks(t, c):
    b, s, h = t.shape[:3]
    return jnp.moveaxis(t.reshape((b, s // c, c, h) + t.shape[3:]), 3, 1)

def _from_chunks(t):
    b, h, n, c, d = t.shape
    return jnp.moveaxis(t, 1, 3).reshape(b, n * c, h, d)

def rg_lru(u, conv_w, conv_b, w_a, b_a, w_x, b_x, lam):
    b, s, _ = u.shape
    xc = (causal_depthwise_conv(u, conv_w) + conv_b).astype(jnp.float32)
    xblk = xc.reshape(b, s, LRU_BLOCKS, LRU_BLOCK_DIM)
    r = jax.nn.sigmoid(jnp.einsum("bsgi,gij->bsgj", xblk, w_a.astype(jnp.float32)).reshape(b, s, LRU_WIDTH) + b_a)
    i = jax.nn.sigmoid(jnp.einsum("bsgi,gij->bsgj", xblk, w_x.astype(jnp.float32)).reshape(b, s, LRU_WIDTH) + b_x)
    log_a = -LRU_C * r * jax.nn.softplus(-lam.astype(jnp.float32))
    a = jnp.exp(log_a)
    mult = jnp.sqrt(-jnp.expm1(2.0 * log_a))
    mult = jnp.where(jnp.arange(s)[None, :, None] == 0, 1.0, mult)
    inp = mult * i * xc

    def combine(lhs, rhs):
        return (lhs[0] * rhs[0], rhs[0] * lhs[1] + rhs[1])

    _, h = lax.associative_scan(combine, (a, inp), axis=1)
    return h

def gated_delta_rule_chunked(q, k, v, g, beta):
    b, s, h, dk = q.shape
    dv = v.shape[-1]
    c = GDN_CHUNK
    q, k, v = _to_chunks(q, c), _to_chunks(k, c), _to_chunks(v, c)
    g, beta = _to_chunks(g, c), _to_chunks(beta, c)
    gc = jnp.cumsum(g, axis=-1)
    causal = jnp.tril(jnp.ones((c, c), dtype=bool))
    strict = jnp.tril(jnp.ones((c, c), dtype=bool), k=-1)
    decay = jnp.exp(jnp.where(causal, gc[..., :, None] - gc[..., None, :], -jnp.inf))
    k_beta = k * beta[..., None]
    a_mat = jnp.where(strict, jnp.einsum("bhnik,bhnjk->bhnij", k_beta, k) * decay, 0.0)
    eye = jnp.broadcast_to(jnp.eye(c, dtype=a_mat.dtype), a_mat.shape)
    t_inv = lax.linalg.triangular_solve(a_mat, eye, left_side=True, lower=True, unit_diagonal=True)
    u = t_inv @ (v * beta[..., None])
    w = t_inv @ (k_beta * jnp.exp(gc)[..., None])
    q_dec = q * jnp.exp(gc)[..., None]
    attn = jnp.einsum("bhnik,bhnjk->bhnij", q, k) * decay
    k_dec = k * jnp.exp(gc[..., -1:] - gc)[..., None]
    g_last = jnp.exp(gc[..., -1])

    def step(state, xs):
        u_i, w_i, q_i, attn_i, kd_i, gl_i = xs
        v_new = u_i - w_i @ state
        o_i = q_i @ state + attn_i @ v_new
        state = state * gl_i[..., None, None] + jnp.swapaxes(kd_i, -1, -2) @ v_new
        return state, o_i

    xs = tuple(jnp.moveaxis(t, 2, 0) for t in (u, w, q_dec, attn, k_dec, g_last))
    state0 = jnp.zeros((b, h, dk, dv), q.dtype)
    _, o = lax.scan(step, state0, xs)
    return _from_chunks(jnp.moveaxis(o, 0, 2))

def gla_chunked(q, k, v, gk):
    b, s, h, dk = q.shape
    dv = v.shape[-1]
    c = GLA_CHUNK
    q, k, v, gk = (_to_chunks(t, c) for t in (q, k, v, gk))
    bcum = jnp.cumsum(gk, axis=-2)
    q_dec = q * jnp.exp(bcum)
    k_inv = k * jnp.exp(-bcum)
    causal = jnp.tril(jnp.ones((c, c), dtype=bool))
    attn = jnp.where(causal, jnp.einsum("bhnik,bhnjk->bhnij", q_dec, k_inv), 0.0)
    o_intra = attn @ v
    k_dec = k * jnp.exp(bcum[..., -1:, :] - bcum)
    g_last = jnp.exp(bcum[..., -1, :])

    def step(state, xs):
        q_i, kd_i, v_i, gl_i = xs
        o_i = q_i @ state
        state = state * gl_i[..., :, None] + jnp.swapaxes(kd_i, -1, -2) @ v_i
        return state, o_i

    xs = tuple(jnp.moveaxis(t, 2, 0) for t in (q_dec, k_dec, v, g_last))
    state0 = jnp.zeros((b, h, dk, dv), q.dtype)
    _, o_inter = lax.scan(step, state0, xs)
    return _from_chunks(o_intra + jnp.moveaxis(o_inter, 0, 2))

def stick_breaking_attention(q, k, v):
    b, s, h, dh = q.shape
    q = jnp.swapaxes(q, 1, 2) * dh ** -0.5
    k = jnp.swapaxes(k, 1, 2)
    v = jnp.swapaxes(v, 1, 2)
    outs = []
    for blk in range(s // SB_BLOCK):
        start = blk * SB_BLOCK
        end = start + SB_BLOCK
        z = jnp.einsum("bhqd,bhkd->bhqk", q[:, :, start:end], k[:, :, :end])
        strict = jnp.arange(end)[None, :] < (start + jnp.arange(SB_BLOCK))[:, None]
        log_keep = jnp.where(strict, jax.nn.log_sigmoid(-z), 0.0)
        between = lax.cumsum(log_keep, axis=3, reverse=True) - log_keep
        weights = jnp.where(strict, jnp.exp(jax.nn.log_sigmoid(z) + between), 0.0)
        outs.append(jnp.einsum("bhqk,bhkd->bhqd", weights, v[:, :, :end]))
    o = jnp.concatenate(outs, axis=2)
    return jnp.swapaxes(o, 1, 2).reshape(b, s, h * dh)

def mixer(x, w_in, conv_a_w, conv_a_b, rg_w_a, rg_b_a, rg_w_x, rg_b_x, rg_lambda,
          gdn_conv_w, gdn_a_log, gdn_dt_bias, gdn_norm_w,
          gla_w_gate_up, gla_b_gate, gla_norm_w, w_branch, w_out):
    b, s, _ = x.shape
    f32 = jnp.float32
    proj = jnp.einsum("bsd,de->bse", x, w_in)
    offsets = np.cumsum(IN_SPLITS)[:-1].tolist()
    (a_in, gdn_qkv, gdn_beta_in, gdn_decay_in, gdn_gate_in,
     sb_qkv, gla_qkv, gla_lr, gla_gate_in, merge_in) = jnp.split(proj, offsets, axis=-1)

    y_a = rg_lru(a_in, conv_a_w, conv_a_b, rg_w_a, rg_b_a, rg_w_x, rg_b_x, rg_lambda)

    qkv = jax.nn.silu(causal_depthwise_conv(gdn_qkv, gdn_conv_w)).astype(f32)
    q, k, v = jnp.split(qkv, [GDN_HEADS * GDN_DK, 2 * GDN_HEADS * GDN_DK], axis=-1)
    q = l2_normalize(q.reshape(b, s, GDN_HEADS, GDN_DK)) * GDN_DK ** -0.5
    k = l2_normalize(k.reshape(b, s, GDN_HEADS, GDN_DK))
    v = v.reshape(b, s, GDN_HEADS, GDN_DV)
    beta = jax.nn.sigmoid(gdn_beta_in.astype(f32))
    g = -jnp.exp(gdn_a_log.astype(f32)) * jax.nn.softplus(gdn_decay_in.astype(f32) + gdn_dt_bias)
    o_b = gated_delta_rule_chunked(q, k, v, g, beta)
    y_b = (rms_norm_2(o_b, gdn_norm_w) * jax.nn.silu(gdn_gate_in.reshape(b, s, GDN_HEADS, GDN_DV).astype(f32))).reshape(b, s, -1)

    q, k, v = jnp.split(sb_qkv.astype(f32), 3, axis=-1)
    y_c = stick_breaking_attention(q.reshape(b, s, SB_HEADS, SB_DH), k.reshape(b, s, SB_HEADS, SB_DH),
                                   v.reshape(b, s, SB_HEADS, SB_DH))

    q, k, v = jnp.split(gla_qkv.astype(f32), [GLA_HEADS * GLA_DK, 2 * GLA_HEADS * GLA_DK], axis=-1)
    gk = jax.nn.log_sigmoid(jnp.einsum("bsr,rc->bsc", gla_lr.astype(f32), gla_w_gate_up.astype(f32)) + gla_b_gate) / GLA_TAU
    o_d = gla_chunked(q.reshape(b, s, GLA_HEADS, GLA_DK) * GLA_DK ** -0.5, k.reshape(b, s, GLA_HEADS, GLA_DK),
                      v.reshape(b, s, GLA_HEADS, GLA_DV), gk.reshape(b, s, GLA_HEADS, GLA_DK))
    y_d = (rms_norm_2(o_d, gla_norm_w) * jax.nn.silu(gla_gate_in.reshape(b, s, GLA_HEADS, GLA_DV).astype(f32))).reshape(b, s, -1)

    gates = jax.nn.sigmoid(merge_in.reshape(b, s, N_BRANCHES_2, D_MODEL))
    merged = jnp.zeros_like(x)
    for n, y_n in enumerate((y_a, y_b, y_c, y_d)):
        merged = merged + gates[:, :, n] * jnp.einsum("bsc,cd->bsd", y_n.astype(x.dtype), w_branch[n])
    return jnp.einsum("bsd,de->bse", merged, w_out)

def moe(x, w_router, router_bias, w_gate, w_up, w_down):
    b, s, _ = x.shape
    scores = jax.nn.sigmoid(jnp.einsum("bsd,de->bse", x.astype(jnp.float32), w_router.astype(jnp.float32)))
    biased = scores + router_bias.astype(jnp.float32)
    grouped = biased.reshape(b, s, N_GROUPS, EXPERTS_PER_GROUP)
    group_score = jnp.sum(lax.top_k(grouped, TOP_K)[0], axis=-1)
    group_mask = jnp.argmax(group_score, axis=-1)[..., None] == jnp.arange(N_GROUPS)
    masked = jnp.where(group_mask[..., None], grouped, -jnp.inf).reshape(b, s, N_EXPERTS)
    _, expert_idx = lax.top_k(masked, TOP_K)
    w = jnp.take_along_axis(scores, expert_idx, axis=-1)
    w = w / jnp.sum(w, axis=-1, keepdims=True)
    combine = jnp.sum(jax.nn.one_hot(expert_idx, N_EXPERTS, dtype=jnp.float32) * w[..., None], axis=-2)
    combine = combine.astype(x.dtype)
    y = jnp.zeros_like(x)
    for e in range(N_EXPERTS):
        h = jax.nn.silu(jnp.einsum("bsd,df->bsf", x, w_gate[e])) * jnp.einsum("bsd,df->bsf", x, w_up[e])
        y = y + combine[..., e:e + 1] * jnp.einsum("bsf,fd->bsd", h, w_down[e])
    return y

def second_inputs(seed: int = 0) -> dict:
    key = jax.random.key(seed)
    ks = jax.random.split(key, 32)
    f32 = jnp.float32
    L = DEPTH_2

    def nrm(i, shape, scale):
        return jax.random.normal(ks[i], shape, f32) * scale

    x = nrm(0, (BATCH, SEQ, D_MODEL), 1.0)
    w_in = nrm(1, (L, D_MODEL, D_IN), D_MODEL ** -0.5)
    conv_a_w = nrm(2, (L, CONV_WIDTH, LRU_WIDTH), CONV_WIDTH ** -0.5)
    conv_a_b = nrm(3, (L, LRU_WIDTH), 0.01)
    rg_w_a = nrm(4, (L, LRU_BLOCKS, LRU_BLOCK_DIM, LRU_BLOCK_DIM), LRU_BLOCK_DIM ** -0.5)
    rg_b_a = nrm(5, (L, LRU_WIDTH), 0.01)
    rg_w_x = nrm(6, (L, LRU_BLOCKS, LRU_BLOCK_DIM, LRU_BLOCK_DIM), LRU_BLOCK_DIM ** -0.5)
    rg_b_x = nrm(7, (L, LRU_WIDTH), 0.01)
    a_pow = jax.random.uniform(ks[8], (L, LRU_WIDTH), f32, 0.9, 0.999)
    a0 = a_pow ** (1.0 / LRU_C)
    rg_lambda = jnp.log(a0) - jnp.log1p(-a0)
    gdn_conv_w = nrm(9, (L, CONV_WIDTH, 3 * GDN_HEADS * GDN_DK), CONV_WIDTH ** -0.5)
    gdn_a_log = jnp.log(jax.random.uniform(ks[10], (L, GDN_HEADS), f32, 1.0, 16.0))
    dt = jnp.exp(jax.random.uniform(ks[11], (L, GDN_HEADS), f32, float(np.log(1e-3)), float(np.log(1e-1))))
    gdn_dt_bias = dt + jnp.log(-jnp.expm1(-dt))
    gdn_norm_w = 1.0 + nrm(12, (L, GDN_DV), 0.01)
    gla_w_gate_up = nrm(13, (L, GLA_GATE_RANK, GLA_HEADS * GLA_DK), GLA_GATE_RANK ** -0.5)
    gla_b_gate = nrm(14, (L, GLA_HEADS * GLA_DK), 0.01)
    gla_norm_w = 1.0 + nrm(15, (L, GLA_DV), 0.01)
    w_branch = nrm(16, (L, N_BRANCHES_2, BRANCH_WIDTH, D_MODEL), BRANCH_WIDTH ** -0.5)
    w_out = nrm(17, (L, D_MODEL, D_MODEL), D_MODEL ** -0.5 * DN_BETA)
    ln1_g = 1.0 + nrm(18, (L, D_MODEL), 0.01)
    ln1_b = nrm(19, (L, D_MODEL), 0.01)
    w_router = nrm(20, (D_MODEL, N_EXPERTS), D_MODEL ** -0.5)
    router_bias = nrm(21, (N_EXPERTS,), 0.01)
    w_gate = nrm(22, (L, N_EXPERTS, D_MODEL, D_EXPERT), D_MODEL ** -0.5)
    w_up = nrm(23, (L, N_EXPERTS, D_MODEL, D_EXPERT), D_MODEL ** -0.5)
    w_down = nrm(24, (L, N_EXPERTS, D_EXPERT, D_MODEL), D_EXPERT ** -0.5 * DN_BETA)
    ln2_g = 1.0 + nrm(25, (L, D_MODEL), 0.01)
    ln2_b = nrm(26, (L, D_MODEL), 0.01)
    return {"x": x, "w_in": w_in, "conv_a_w": conv_a_w, "conv_a_b": conv_a_b,
            "rg_w_a": rg_w_a, "rg_b_a": rg_b_a, "rg_w_x": rg_w_x, "rg_b_x": rg_b_x,
            "rg_lambda": rg_lambda, "gdn_conv_w": gdn_conv_w, "gdn_a_log": gdn_a_log,
            "gdn_dt_bias": gdn_dt_bias, "gdn_norm_w": gdn_norm_w, "gla_w_gate_up": gla_w_gate_up,
            "gla_b_gate": gla_b_gate, "gla_norm_w": gla_norm_w, "w_branch": w_branch,
            "w_out": w_out, "ln1_g": ln1_g, "ln1_b": ln1_b, "w_router": w_router,
            "router_bias": router_bias, "w_gate": w_gate, "w_up": w_up, "w_down": w_down,
            "ln2_g": ln2_g, "ln2_b": ln2_b}

def second_block(x, w_in, conv_a_w, conv_a_b, rg_w_a, rg_b_a, rg_w_x, rg_b_x, rg_lambda,
              gdn_conv_w, gdn_a_log, gdn_dt_bias, gdn_norm_w, gla_w_gate_up, gla_b_gate,
              gla_norm_w, w_branch, w_out, ln1_g, ln1_b, w_router, router_bias,
              w_gate, w_up, w_down, ln2_g, ln2_b):
    for l in range(DEPTH_2):
        h = mixer(x, w_in[l], conv_a_w[l], conv_a_b[l], rg_w_a[l], rg_b_a[l], rg_w_x[l], rg_b_x[l],
                  rg_lambda[l], gdn_conv_w[l], gdn_a_log[l], gdn_dt_bias[l], gdn_norm_w[l],
                  gla_w_gate_up[l], gla_b_gate[l], gla_norm_w[l], w_branch[l], w_out[l])
        x = layer_norm(DN_ALPHA * x + h, ln1_g[l], ln1_b[l])
        h = moe(x, w_router, router_bias, w_gate[l], w_up[l], w_down[l])
        x = layer_norm(DN_ALPHA * x + h, ln2_g[l], ln2_b[l])
    return x


_first_inputs = second_inputs


def second_inputs(seed=0):
    import zlib

    import numpy as np

    out = dict(_first_inputs(seed))
    spreads = {}
    factors = {'conv_a_b': 5.658,
     'rg_b_a': 8.0,
     'rg_b_x': 8.0,
     'gdn_norm_w': 8.0,
     'gla_b_gate': 8.0,
     'gla_norm_w': 8.0,
     'ln1_b': 3.457,
     'ln2_g': 5.612,
     'ln2_b': 5.603}
    for name, (base, spread) in spreads.items():
        noise = np.random.default_rng([zlib.crc32(name.encode()), seed]).standard_normal(out[name].shape)
        drawn = base * np.exp(spread * noise) if base else spread * noise
        out[name] = __import__('jax').numpy.asarray(drawn.astype(out[name].dtype))
    for name, factor in factors.items():
        out[name] = (out[name] * factor).astype(out[name].dtype)
    return out


_narrow_inputs = second_inputs


def second_inputs(seed=0):
    out = dict(_narrow_inputs(seed))
    wider = {'rg_b_a': 12.0, 'rg_b_x': 12.0, 'gla_norm_w': 5.25, 'ln2_g': 6.32, 'ln2_b': 6.31}
    for name, times in wider.items():
        mean = out[name].mean()
        out[name] = (mean + times * (out[name] - mean)).astype(out[name].dtype)
    return out


def setup_inputs(seed=0):
    out = dict(first_inputs(seed))
    for name, value in second_inputs(seed + 1).items():
        if name != "x":
            out[name + "_2"] = value
    return out


def reference(
    x, c, ada_w, ada_b, norm_mix_g, norm_ffn_g, w_in, na_rpb, mla_q_norm_g, mla_kv_norm_g,
    mla_w_uq, mla_w_ukv, gqa_q_norm_g, gqa_k_norm_g, w_br_na, w_br_mla, w_br_gqa, w_out,
    ffn_w_gate_up, ffn_w_down, final_norm_g, w_in_2, conv_a_w_2, conv_a_b_2, rg_w_a_2, rg_b_a_2,
    rg_w_x_2, rg_b_x_2, rg_lambda_2, gdn_conv_w_2, gdn_a_log_2, gdn_dt_bias_2, gdn_norm_w_2,
    gla_w_gate_up_2, gla_b_gate_2, gla_norm_w_2, w_branch_2, w_out_2, ln1_g_2, ln1_b_2,
    w_router_2, router_bias_2, w_gate_2, w_up_2, w_down_2, ln2_g_2, ln2_b_2,
):
    x = first_block(
        x, c, ada_w, ada_b, norm_mix_g, norm_ffn_g, w_in, na_rpb, mla_q_norm_g, mla_kv_norm_g,
        mla_w_uq, mla_w_ukv, gqa_q_norm_g, gqa_k_norm_g, w_br_na, w_br_mla, w_br_gqa, w_out,
        ffn_w_gate_up, ffn_w_down, final_norm_g,
    )
    return second_block(
        x, w_in_2, conv_a_w_2, conv_a_b_2, rg_w_a_2, rg_b_a_2, rg_w_x_2, rg_b_x_2, rg_lambda_2,
        gdn_conv_w_2, gdn_a_log_2, gdn_dt_bias_2, gdn_norm_w_2, gla_w_gate_up_2, gla_b_gate_2,
        gla_norm_w_2, w_branch_2, w_out_2, ln1_g_2, ln1_b_2, w_router_2, router_bias_2,
        w_gate_2, w_up_2, w_down_2, ln2_g_2, ln2_b_2,
    )


_drawn_inputs = setup_inputs


def setup_inputs(seed=0):
    import zlib

    import numpy as np

    out = dict(_drawn_inputs(seed))
    spreads = {}
    factors = {'mla_q_norm_g': 3.308, 'gqa_q_norm_g': 8.0, 'gqa_k_norm_g': 3.313, 'gdn_norm_w_2': 2.757}
    for name, (base, spread) in spreads.items():
        noise = np.random.default_rng([zlib.crc32(name.encode()), seed]).standard_normal(out[name].shape)
        drawn = base * np.exp(spread * noise) if base else spread * noise
        out[name] = __import__('jax').numpy.asarray(drawn.astype(out[name].dtype))
    for name, factor in factors.items():
        out[name] = (out[name] * factor).astype(out[name].dtype)
    return out
```

```python
import numpy as np
import concourse.bass as bass
from concourse import mybir
from contextlib import ExitStack

P = 128
D = 1024
S = 256
TILES = S // P
KD = D // P
DEPTH = 2
EPS = 1e-6
LN_EPS = 1e-5
GRID_W = 64
NEG = -1e30
FFN = 2816
IN1 = 5024
IN2 = 10264
N_EXPERTS = 16
D_EXPERT = 512
ALPHA = 2 ** 0.25
SLOT = 8 * 512

FP = mybir.dt.float32
ALU = mybir.AluOpType
ACT = mybir.ActivationFunctionType
AX = mybir.AxisListType.X


def constants():
    p = np.arange(P)
    j, i = p[:, None], p[None, :]
    c = {"ident": np.eye(P), "ones": np.ones((P, P))}
    qc, kc = (p % GRID_W)[:, None], np.arange(GRID_W)[None, :]
    start = np.clip(qc - 8, 0, GRID_W - 16)
    seen = (kc >= start) & (kc < start + 16)
    c["na_seen"] = seen
    c["na_neg"] = np.where(seen, 0.0, NEG)
    t = np.arange(S)

    def rotary(pos, half):
        inv = (1.0 / (np.float32(10000.0) ** (np.arange(half, dtype=np.float32) / half))).astype(np.float32)
        a = pos.astype(np.float32)[:, None] * inv[None, :]
        co, si = np.cos(a), np.sin(a)
        return np.stack([co, co], 1), np.stack([-si, si], 1)

    def tiled(a):
        return a.reshape(TILES, P, -1).transpose(1, 0, 2).reshape(P, -1)

    c["mla_cos"], c["mla_sin"] = (tiled(a) for a in rotary(t, 16))
    rows, cols = rotary(t // GRID_W, 16), rotary(t % GRID_W, 16)
    c["ax_cos"] = tiled(np.stack([rows[0], cols[0]], 1))
    c["ax_sin"] = tiled(np.stack([rows[1], cols[1]], 1))
    same64 = j // 64 == i // 64
    c["cum64"] = same64 & (j <= i)
    c["blk64"] = same64
    c["strict64"] = same64 & (j < i)
    for s in (1, 2, 4, 8, 16, 32):
        low = (j // (2 * s) == i // (2 * s)) & (j % (2 * s) >= s) & (i % (2 * s) < s)
        c[f"level{s}"] = low
    c["level1_t"] = c["level1"].T
    c["causal16"] = (j // 16 == i // 16) & (j <= i)
    c["sb_strict"] = j < i
    c["sb_incl"] = j >= i
    c["parity"] = np.stack([(p // 16) % 2 == 0, (p // 16) % 2 == 1], 1)
    c["restart16"] = np.broadcast_to((np.arange(4 * S) % 16 != 0)[None], (P, 4 * S))
    c["rank16"] = np.broadcast_to(np.arange(16, 0, -1)[None], (P, 16))
    c["rank4"] = np.broadcast_to(np.arange(4, 0, -1)[None], (P, 4))
    return {k: np.asarray(v, np.float32) for k, v in c.items()}


class Count:

    def __init__(self, nc, name):
        self.sem = nc.alloc_semaphore(name)
        self.n = 0


def done(eng, ins, s):
    ins.then_inc(s.sem, 1)
    s.n += 1
    eng.wait_ge(s.sem, s.n)


def signal(ins, s):
    ins.then_inc(s.sem, 1)
    s.n += 1


class Ring:

    def __init__(self, nc, name, slots, units):
        self.units, self.slots = units, slots
        self.depth = slots.shape[1]
        self.landed = [nc.alloc_semaphore(f"{name}_landed{s}") for s in range(self.depth)]
        self.used = nc.alloc_semaphore(f"{name}_units_used")
        self.value, count = [], [0] * self.depth
        for n, parts in enumerate(units):
            count[n % self.depth] += 16 * len(parts)
            self.value.append(count[n % self.depth])
        self.issued = 0

    def feed(self, sp, before):
        for n in range(self.issued, min(before + self.depth, len(self.units))):
            if n >= self.depth:
                sp.wait_ge(self.used, n - self.depth + 1)
            for at, k, width, c0, c1, src in self.units[n]:
                sp.dma_start(self.view(n, k, width, at)[:, :, c0:c1], src).then_inc(self.landed[n % self.depth], 16)
            self.issued = n + 1

    def arrived(self, pe, n):
        pe.wait_ge(self.landed[n % self.depth], self.value[n])

    def view(self, n, k, width, at=0):
        return self.slots[:, n % self.depth, at:at + k * width].rearrange("p (k n) -> p k n", k=k)


class Job:

    def __init__(self, unit, kind, idx, width, act, out, last=None, k=KD, lhs=None, at=0, unit_width=None, k0=0,
                 col0=0):
        self.unit, self.kind, self.idx, self.width, self.act, self.out = unit, kind, idx, width, act, out
        self.last = idx == (3 if kind == "fm" else 1) if last is None else last
        self.k, self.lhs, self.at, self.unit_width, self.k0, self.col0 = k, lhs, at, unit_width or 512, k0, col0


def program(nc, A, OUT, dbg=None):
    es = ExitStack()
    dbg = dbg or {}
    with es:
        def sb(name, shape, stack=es):
            return stack.enter_context(nc.sbuf_tensor(name, shape, FP))

        ps = [es.enter_context(nc.psum_tensor(f"bank{b}", [P, 512], FP)) for b in range(8)]
        layout, width = {}, 0
        for name, table in constants().items():
            layout[name] = (width, table.shape[1])
            width += table.shape[1]
        cst = sb("cst", [P, width])

        def const(name):
            at, n = layout[name]
            return cst[:, at:at + n]

        ident, ones = const("ident"), const("ones")
        x = sb("x", [P, TILES, D])
        hT = sb("hT", [P, KD, S])
        rstat = sb("rstat", [P, 8])
        half_neg = sb("half_neg", [P, 64])
        setup_loaded = nc.alloc_semaphore("setup_loaded")
        half_set = nc.alloc_semaphore("half_set")
        strips = nc.dram_tensor("na_bias_strips", [DEPTH, P, TILES * 4 * 256], FP, kind="Internal").ap()
        strips_written = nc.alloc_semaphore("strips_written")

        def dump(name, ap):
            if name in dbg:
                s = nc.alloc_semaphore("dbg" + name)
                with nc.Block() as block:
                    @block.sync
                    def _(sp):
                        sp.dma_start(dbg[name], ap).then_inc(s, 16)
                        sp.wait_ge(s, 16)

        with nc.Block() as block:
            @block.sync
            def _(sp):
                sp.dma_start(cst[:, :], A["constants"]).then_inc(setup_loaded, 16)
                sp.dma_start(x[:, :, :], A["x"].rearrange("o (t p) d -> p (o t) d", p=P)).then_inc(setup_loaded, 16)
                n = 0
                for l in range(DEPTH):
                    for qr in range(4):
                        for h in range(4):
                            src = bass.AP(A["na_rpb"].tensor, (l * 4 + h) * 465 + (7 - qr) * 31 + 15,
                                          [[31, 4], [-1, 64], [1, 64]])
                            at = ((qr // 2) * 4 + h) * 256
                            dst = strips[l, 64 * (qr % 2):64 * (qr % 2) + 64, at:at + 256]
                            sp.dma_start(dst.rearrange("p (r c) -> r p c", r=4), src).then_inc(strips_written, 16)
                            n += 16
                sp.wait_ge(setup_loaded, 32)
                sp.wait_ge(strips_written, n)

            @block.gpsimd
            def _(pool):
                pool.memset(half_neg[:, :], -0.5).then_inc(half_set, 1)

        def rsqrt_on_pool(pool, out, ms, n, s, mul, eps):
            done(pool, pool.tensor_scalar(ms, ms, mul, eps, ALU.mult, ALU.add), s)
            done(pool, pool.tensor_tensor(out, ms, half_neg[:, 0:n], ALU.pow), s)

        def evac(eng, act, out, in_):
            return nc.scalar.activation(out, in_, ACT.Copy) if act else nc.vector.tensor_copy(out, in_)

        def transpose_pe(pe, src, chunks, ready, s, bank0=0):
            for k in range(chunks):
                for t in range(TILES):
                    if ready is not None and k == 0:
                        pe.wait_ge(ready[0], ready[1][t])
                    ins = nc.tensor.transpose(ps[bank0 + k // 2][:, (k % 2) * S + t * P:(k % 2) * S + (t + 1) * P],
                                              src[:, t, k * P:(k + 1) * P], ident)
                if k % 2:
                    signal(ins, s)

        def rms_norm_to_fm(tag, scale=None, bias=None, row_gain=None, keep=False):
            with ExitStack() as st:
                junk = sb(f"{tag}_junk", [P, TILES, D], st)
                xn = sb(f"{tag}_xn", [P, TILES, D], st)
                squared, rooted, normed, turned, act_out, dve_out = (Count(nc, f"{tag}_{n}") for n in
                    ("squared", "rooted", "normed", "turned", "act_out", "dve_out"))
                dst = x if keep else xn
                with nc.Block() as block:
                    @block.scalar
                    def _(act):
                        for t in range(TILES):
                            done(act, nc.scalar.activation(junk[:, t, :], x[:, t, :], ACT.Square,
                                                           accum_out=rstat[:, t:t + 1]), squared)
                        for k in (0, 1, 4, 5):
                            act.wait_ge(turned.sem, k // 2 + 1)
                            src = ps[k // 2][:, (k % 2) * S:(k % 2 + 1) * S]
                            if scale is None:
                                ins = nc.scalar.activation(hT[:, k, :], src, ACT.Copy)
                            else:
                                ins = nc.scalar.activation(hT[:, k, :], src, ACT.Identity,
                                                           bias=bias[:, k:k + 1], scale=scale[:, k:k + 1])
                            signal(ins, act_out)

                    @block.gpsimd
                    def _(pool):
                        pool.wait_ge(squared.sem, 2)
                        rsqrt_on_pool(pool, rstat[:, 4:6], rstat[:, 0:2], 2, rooted, 1.0 / D, EPS)

                    @block.vector
                    def _(dve):
                        dve.wait_ge(rooted.sem, 2)
                        for t in range(TILES):
                            r = rstat[:, 4 + t:5 + t]
                            if row_gain is None:
                                ins = nc.vector.tensor_scalar(dst[:, t, :], x[:, t, :], r, None, ALU.mult)
                            else:
                                ins = nc.vector.scalar_tensor_tensor(dst[:, t, :], x[:, t, :], r, row_gain,
                                                                     ALU.mult, ALU.mult)
                            signal(ins, normed)
                        for k in (2, 3, 6, 7):
                            dve.wait_ge(turned.sem, k // 2 + 1)
                            src = ps[k // 2][:, (k % 2) * S:(k % 2 + 1) * S]
                            if scale is None:
                                ins = nc.vector.tensor_copy(hT[:, k, :], src)
                            else:
                                ins = nc.vector.tensor_scalar(hT[:, k, :], src, scale[:, k:k + 1],
                                                              bias[:, k:k + 1], ALU.mult, ALU.add)
                            signal(ins, dve_out)

                    @block.tensor
                    def _(pe):
                        transpose_pe(pe, dst, KD, (normed.sem, (1, 2)), turned)

        def products(ring, job, out):
            w = ring.view(job.unit, job.k, job.unit_width, job.at)
            h = hT if job.lhs is None else job.lhs
            for c in range(job.k):
                tokens, weights = h[:, job.k0 + c, :], w[:, c, :]
                if job.kind == "tok":
                    lhs, rhs = tokens[:, job.idx * P:(job.idx + 1) * P], weights[:, job.col0:job.col0 + job.width]
                else:
                    lhs, rhs = weights[:, job.idx * P:(job.idx + 1) * P], tokens
                ins = nc.tensor.matmul(out, lhs, rhs, start=c == 0, stop=c == job.k - 1)
            return ins

        def project(tag, ring, jobs, feed_to, banks=8, extra=None, block_of=None):
            extra = extra or {}
            summed, act_out, dve_out = (Count(nc, f"{tag}_{n}") for n in ("summed", "act_out", "dve_out"))
            n_summed, n_out = 0, {True: 0, False: 0}
            for g, job in enumerate(jobs):
                if job.last:
                    job.ready = (ring.used, job.unit + 1)
                else:
                    n_summed += 1
                    job.ready = (summed.sem, n_summed)
                n_out[job.act] += 1
                job.left = ((act_out if job.act else dve_out).sem, n_out[job.act])

            def shape(job, g):
                return ps[g % banks][:, 0:job.width if job.kind == "tok" else S]

            def drain(eng, act, s):
                for g, job in enumerate(jobs):
                    if job.act == act:
                        eng.wait_ge(*job.ready)
                        (signal if act else lambda ins, s: done(eng, ins, s))(job.out(shape(job, g)), s)

            with nc.Block() as block:
                @block.sync
                def _(sp):
                    ring.feed(sp, feed_to)
                    if "sync" in extra:
                        extra["sync"](sp)

                @block.tensor
                def _(pe):
                    for g, job in enumerate(jobs):
                        if g == 0 or jobs[g - 1].unit != job.unit:
                            ring.arrived(pe, job.unit)
                        if g >= banks:
                            pe.wait_ge(*jobs[g - banks].left)
                        ins = products(ring, job, shape(job, g))
                        ins.then_inc(ring.used if job.last else summed.sem, 1)
                    if "tensor" in extra:
                        extra["tensor"](pe)

                @block.scalar
                def _(act):
                    drain(act, True, act_out)
                    if "scalar" in extra:
                        extra["scalar"](act)

                @block.vector
                def _(dve):
                    if "vector_first" in extra:
                        extra["vector_first"](dve)
                    drain(dve, False, dve_out)
                    if "vector" in extra:
                        extra["vector"](dve)

                if "gpsimd" in extra:
                    @block.gpsimd
                    def _(pool):
                        extra["gpsimd"](pool)

        def copy_out(act, dst):
            return lambda src: nc.scalar.activation(dst, src, ACT.Copy) if act else nc.vector.tensor_copy(dst, src)

        def gated_hidden(tag, ring, first, blocks, gain):
            def gu(n):
                return first + (0 if n == 0 else 2 * n - 1)

            def dn(n):
                return first + (2 * n + 2 if n < blocks - 1 else 2 * n + 1)

            with ExitStack() as st:
                sig = sb(f"{tag}_sig", [P, 2, TILES, 256], st)
                a = sb(f"{tag}_a", [P, 2, TILES, 256], st)
                aT = sb(f"{tag}_aT", [P, 2, 2, S], st)
                hidden, gated, acted, turned, copied, chain = (Count(nc, f"{tag}_{n}") for n in
                    ("hidden", "gated", "acted", "turned", "copied", "dve_step"))
                with nc.Block() as block:
                    @block.sync
                    def _(sp):
                        ring.feed(sp, len(ring.units))

                    @block.tensor
                    def _(pe):
                        def gate_up(n, t):
                            if t == 0:
                                ring.arrived(pe, gu(n))
                            if n >= 1:
                                pe.wait_ge(acted.sem, 2 * (n - 1) + t + 1)
                            ins = products(ring, Job(gu(n), "tok", t, 512, True, None), ps[t][:, :])
                            ins.then_inc(ring.used if t else hidden.sem, 1)

                        def turn(n):
                            if n >= 2:
                                pe.wait_ge(copied.sem, n - 1)
                            for t in range(TILES):
                                pe.wait_ge(acted.sem, 2 * n + t + 1)
                                for c in range(2):
                                    ins = nc.tensor.transpose(ps[2 + n % 2][:, c * S + t * P:c * S + (t + 1) * P],
                                                              a[:, n % 2, t, c * P:(c + 1) * P], ident)
                            ins.then_inc(turned.sem, 1)

                        def down(n):
                            pe.wait_ge(copied.sem, n + 1)
                            ring.arrived(pe, dn(n))
                            w = ring.view(dn(n), 2, D)
                            for t in range(TILES):
                                for nb in range(2):
                                    for c in range(2):
                                        ins = nc.tensor.matmul(
                                            ps[4 + 2 * t + nb][:, :], aT[:, n % 2, c, t * P:(t + 1) * P],
                                            w[:, c, nb * 512:(nb + 1) * 512],
                                            start=n == 0 and c == 0, stop=n == blocks - 1 and c == 1)
                            ins.then_inc(ring.used, 1)

                        for n in range(blocks + 1):
                            if n < blocks:
                                gate_up(n, 0)
                            if n >= 1:
                                turn(n - 1)
                            if n < blocks:
                                gate_up(n, 1)
                            if n >= 1:
                                down(n - 1)

                    @block.scalar
                    def _(act):
                        def copy_turned(n):
                            act.wait_ge(turned.sem, n + 1)
                            if n >= 2:
                                act.wait_ge(ring.used, dn(n - 2) + 1)
                            nc.scalar.activation(aT[:, n % 2, :, :].rearrange("p c s -> p (c s)"),
                                                 ps[2 + n % 2][:, :], ACT.Copy).then_inc(copied.sem, 1)

                        for n in range(blocks):
                            for t in range(TILES):
                                if t == 0:
                                    act.wait_ge(hidden.sem, n + 1)
                                else:
                                    act.wait_ge(ring.used, gu(n) + 1)
                                if n >= 2:
                                    act.wait_ge(acted.sem, 2 * (n - 2) + t + 1)
                                nc.scalar.activation(sig[:, n % 2, t, :], ps[t][:, 0:256],
                                                     ACT.Sigmoid).then_inc(gated.sem, 1)
                                if t == 0 and n >= 1:
                                    copy_turned(n - 1)
                        copy_turned(blocks - 1)

                    @block.vector
                    def _(dve):
                        for n in range(blocks):
                            for t in range(TILES):
                                dve.wait_ge(gated.sem, 2 * n + t + 1)
                                g = sig[:, n % 2, t, :]
                                done(dve, nc.vector.tensor_tensor(g, ps[t][:, 0:256], g, ALU.mult), chain)
                                if n >= 2 and t == 0:
                                    dve.wait_ge(turned.sem, n - 1)
                                c = gain(n, t)
                                out = a[:, n % 2, t, :]
                                if c is None:
                                    ins = nc.vector.tensor_tensor(out, ps[t][:, 256:512], g, ALU.mult)
                                else:
                                    ins = nc.vector.scalar_tensor_tensor(out, ps[t][:, 256:512], c, g,
                                                                         ALU.mult, ALU.mult)
                                ins.then_inc(acted.sem, 1)

        def hidden_units(blocks, gate, up, down):
            def gate_up(n):
                return [(0, 8, 512, 0, 256, gate(n)), (0, 8, 512, 256, 512, up(n))]

            units = [gate_up(0)]
            for n in range(blocks):
                if n + 1 < blocks:
                    units.append(gate_up(n + 1))
                units.append([(0, 2, D, 0, D, down(n))])
            return units

        def add_gated(tag, gain):
            with ExitStack() as st:
                tmp = sb(f"{tag}_tmp", [P, 4, 512], st)
                chain = Count(nc, f"{tag}_step")
                with nc.Block() as block:
                    @block.vector
                    def _(dve):
                        for q in range(4):
                            t, cut = q // 2, slice((q % 2) * 512, (q % 2) * 512 + 512)
                            done(dve, nc.vector.tensor_tensor(tmp[:, q, :], ps[4 + q][:, :], gain[:, cut], ALU.mult), chain)
                            done(dve, nc.vector.tensor_tensor(x[:, t, cut], x[:, t, cut], tmp[:, q, :], ALU.add), chain)

        def attend(tag, heads, oT):
            with ExitStack() as st:
                prob = sb(f"{tag}_prob", [P, 2, TILES, S], st)
                score = sb(f"{tag}_score", [P, 2, TILES, S], st)
                probT = sb(f"{tag}_probT", [P, 2, TILES, S], st)
                stat = sb(f"{tag}_stat", [P, 2, 4, TILES], st)
                scored, maxed, expd, normed, turned, copied, mixed, stored_o, chain = (
                    Count(nc, f"{tag}_{n}") for n in ("scored", "maxed", "expd", "normed", "turned", "copied",
                                                      "mixed", "out", "step"))
                N = len(heads)
                with nc.Block() as block:
                    @block.tensor
                    def _(pe):
                        for i in range(N + 2):
                            if i < N:
                                qT, kT, v, scale, bias = heads[i]
                                if i >= 2:
                                    pe.wait_ge(expd.sem, 2 * (i - 1))
                                    pe.wait_ge(maxed.sem, i - 1)
                                for t in range(TILES):
                                    ins = nc.tensor.matmul(ps[i % 2][:, t * S:(t + 1) * S], qT[:, t * P:(t + 1) * P],
                                                           kT, start=True, stop=True)
                                ins.then_inc(scored.sem, 1)
                            if 1 <= i <= N:
                                n = i - 1
                                pe.wait_ge(normed.sem, n + 1)
                                if n >= 2:
                                    pe.wait_ge(copied.sem, n - 1)
                                for t in range(TILES):
                                    for kt in range(TILES):
                                        ins = nc.tensor.transpose(ps[2 + n % 2][:, kt * S + t * P:kt * S + (t + 1) * P],
                                                                  prob[:, n % 2, t, kt * P:(kt + 1) * P], ident)
                                ins.then_inc(turned.sem, 1)
                            if i >= 2:
                                n = i - 2
                                v = heads[n][2]
                                pe.wait_ge(copied.sem, n + 1)
                                if n >= 2:
                                    pe.wait_ge(stored_o.sem, n - 1)
                                base = 64 * (n % 2)
                                for kt in range(TILES):
                                    ins = nc.tensor.matmul(ps[4 + n % 2][base:base + 64, 0:S], v(kt),
                                                           probT[:, n % 2, kt, :], start=kt == 0, stop=kt == 1)
                                ins.then_inc(mixed.sem, 1)

                    @block.vector
                    def _(dve):
                        for i in range(N + 2):
                            if i < N:
                                scale, bias = heads[i][3:5]
                                dve.wait_ge(scored.sem, i + 1)
                                if i >= 2:
                                    dve.wait_ge(normed.sem, i - 1)
                                src = ps[i % 2][:, :].rearrange("p (t s) -> p t s", t=TILES)
                                if bias is not None:
                                    dst = score[:, i % 2, :, :]
                                    if i >= 2:
                                        dve.wait_ge(expd.sem, 2 * (i - 1))
                                    done(dve, nc.vector.scalar_tensor_tensor(dst, src, scale, bias, ALU.mult, ALU.add), chain)
                                    src = dst
                                done(dve, nc.vector.tensor_reduce(stat[:, i % 2, 1, :], src, AX, ALU.max), chain)
                                nc.vector.tensor_scalar(stat[:, i % 2, 0, :], stat[:, i % 2, 1, :],
                                                        -1.0 if bias is not None else -scale, None,
                                                        ALU.mult).then_inc(maxed.sem, 1)
                            if 1 <= i <= N:
                                n = i - 1
                                dve.wait_ge(expd.sem, 2 * n + 2)
                                done(dve, nc.vector.reciprocal(stat[:, n % 2, 3, :], stat[:, n % 2, 2, :]), chain)
                                nc.vector.tensor_tensor(
                                    prob[:, n % 2, :, :], prob[:, n % 2, :, :],
                                    stat[:, n % 2, 3, :].unsqueeze(2).broadcast_to([P, TILES, S]),
                                    ALU.mult).then_inc(normed.sem, 1)
                            if i >= 2:
                                n = i - 2
                                base = 64 * (n % 2)
                                dve.wait_ge(mixed.sem, n + 1)
                                nc.vector.tensor_copy(oT[base:base + 64, n // 2, :],
                                                      ps[4 + n % 2][base:base + 64, 0:S]).then_inc(stored_o.sem, 1)

                    @block.scalar
                    def _(act):
                        for i in range(N + 1):
                            if i < N:
                                scale, bias = heads[i][3:5]
                                act.wait_ge(maxed.sem, i + 1)
                                if i >= 2:
                                    act.wait_ge(turned.sem, i - 1)
                                for t in range(TILES):
                                    src = ps[i % 2][:, t * S:(t + 1) * S] if bias is None else score[:, i % 2, t, :]
                                    nc.scalar.activation(prob[:, i % 2, t, :], src, ACT.Exp,
                                                         bias=stat[:, i % 2, 0, t:t + 1],
                                                         scale=scale if bias is None else 1.0,
                                                         accum_out=stat[:, i % 2, 2, t:t + 1]).then_inc(expd.sem, 1)
                            if i >= 1:
                                n = i - 1
                                act.wait_ge(turned.sem, n + 1)
                                if n >= 2:
                                    act.wait_ge(mixed.sem, n - 1)
                                nc.scalar.activation(probT[:, n % 2, :, :].rearrange("p k s -> p (k s)"),
                                                     ps[2 + n % 2][:, :], ACT.Copy).then_inc(copied.sem, 1)

        def rotate(dve, s, out, src, cos, sin, tmp, heads, parts):
            w = parts * 32
            bc = [P, TILES, heads, w]

            def table(c):
                return c.rearrange("p (t w) -> p t w", t=TILES).unsqueeze(2).broadcast_to(bc)

            for t in range(TILES):
                for half in range(2):
                    pick = "p h (a f w) -> p h a f w"
                    got = src[:, t, :, :].rearrange(pick, a=parts, f=2)[:, :, :, 1 - half, :]
                    put = tmp[:, t, :, :].rearrange(pick, a=parts, f=2)[:, :, :, half, :]
                    by = sin[:, t * w:(t + 1) * w].unsqueeze(1).broadcast_to([P, heads, w]) \
                        .rearrange(pick, a=parts, f=2)[:, :, :, half, :]
                    signal(nc.vector.tensor_tensor(put, got, by, ALU.mult), s)
            dve.wait_ge(s.sem, s.n)
            done(dve, nc.vector.tensor_tensor(out, src, table(cos), ALU.mult), s)
            done(dve, nc.vector.tensor_tensor(out, out, tmp, ALU.add), s)

        def layer(l):
            def cols(name, c0, c1):
                return A[name][bass.ds(l, 1), :, c0:c1].rearrange("o (k p) n -> p (o k) n", p=P)

            def rows(name, r0, r1):
                return A[name][bass.ds(l, 1), r0:r1, :].rearrange("o (k p) n -> p (o k) n", p=P)

            units = [[(0, 8, 512, 0, 512, cols("ada_w", 512 * b, 512 * b + 512))] for b in range(12)]
            PROJ = len(units)
            for c0, c1 in ((0, 512), (512, 1024), (1024, 1536), (1536, 1952)):
                units.append([(0, 8, 512, 0, c1 - c0, cols("w_in", c0, c1))])
            GATES = len(units)
            for b in range(6):
                units.append([(0, 8, 512, 0, 512, cols("w_in", 1952 + 512 * b, 2464 + 512 * b))])
            LORA = len(units)
            units.append([(0, 2, 384, 0, 384, cols("mla_w_uq", 0, 384)),
                          (768, 1, 512, 0, 512, cols("mla_w_ukv", 0, 512))])
            BRANCH = len(units)
            for nb in range(2):
                n0, n1 = 512 * nb, 512 * nb + 512
                units.append([(0, 2, 512, 0, 512, cols("w_br_na", n0, n1)),
                              (1024, 2, 512, 0, 512, cols("w_br_mla", n0, n1)),
                              (2048, 4, 512, 0, 512, cols("w_br_gqa", n0, n1))])
            MERGED = len(units)
            for nb in range(2):
                units.append([(0, 8, 512, 0, 512, cols("w_out", 512 * nb, 512 * nb + 512))])
            HIDDEN = len(units)
            n_hidden = FFN // 256
            units += hidden_units(n_hidden, lambda n: cols("ffn_w_gate_up", 256 * n, 256 * n + 256),
                                  lambda n: cols("ffn_w_gate_up", FFN + 256 * n, FFN + 256 * n + 256),
                                  lambda n: rows("ffn_w_down", 256 * n, 256 * n + 256))
            with ExitStack() as st:
                slots = sb("layer_weights", [P, 5, SLOT], st)
                ring = Ring(nc, "layer", slots, units)
                col = sb("columns", [P, 75], st)
                mod = sb("mod", [P, 48], st)
                Gm = sb("gain_mix", [P, 8], st)
                Gf = sb("gain_ffn", [P, 8], st)
                gate_rows = sb("gate_rows", [P, 2, D], st)
                small = nc.alloc_semaphore("small_loaded")
                turned, copied, silud, modded, spread, diag_ready = (Count(nc, f"mod_{n}") for n in
                    ("turned", "copied", "silud", "modded", "spread", "diag_ready"))

                with ExitStack() as s1:
                    raw = sb("raw_rows", [P, P], s1)
                    sc = sb("silu_c", [P, 8], s1)
                    sg = sb("sigmoid_c", [P, 8], s1)
                    diag = sb("diag", [P, 4, 512], s1)
                    with nc.Block() as block:
                        @block.sync
                        def _(sp):
                            def row_block(name, r, n):
                                src = A[name] if name == "c" else A[name][bass.ds(l, 1), :]
                                sp.dma_start(raw[r:r + n, :], src.rearrange("o (r p) -> (o r) p", p=P)).then_inc(small, 16)

                            row_block("ada_b", 0, 48)
                            row_block("norm_mix_g", 48, 8)
                            row_block("norm_ffn_g", 56, 8)
                            row_block("mla_q_norm_g", 64, 2)
                            row_block("mla_kv_norm_g", 66, 1)
                            row_block("c", 67, 8)
                            ring.feed(sp, PROJ)

                        @block.tensor
                        def _(pe):
                            pe.wait_ge(small, 16 * 6)
                            nc.tensor.transpose(ps[0][:, 0:75], raw[0:75, :], ident[0:75, 0:75]).then_inc(turned.sem, 1)
                            pe.wait_ge(silud.sem, 2)
                            for b in range(48):
                                if b % 4 == 0:
                                    ring.arrived(pe, b // 4)
                                w = ring.view(b // 4, 8, 512)
                                for k in range(8):
                                    ins = nc.tensor.matmul(ps[1][:, b:b + 1], w[:, k, (b % 4) * P:(b % 4 + 1) * P],
                                                           sc[:, k:k + 1], start=k == 0, stop=k == 7)
                                if b % 4 == 3:
                                    ins.then_inc(ring.used, 1)
                            for h in range(4):
                                pe.wait_ge(diag_ready.sem, h + 1)
                                nc.tensor.matmul(ps[2 + h][:, :], ones, diag[:, h, :], start=True,
                                                 stop=True).then_inc(spread.sem, 1)

                        @block.scalar
                        def _(act):
                            act.wait_ge(turned.sem, 1)
                            done(act, nc.scalar.activation(col[:, :], ps[0][:, 0:75], ACT.Copy), copied)
                            done(act, nc.scalar.activation(sg[:, :], col[:, 67:75], ACT.Sigmoid), silud)
                            for h in range(4):
                                act.wait_ge(spread.sem, h + 1)
                                signal(nc.scalar.activation(gate_rows[:, h // 2, (h % 2) * 512:(h % 2 + 1) * 512],
                                                            ps[2 + h][:, :], ACT.Copy), copied)

                        @block.vector
                        def _(dve):
                            dve.wait_ge(silud.sem, 1)
                            nc.vector.tensor_tensor(sc[:, :], sg[:, :], col[:, 67:75], ALU.mult).then_inc(silud.sem, 1)
                            dve.wait_ge(ring.used, 12)
                            done(dve, nc.vector.tensor_tensor(mod[:, :], ps[1][:, 0:48], col[:, 0:48], ALU.add), modded)
                            for G, at, g in ((Gm, 8, 48), (Gf, 32, 56)):
                                done(dve, nc.vector.scalar_tensor_tensor(G[:, :], mod[:, at:at + 8], 1.0, col[:, g:g + 8],
                                                                         ALU.add, ALU.mult), modded)
                            for h in range(4):
                                base = (16 if h < 2 else 40) + (h % 2) * 4
                                signal(nc.vector.tensor_tensor(
                                    diag[:, h, :].rearrange("p (b n) -> p b n", b=4),
                                    ident.unsqueeze(1).broadcast_to([P, 4, P]),
                                    mod[:, base:base + 4].unsqueeze(2).broadcast_to([P, 4, P]), ALU.mult), diag_ready)
                dump("mod", mod[:, :])
                dump("gate_rows", gate_rows[:, :, :])

                rms_norm_to_fm("mix", Gm, mod[:, 0:8])
                with ExitStack() as s2:
                    oT = sb("oT", [P, 8, S], s2)
                    sg3 = sb("branch_gates", [P, TILES, 3 * D], s2)
                    attention(l, ring, PROJ, GATES, LORA, BRANCH, col, oT, sg3)
                    dump("oT", oT[:, :, :])
                    merge(ring, "merge", BRANCH, MERGED, HIDDEN, ((0, 2), (2, 2), (4, 4)), oT, sg3, gate_rows[:, 0, :])
                dump("xmid", x[:, :, :])
                rms_norm_to_fm("ffn", Gf, mod[:, 24:32])
                gated_hidden("ffnh", ring, HIDDEN, n_hidden, lambda n, t: None)
                add_gated("ffn_add", gate_rows[:, 1, :])

        def attention(l, ring, PROJ, GATES, LORA, BRANCH, col, oT, sg3):
            with ExitStack() as s3:
                VA, CQ, CKV, KR, QC, KC, VC = 0, 256, 512, 640, 672, 1184, 1312
                p1 = sb("proj_tok", [P, TILES, 1440], s3)
                na_qk = sb("na_qkT", [P, 4, S], s3)
                na_bias = sb("na_bias", [P, TILES, 4, 4, GRID_W], s3)
                gqa_g = sb("gqa_g", [P, 2, 64], s3)
                bias_loaded = nc.alloc_semaphore("na_bias_loaded")
                gains_loaded = nc.alloc_semaphore("gqa_gains_loaded")

                jobs = []
                for b in range(4):
                    act = b % 2 == 0
                    jobs.append(Job(PROJ, "fm", b, S, act, copy_out(act, na_qk[:, b, :])))
                for u in range(3):
                    w = 416 if u == 2 else 512
                    for t in range(TILES):
                        act = t == 0
                        jobs.append(Job(PROJ + 1 + u, "tok", t, w, act,
                                        copy_out(act, p1[:, t, 512 * u:512 * u + w])))

                def load_small(sp):
                    for i, name in enumerate(("gqa_q_norm_g", "gqa_k_norm_g")):
                        src = A[name][bass.ds(l, 1), :].broadcast_to([P, 64])
                        sp.dma_start(gqa_g[:, i, :], src).then_inc(gains_loaded, 16)
                    sp.dma_start(na_bias[:, :, :, :, :].rearrange("p t h r c -> p (t h r c)"),
                                 strips[bass.ds(l, 1), :, :].rearrange("o p n -> (o p) n")).then_inc(bias_loaded, 16)

                project("proj", ring, jobs, GATES, extra={"sync": load_small})
                dump("p1", p1[:, :, :])
                dump("na_qk", na_qk[:, :, :])

                ms = sb("mean_squares", [P, TILES, 12], s3)
                rs = sb("inv_rms", [P, TILES, 12], s3)
                roped = sb("gqa_roped", [P, TILES, 12, 64], s3)
                kpe = sb("mla_k_pe", [P, TILES, 1, 32], s3)
                scratch = ExitStack()
                sq = sb("squares", [P, TILES, 1056], scratch)
                prep = Count(nc, "prep_step")
                rooted = Count(nc, "prep_rooted")
                summed_sq = nc.alloc_semaphore("prep_sums")

                jobs = [Job(GATES + b, "tok", t, 512, True,
                            (lambda dst: lambda src: nc.scalar.activation(dst, src, ACT.Sigmoid))(
                                sg3[:, t, 512 * b:512 * b + 512])) for b in range(6) for t in range(TILES)]

                def prepare(dve):
                    v = nc.vector
                    dve.wait_ge(bias_loaded, 16)
                    bias4 = na_bias[:, :, :, :, :].rearrange("p t h r c -> p (t h r) c")
                    for name, op in (("na_seen", ALU.mult), ("na_neg", ALU.add)):
                        done(dve, v.tensor_tensor(bias4, bias4, const(name).unsqueeze(1).broadcast_to([P, 32, 64]), op), prep)
                    done(dve, v.tensor_tensor(sq[:, :, :], p1[:, :, CQ:VC], p1[:, :, CQ:VC], ALU.mult), prep)
                    done(dve, v.tensor_reduce(ms[:, :, 0:1], sq[:, :, 0:256], AX, ALU.add), prep)
                    done(dve, v.tensor_reduce(ms[:, :, 1:2], sq[:, :, 256:384], AX, ALU.add), prep)
                    done(dve, v.tensor_reduce(ms[:, :, 2:12], sq[:, :, 416:1056].rearrange("p t (h d) -> p t h d", h=10),
                                              AX, ALU.add), prep)
                    for c0, c1, n in ((0, 1, 256), (1, 2, 128), (2, 12, 64)):
                        ins = v.tensor_scalar(ms[:, :, c0:c1], ms[:, :, c0:c1], 1.0 / n, EPS, ALU.mult, ALU.add)
                        if c0 < 2:
                            done(dve, ins, prep)
                    ins.then_inc(summed_sq, 1)
                    rotate(dve, prep, kpe[:, :, :, :], p1[:, :, KR:KR + 32].unsqueeze(2), const("mla_cos"),
                           const("mla_sin"), sq[:, :, 0:32].unsqueeze(2), 1, 1)
                    dve.wait_ge(rooted.sem, 1)
                    dve.wait_ge(gains_loaded, 32)
                    for at, n, j in ((CQ, 256, 0), (CKV, 128, 1)):
                        done(dve, v.tensor_tensor(p1[:, :, at:at + n], p1[:, :, at:at + n],
                                                  rs[:, :, j:j + 1].broadcast_to([P, TILES, n]), ALU.mult), prep)
                    qk = p1[:, :, QC:VC].rearrange("p t (h d) -> p t h d", h=10)
                    done(dve, v.tensor_tensor(qk, qk, rs[:, :, 2:12].unsqueeze(3).broadcast_to([P, TILES, 10, 64]),
                                              ALU.mult), prep)
                    for h0, h1, g in ((0, 8, 0), (8, 10, 1)):
                        by = gqa_g[:, g, :].unsqueeze(1).unsqueeze(1).broadcast_to([P, TILES, h1 - h0, 64])
                        done(dve, v.tensor_tensor(qk[:, :, h0:h1, :], qk[:, :, h0:h1, :], by, ALU.mult), prep)
                    rotate(dve, prep, roped[:, :, 0:10, :], qk, const("ax_cos"), const("ax_sin"),
                           sq[:, :, 0:640].rearrange("p t (h d) -> p t h d", h=10), 10, 2)
                    done(dve, v.tensor_copy(roped[:, :, 10, :], roped[:, :, 9, :]), prep)
                    done(dve, v.tensor_copy(roped[:, :, 11, :], roped[:, :, 8, :]), prep)

                def roots(pool):
                    pool.wait_ge(summed_sq, 1)
                    pool.tensor_tensor(rs[:, :, :].rearrange("p t c -> p (t c)"),
                                       ms[:, :, :].rearrange("p t c -> p (t c)"),
                                       half_neg[:, 0:24], ALU.pow).then_inc(rooted.sem, 1)

                project("gates", ring, jobs, LORA, extra={"vector": prepare, "gpsimd": roots})
                scratch.close()
                dump("roped", roped[:, :, :, :])

                gqaT = sb("gqa_T", [P, 6, S], s3)
                kvb = sb("mla_kv", [P, TILES, 4, P], s3)
                lora = ExitStack()
                cT = sb("mla_cT", [P, 3, S], lora)
                qfull = sb("mla_q", [P, TILES, 4, 96], lora)
                kfull = sb("mla_k", [P, TILES, 4, 96], lora)
                rot = sb("mla_rotated", [P, TILES, 4, 32], lora)
                tmp = sb("mla_rot_tmp", [P, TILES, 4, 32], lora)
                turned, scaled, lifted, act_copied, gqa_turned, step = (Count(nc, f"mla_{n}") for n in
                    ("turned", "scaled", "lifted", "copied", "gqa_turned", "step"))
                with nc.Block() as block:
                    @block.sync
                    def _(sp):
                        ring.feed(sp, BRANCH)

                    @block.tensor
                    def _(pe):
                        for c in range(3):
                            for t in range(TILES):
                                at = CQ + c * P
                                ins = nc.tensor.transpose(ps[c // 2][:, (c % 2) * S + t * P:(c % 2) * S + (t + 1) * P],
                                                          p1[:, t, at:at + P], ident)
                            ins.then_inc(turned.sem, 1)
                        for b in range(6):
                            for t in range(TILES):
                                ins = nc.tensor.transpose(ps[2 + b // 2][:, (b % 2) * S + t * P:(b % 2) * S + (t + 1) * P],
                                                          roped[:, t, 2 * b:2 * b + 2, :].rearrange("p h d -> p (h d)"), ident)
                            if b % 2:
                                ins.then_inc(gqa_turned.sem, 1)
                        ring.arrived(pe, LORA)
                        pe.wait_ge(scaled.sem, 3)
                        pe.wait_ge(act_copied.sem, 1)
                        wq = ring.view(LORA, 2, 384)
                        wkv = ring.view(LORA, 1, 512, 768)
                        bank = (6, 7, 0, 2)
                        for t in range(TILES):
                            for c in range(2):
                                ins = nc.tensor.matmul(ps[bank[t]][:, 0:384], cT[:, c, t * P:(t + 1) * P], wq[:, c, :],
                                                       start=c == 0, stop=c == 1)
                            ins.then_inc(lifted.sem, 1)
                        for t in range(TILES):
                            ins = nc.tensor.matmul(ps[bank[2 + t]][:, :], cT[:, 2, t * P:(t + 1) * P], wkv[:, 0, :],
                                                   start=True, stop=True)
                            ins.then_inc(lifted.sem if t == 0 else ring.used, 1)

                    @block.scalar
                    def _(act):
                        for c in range(3):
                            act.wait_ge(turned.sem, max(c + 1, 2))
                            nc.scalar.activation(cT[:, c, :], ps[c // 2][:, (c % 2) * S:(c % 2 + 1) * S], ACT.Copy,
                                                 scale=col[:, 64 + c:65 + c]).then_inc(scaled.sem, 1)
                        for b in range(3):
                            act.wait_ge(gqa_turned.sem, b + 1)
                            nc.scalar.activation(gqaT[:, 2 * b:2 * b + 2, :].rearrange("p b s -> p (b s)"),
                                                 ps[2 + b][:, :], ACT.Copy).then_inc(act_copied.sem, 1)

                    @block.vector
                    def _(dve):
                        v = nc.vector
                        for t in range(TILES):
                            dve.wait_ge(lifted.sem, t + 1)
                            done(dve, v.tensor_copy(qfull[:, t, :, :].rearrange("p h d -> p (h d)"),
                                                    ps[6 + t][:, 0:384]), step)
                        for t in range(TILES):
                            dve.wait_ge(*((lifted.sem, 3) if t == 0 else (ring.used, LORA + 1)))
                            done(dve, v.tensor_copy(kvb[:, t, :, :].rearrange("p h d -> p (h d)"),
                                                    ps[(0, 2)[t]][:, :]), step)
                        rotate(dve, step, rot[:, :, :, :], qfull[:, :, :, 64:96], const("mla_cos"), const("mla_sin"),
                               tmp[:, :, :, :], 4, 1)
                        done(dve, v.tensor_copy(qfull[:, :, :, 64:96], rot[:, :, :, :]), step)
                        done(dve, v.tensor_copy(kfull[:, :, :, 0:64], kvb[:, :, :, 0:64]), step)
                        done(dve, v.tensor_copy(kfull[:, :, :, 64:96], kpe[:, :, :, :].broadcast_to([P, TILES, 4, 32])), step)
                dump("qfull", qfull[:, :, :, :])

                mT = hT[0:96, :, :].rearrange("p (i h) s -> p i h s", i=2)
                m_turned, m_out = nc.alloc_semaphore("mla_heads_turned"), nc.alloc_semaphore("mla_heads_out")
                with nc.Block() as block:
                    @block.tensor
                    def _(pe):
                        for i, src in enumerate((qfull, kfull)):
                            for h in range(4):
                                for t in range(TILES):
                                    ins = nc.tensor.transpose(
                                        ps[2 * i + h // 2][0:96, (h % 2) * S + t * P:(h % 2) * S + (t + 1) * P],
                                        src[:, t, h, :], ident)
                                if h % 2:
                                    ins.then_inc(m_turned, 1)

                    @block.scalar
                    def _(act):
                        for b in range(4):
                            act.wait_ge(m_turned, b + 1)
                            nc.scalar.activation(mT[:, b // 2, 2 * (b % 2):2 * (b % 2) + 2, :].rearrange("p b s -> p (b s)"),
                                                 ps[b][0:96, :], ACT.Copy).then_inc(m_out, 1)

                lora.close()
                heads = []
                for h in range(4):
                    base = 64 * (h % 2)
                    heads.append((na_qk[base:base + 64, h // 2, :], na_qk[base:base + 64, 2 + h // 2, :],
                                  (lambda h: lambda kt: p1[:, kt, VA + 64 * h:VA + 64 * h + 64])(h), 64 ** -0.5,
                                  na_bias[:, :, h, :, :].rearrange("p t r c -> p t (r c)")))
                for h in range(4):
                    heads.append((mT[:, 0, h, :], mT[:, 1, h, :],
                                  (lambda h: lambda kt: kvb[:, kt, h, 64:128])(h), 96 ** -0.5, None))
                for h in range(8):
                    base, kv = 64 * (h % 2), h // 4
                    block_k = 4 if kv == h % 2 else 5
                    heads.append((gqaT[base:base + 64, h // 2, :], gqaT[base:base + 64, block_k, :],
                                  (lambda kv: lambda kt: p1[:, kt, VC + 64 * kv:VC + 64 * kv + 64])(kv), 64 ** -0.5, None))
                attend("att", heads, oT)

        def merge(ring, tag, first, second, feed_to, chunks, yT, gates, gain):
            n_br = len(chunks)
            with ExitStack() as st:
                m = sb(f"{tag}_sum", [P, TILES, D], st)
                part = sb(f"{tag}_part", [P, 2, 512], st)
                step = Count(nc, f"{tag}_step")
                jobs = []
                n = 0
                for nb in range(2):
                    for t in range(TILES):
                        for b, (c0, k) in enumerate(chunks):
                            cut = slice(nb * 512, nb * 512 + 512)

                            def out(src, t=t, b=b, cut=cut, n=n):
                                gate = gates[:, t, b * D + cut.start:b * D + cut.stop]
                                dst = m[:, t, cut]
                                if b == 0:
                                    return nc.vector.tensor_tensor(dst, src, gate, ALU.mult)
                                done(nc.vector, nc.vector.tensor_tensor(part[:, n % 2, :], src, gate, ALU.mult), step)
                                return nc.vector.tensor_tensor(dst, dst, part[:, n % 2, :], ALU.add)

                            jobs.append(Job(first + nb, "tok", t, 512, False, out, last=t == 1 and b == n_br - 1,
                                            k=k, lhs=yT, at=512 * c0, k0=c0))
                            n += 1
                project(tag, ring, jobs, second)
                transpose_block(f"{tag}_T", m, hT)
                jobs = []
                for nb in range(2):
                    for t in range(TILES):
                        cut = slice(nb * 512, nb * 512 + 512)

                        def out(src, t=t, cut=cut, q=2 * nb + t):
                            if gain is None:
                                return nc.vector.scalar_tensor_tensor(x[:, t, cut], x[:, t, cut], ALPHA, src,
                                                                      ALU.mult, ALU.add)
                            done(nc.vector, nc.vector.tensor_tensor(part[:, q % 2, :], src, gain[:, cut], ALU.mult), step)
                            return nc.vector.tensor_tensor(x[:, t, cut], x[:, t, cut], part[:, q % 2, :], ALU.add)

                        jobs.append(Job(second + nb, "tok", t, 512, False, out))
                project(f"{tag}_out", ring, jobs, feed_to)

        def transpose_block(tag, src, dst):
            turned, out = Count(nc, f"{tag}_turned"), nc.alloc_semaphore(f"{tag}_out")
            with nc.Block() as block:
                @block.tensor
                def _(pe):
                    for b in range(4):
                        for k in (2 * b, 2 * b + 1):
                            for t in range(TILES):
                                ins = nc.tensor.transpose(ps[b][:, (k % 2) * S + t * P:(k % 2) * S + (t + 1) * P],
                                                          src[:, t, k * P:(k + 1) * P], ident)
                        ins.then_inc(turned.sem, 1)

                @block.scalar
                def _(act):
                    for b in (0, 2):
                        act.wait_ge(turned.sem, b + 1)
                        nc.scalar.activation(dst[:, 2 * b:2 * b + 2, :].rearrange("p b s -> p (b s)"), ps[b][:, :],
                                             ACT.Copy).then_inc(out, 1)

                @block.vector
                def _(dve):
                    for b in (1, 3):
                        dve.wait_ge(turned.sem, b + 1)
                        nc.vector.tensor_copy(dst[:, 2 * b:2 * b + 2, :].rearrange("p b s -> p (b s)"),
                                              ps[b][:, :]).then_inc(out, 1)

        def second_part():
            def cols(name, c0, c1):
                return A[name][0, :, c0:c1].rearrange("(k p) n -> p k n", p=P)

            units = []

            def unit(name, c0, c1, k=KD):
                units.append([(0, k, c1 - c0, 0, c1 - c0, cols(name, c0, c1))])
                return len(units) - 1

            U_A = unit("w_in_2", 0, 512)
            U_QKV = [unit("w_in_2", 512 + 512 * i, 1024 + 512 * i) for i in range(3)]
            U_GGATE = unit("w_in_2", 2056, 2568)
            U_MERGE = [unit("w_in_2", 6168 + 512 * i, 6680 + 512 * i) for i in range(8)]
            U_SB = [unit("w_in_2", 2568 + 512 * i, 3080 + 512 * i) for i in range(3)]
            U_GLA = [unit("w_in_2", 4104 + 512 * i, 4616 + 512 * i) for i in range(3)]
            U_LGATE = unit("w_in_2", 5656, 6168)
            U_BR = len(units)
            for n in range(4):
                units.append([(0, 4, D, 0, D, A["w_branch_2"][0, n, :, :].rearrange("(k p) n -> p k n", p=P))])
            U_OUT = unit("w_out_2", 0, 512)
            unit("w_out_2", 512, 1024)
            U_HID = len(units)
            n_hidden = N_EXPERTS * D_EXPERT // 256
            per = D_EXPERT // 256

            def of_expert(name, n):
                c0 = 256 * (n % per)
                return A[name][0, n // per, :, c0:c0 + 256].rearrange("(k p) n -> p k n", p=P)

            units += hidden_units(n_hidden, lambda n: of_expert("w_gate_2", n), lambda n: of_expert("w_up_2", n),
                                  lambda n: A["w_down_2"][0, n // per, 256 * (n % per):256 * (n % per) + 256, :]
                                  .rearrange("(k p) n -> p k n", p=P))
            with ExitStack() as st:
                slots = sb("weights_2", [P, 4, SLOT], st)
                ring = Ring(nc, "second", slots, units)
                comb = sb("combine", [P, TILES, N_EXPERTS], st)
                with ExitStack() as s1:
                    mixer(ring, s1, U_A, U_QKV, U_GGATE, U_MERGE, U_SB, U_GLA, U_LGATE, U_BR, U_OUT, U_HID)
                dump("pre1", x[:, :, :])
                layer_norm("ln1", "ln1_g_2", "ln1_b_2")
                dump("x3", x[:, :, :])
                transpose_block("x3_T", x, hT)
                router(comb)
                dump("comb", comb[:, :, :])
                gated_hidden("moe", ring, U_HID, n_hidden, lambda n, t: comb[:, t, n // per:n // per + 1])
                scaled_add()
                layer_norm("ln2", "ln2_g_2", "ln2_b_2")
            with nc.Block() as block:
                @block.sync
                def _(sp):
                    stored = nc.alloc_semaphore("stored")
                    sp.dma_start(OUT.rearrange("o (t p) d -> p (o t) d", p=P), x[:, :, :]).then_inc(stored, 16)
                    sp.wait_ge(stored, 16)

        def scaled_add():
            step = Count(nc, "moe_added")
            with nc.Block() as block:
                @block.vector
                def _(dve):
                    for q in range(4):
                        t, cut = q // 2, slice((q % 2) * 512, (q % 2) * 512 + 512)
                        signal(nc.vector.scalar_tensor_tensor(x[:, t, cut], x[:, t, cut], ALPHA, ps[4 + q][:, :],
                                                              ALU.mult, ALU.add), step)

        def layer_norm(tag, gain_name, bias_name):
            with ExitStack() as st:
                rows = sb(f"{tag}_rows", [P, 2, D], st)
                junk = sb(f"{tag}_junk", [P, TILES, D], st)
                loaded = nc.alloc_semaphore(f"{tag}_rows_loaded")
                step, squared, rooted = (Count(nc, f"{tag}_{n}") for n in ("step", "squared", "rooted"))
                with nc.Block() as block:
                    @block.sync
                    def _(sp):
                        for i, name in enumerate((gain_name, bias_name)):
                            sp.dma_start(rows[:, i, :], A[name].broadcast_to([P, D])).then_inc(loaded, 16)

                    @block.vector
                    def _(dve):
                        v = nc.vector
                        done(dve, v.tensor_reduce(rstat[:, 0:2], x[:, :, :], AX, ALU.add), step)
                        done(dve, v.tensor_scalar(rstat[:, 0:2], rstat[:, 0:2], 1.0 / D, None, ALU.mult), step)
                        for t in range(TILES):
                            done(dve, v.tensor_scalar(x[:, t, :], x[:, t, :], rstat[:, t:t + 1], None, ALU.subtract), step)
                        dve.wait_ge(rooted.sem, 2)
                        dve.wait_ge(loaded, 32)
                        for t in range(TILES):
                            done(dve, v.scalar_tensor_tensor(x[:, t, :], x[:, t, :], rstat[:, 4 + t:5 + t], rows[:, 0, :],
                                                             ALU.mult, ALU.mult), step)
                            done(dve, v.tensor_tensor(x[:, t, :], x[:, t, :], rows[:, 1, :], ALU.add), step)

                    @block.scalar
                    def _(act):
                        for t in range(TILES):
                            act.wait_ge(step.sem, 3 + t)
                            signal(nc.scalar.activation(junk[:, t, :], x[:, t, :], ACT.Square,
                                                        accum_out=rstat[:, 2 + t:3 + t]), squared)

                    @block.gpsimd
                    def _(pool):
                        pool.wait_ge(squared.sem, 2)
                        rsqrt_on_pool(pool, rstat[:, 4:6], rstat[:, 2:4], 2, rooted, 1.0 / D, LN_EPS)

        def router(comb):
            with ExitStack() as st:
                w = sb("router_w", [P, KD, N_EXPERTS], st)
                bias = sb("router_bias", [P, N_EXPERTS], st)
                sc = sb("router_scores", [P, TILES, 16], st)
                bi = sb("router_biased", [P, TILES, 16], st)
                t1 = sb("router_t1", [P, TILES, 16], st)
                t2 = sb("router_t2", [P, TILES, 16], st)
                gs = sb("router_groups", [P, TILES, 4], st)
                g1 = sb("router_g1", [P, TILES, 4], st)
                g2 = sb("router_g2", [P, TILES, 4], st)
                m = sb("router_max", [P, TILES, 1], st)
                loaded = nc.alloc_semaphore("router_loaded")
                scored, squashed, step = (Count(nc, f"router_{n}") for n in ("scored", "squashed", "step"))
                with nc.Block() as block:
                    @block.sync
                    def _(sp):
                        sp.dma_start(w[:, :, :], A["w_router_2"].rearrange("(k p) n -> p k n", p=P)).then_inc(loaded, 16)
                        sp.dma_start(bias[:, :], A["router_bias_2"].rearrange("(o n) -> o n", o=1)
                                     .broadcast_to([P, 16])).then_inc(loaded, 16)

                    @block.tensor
                    def _(pe):
                        pe.wait_ge(loaded, 32)
                        for t in range(TILES):
                            for k in range(KD):
                                ins = nc.tensor.matmul(ps[t][:, 0:16], hT[:, k, t * P:(t + 1) * P], w[:, k, :],
                                                       start=k == 0, stop=k == KD - 1)
                            ins.then_inc(scored.sem, 1)

                    @block.scalar
                    def _(act):
                        for t in range(TILES):
                            act.wait_ge(scored.sem, t + 1)
                            nc.scalar.activation(sc[:, t, :], ps[t][:, 0:16], ACT.Sigmoid).then_inc(squashed.sem, 1)

                    @block.vector
                    def _(dve):
                        v = nc.vector

                        def do(ins):
                            done(dve, ins, step)

                        def first_max(onehot, values, key, rank, n):
                            bc = [P, TILES, n]
                            do(v.tensor_reduce(m[:, :, :], values, AX, ALU.max))
                            do(v.tensor_tensor(key, values, m[:, :, :].broadcast_to(bc), ALU.is_equal))
                            do(v.tensor_tensor(key, key, rank.unsqueeze(1).broadcast_to(bc), ALU.mult))
                            do(v.tensor_reduce(m[:, :, :], key, AX, ALU.max))
                            do(v.tensor_tensor(onehot, key, m[:, :, :].broadcast_to(bc), ALU.is_equal))

                        dve.wait_ge(loaded, 32)
                        dve.wait_ge(squashed.sem, 2)
                        S16, B16, T1, T2 = (a[:, :, :] for a in (sc, bi, t1, t2))
                        do(v.tensor_tensor(B16, S16, bias[:, :].unsqueeze(1).broadcast_to([P, TILES, 16]), ALU.add))
                        e = B16.rearrange("p t (g e) -> p t g e", e=4)
                        pairs = [(a, b) for a in range(4) for b in range(a + 1, 4)]
                        for i, (a, b) in enumerate(pairs):
                            dst = gs[:, :, :] if i == 0 else g1[:, :, :]
                            do(v.tensor_tensor(dst, e[:, :, :, a], e[:, :, :, b], ALU.add))
                            if i:
                                do(v.tensor_tensor(gs[:, :, :], gs[:, :, :], g1[:, :, :], ALU.max))
                        first_max(g2[:, :, :], gs[:, :, :], g1[:, :, :], const("rank4"), 4)
                        inside = g2[:, :, :].unsqueeze(3).broadcast_to([P, TILES, 4, 4])
                        do(v.tensor_tensor(e, e, inside, ALU.mult))
                        do(v.tensor_scalar(g1[:, :, :], g2[:, :, :], -1.0, -NEG, ALU.add, ALU.mult))
                        do(v.tensor_tensor(e, e, g1[:, :, :].unsqueeze(3).broadcast_to([P, TILES, 4, 4]), ALU.add))
                        first_max(T1, B16, T2, const("rank16"), 16)
                        do(v.scalar_tensor_tensor(B16.rearrange("p t e -> p (t e)"), T1.rearrange("p t e -> p (t e)"),
                                                  4 * NEG, B16.rearrange("p t e -> p (t e)"), ALU.mult, ALU.add))
                        first_max(comb[:, :, :], B16, T2, const("rank16"), 16)
                        do(v.tensor_tensor(comb[:, :, :], comb[:, :, :], T1, ALU.add))
                        do(v.tensor_tensor(comb[:, :, :], comb[:, :, :], S16, ALU.mult))
                        do(v.tensor_reduce(m[:, :, :], comb[:, :, :], AX, ALU.add))
                        do(v.reciprocal(m[:, :, :], m[:, :, :]))
                        do(v.tensor_tensor(comb[:, :, :], comb[:, :, :], m[:, :, :].broadcast_to([P, TILES, 16]), ALU.mult))

        def mixer(ring, s1, U_A, U_QKV, U_GGATE, U_MERGE, U_SB, U_GLA, U_LGATE, U_BR, U_OUT, U_HID):
            v, a = nc.vector, nc.scalar
            yT = [None] * 4
            yT[0] = sb("y_lru", [P, 4, S], s1)
            yT[1] = sb("y_gdn", [P, 4, S], s1)
            par = sb("mixer_columns", [P, 86], s1)
            CONV_A, CONV_B, B_A, B_X, LAM, CONV_G, GDN_N, GLA_B, GLA_N = 0, 16, 20, 24, 28, 32, 80, 81, 85
            merge_gates = sb("merge_gates", [P, TILES, 4 * D], s1)
            small = sb("small_w", [P, KD, 24], s1)
            w_up = sb("gla_up", [16, 512], s1)
            w_ax = sb("lru_w", [P, 2, 4, P], s1)
            tok8 = sb("beta_decay", [P, TILES, 8], s1)
            hrow = sb("head_rows", [P, 8], s1)
            lrT = sb("low_rank_T", [16, S], s1)

            with ExitStack() as s2:
                raw = sb("raw_2", [P, P], s2)
                gain = sb("final_gain", [P, D], s2)
                raw_loaded, gain_loaded = nc.alloc_semaphore("raw_2_loaded"), nc.alloc_semaphore("final_gain_loaded")
                turned, out = nc.alloc_semaphore("raw_2_turned"), nc.alloc_semaphore("raw_2_out")
                cleared = nc.alloc_semaphore("lru_w_cleared")
                with nc.Block() as block:
                    @block.gpsimd
                    def _(pool):
                        pool.memset(w_ax[:, :, :, :], 0.0).then_inc(cleared, 1)

                    @block.sync
                    def _(sp):
                        sp.dma_start(gain[:, :], A["final_norm_g"].rearrange("(o n) -> o n", o=1).broadcast_to([P, D])) \
                            .then_inc(gain_loaded, 16)
                        n = 0
                        for name, at, rows in (("conv_a_w_2", CONV_A, 16), ("conv_a_b_2", CONV_B, 4), ("rg_b_a_2", B_A, 4),
                                               ("rg_b_x_2", B_X, 4), ("rg_lambda_2", LAM, 4), ("gdn_conv_w_2", CONV_G, 48),
                                               ("gdn_norm_w_2", GDN_N, 1), ("gla_b_gate_2", GLA_B, 4),
                                               ("gla_norm_w_2", GLA_N, 1)):
                            src = A[name]
                            src = src[0, :, :].rearrange("k (c p) -> (k c) p", p=P) if len(src.shape) == 3 else \
                                src.rearrange("o (c p) -> (o c) p", p=P)
                            sp.dma_start(raw[at:at + rows, :], src).then_inc(raw_loaded, 16)
                        sp.wait_ge(cleared, 1)
                        for i, name in enumerate(("rg_w_a_2", "rg_w_x_2")):
                            for half in range(2):
                                src = A[name][0, half:8:2, :, :].rearrange("c i j -> i c j")
                                sp.dma_start(w_ax[64 * half:64 * half + 64, i, :, 64 * half:64 * half + 64],
                                             src).then_inc(gain_loaded, 16)
                        sp.dma_start(small[:, :, 0:8], cols2("w_in_2", 2048, 2056)).then_inc(gain_loaded, 16)
                        sp.dma_start(small[:, :, 8:24], cols2("w_in_2", 5640, 5656)).then_inc(gain_loaded, 16)
                        sp.dma_start(w_up[:, :], A["gla_w_gate_up_2"][0, :, :]).then_inc(gain_loaded, 16)
                        sp.dma_start(hrow[:, 0:4], A["gdn_a_log_2"].broadcast_to([P, 4])).then_inc(gain_loaded, 16)
                        sp.dma_start(hrow[:, 4:8], A["gdn_dt_bias_2"].broadcast_to([P, 4])).then_inc(gain_loaded, 16)
                        ring.feed(sp, 0)
                        sp.wait_ge(gain_loaded, 16 * 10)

                    @block.tensor
                    def _(pe):
                        pe.wait_ge(raw_loaded, 16 * 9)
                        nc.tensor.transpose(ps[0][:, 0:86], raw[0:86, :], ident[0:86, 0:86]).then_inc(turned, 1)

                    @block.scalar
                    def _(act):
                        act.wait_ge(turned, 1)
                        a.activation(par[:, :], ps[0][:, 0:86], ACT.Copy).then_inc(out, 1)
                rms_norm_to_fm("final", row_gain=gain[:, :], keep=True)
            dump("x2", x[:, :, :])

            def fm_job(u, b, act, dst, func=None):
                out = copy_out(act, dst) if func is None else (lambda src: a.activation(dst, src, func))
                return Job(u, "fm", b, S, act, out)

            with ExitStack() as s2:
                ain = sb("lru_in", [P, 4, S], s2)
                qkv = sb("gdn_qkv", [P, 12, S], s2)
                ggate = sb("gdn_gate", [P, 4, S], s2)
                jobs = [fm_job(U_A, b, b % 2 == 0, ain[:, b, :]) for b in range(4)]
                for i in range(3):
                    jobs += [fm_job(U_QKV[i], b, b % 2 == 0, qkv[:, 4 * i + b, :]) for b in range(4)]
                jobs += [fm_job(U_GGATE, b, True, ggate[:, b, :], ACT.Silu) for b in range(4)]

                small_done, small_out = nc.alloc_semaphore("small_summed"), nc.alloc_semaphore("small_out")
                def small_copy(act):
                    act.wait_ge(small_done, 1)
                    a.activation(tok8[:, :, :].rearrange("p t c -> p (t c)"), ps[7][:, 0:16], ACT.Copy).then_inc(small_out, 1)
                    a.activation(lrT[:, :], ps[7][0:16, S:2 * S], ACT.Copy).then_inc(small_out, 1)

                def small_products(pe):
                    for t in range(TILES):
                        for k in range(KD):
                            nc.tensor.matmul(ps[7][:, 8 * t:8 * t + 8], hT[:, k, t * P:(t + 1) * P], small[:, k, 0:8],
                                             start=k == 0, stop=k == KD - 1)
                    for k in range(KD):
                        ins = nc.tensor.matmul(ps[7][0:16, S:2 * S], small[:, k, 8:24], hT[:, k, :],
                                               start=k == 0, stop=k == KD - 1)
                    ins.then_inc(small_done, 1)

                project("mix_in", ring, jobs, U_GGATE + 1, banks=7, extra={"tensor": small_products, "scalar": small_copy})
                dump("ain", ain[:, :, :])
                dump("tok8", tok8[:, :, :])

                work = sb("work", [P, 11, 4 * S], s2)

                def W(i, **kw):
                    return work[:, i, :] if not kw else work[:, i, :].rearrange(kw["to"], **kw["sizes"])

                def blocks4(i):
                    return work[:, i, :].rearrange("p (c s) -> p c s", c=4)

                def tiles8(i):
                    return work[:, i, :].rearrange("p (g s) -> p g s", g=8)

                conv = Count(nc, "conv_step")
                xc = blocks4(0)
                silu_out = nc.alloc_semaphore("gdn_silu")
                gdn_conv = [blocks4(i) for i in (1, 2, 3)]

                def convolve(dve):
                    def one(dst, src, w_cols, bias):
                        w3 = par[:, w_cols[3]:w_cols[3] + 1]
                        if bias is None:
                            ins = v.tensor_scalar(dst, src, w3, None, ALU.mult)
                        else:
                            ins = v.tensor_scalar(dst, src, w3, bias, ALU.mult, ALU.add)
                        done(dve, ins, conv)
                        for k in range(3):
                            back = 3 - k
                            done(dve, v.scalar_tensor_tensor(dst[:, back:S], src[:, 0:S - back],
                                                             par[:, w_cols[k]:w_cols[k] + 1], dst[:, back:S],
                                                             ALU.mult, ALU.add), conv)
                    for c in range(4):
                        one(xc[:, c, :], ain[:, c, :], [CONV_A + 4 * k + c for k in range(4)],
                            par[:, CONV_B + c:CONV_B + c + 1])
                    for c in range(12):
                        one(gdn_conv[c // 4][:, c % 4, :], qkv[:, c, :], [CONV_G + 12 * k + c for k in range(4)], None)

                def silus(act):
                    for i in range(3):
                        act.wait_ge(conv.sem, 4 * 4 * (i + 2))
                        a.activation(qkv[:, 4 * i:4 * i + 4, :].rearrange("p c s -> p (c s)"), W(1 + i),
                                     ACT.Silu).then_inc(silu_out, 1)

                jobs = [Job(U_MERGE[b], "tok", t, 512, True,
                            (lambda dst: lambda src: a.activation(dst, src, ACT.Sigmoid))(
                                merge_gates[:, t, 512 * b:512 * b + 512])) for b in range(8) for t in range(TILES)]
                project("merge_gates", ring, jobs, U_MERGE[7] + 1, extra={"vector": convolve, "scalar": silus})
                dump("xc", xc)
                dump("qkv", qkv[:, :, :])

                lru(xc, blocks4, W, par, w_ax, yT[0], B_A, B_X, LAM)
                dump("ylru", yT[0][:, :, :])
                gdn(qkv, ggate, work, blocks4, tiles8, W, tok8, hrow, par[:, GDN_N:GDN_N + 1], yT[1])
                dump("ygdn", yT[1][:, :, :])

            yT[2] = sb("y_sb", [P, 4, S], s1)
            yT[3] = sb("y_gla", [P, 4, S], s1)
            with ExitStack() as s2:
                q = sb("gla_q", [P, 4, S], s2)
                k = sb("gla_k", [P, 4, S], s2)
                vt = sb("gla_v", [P, TILES, 512], s2)
                lgate = sb("gla_gate", [P, 4, S], s2)
                with ExitStack() as s3:
                    sq = sb("sb_q", [P, 4, S], s3)
                    sk = sb("sb_k", [P, 4, S], s3)
                    sv = sb("sb_v", [P, TILES, 512], s3)
                    jobs = []
                    for (uq, uk, uv), (dq, dk, dv) in ((U_SB, (sq, sk, sv)), (U_GLA, (q, k, vt))):
                        for u, dst in ((uq, dq), (uk, dk)):
                            jobs += [fm_job(u, b, b % 2 == 0, dst[:, b, :]) for b in range(4)]
                        jobs += [Job(uv, "tok", t, 512, t == 0, copy_out(t == 0, dv[:, t, :])) for t in range(TILES)]
                    jobs += [fm_job(U_LGATE, b, True, lgate[:, b, :], ACT.Silu) for b in range(4)]
                    project("mix_in_2", ring, jobs, U_LGATE + 1)
                    stick_breaking(sq, sk, sv, yT[2], s3)
                    dump("ysb", yT[2][:, :, :])
                gla(q, k, vt, lgate, lrT, w_up, par, GLA_B, par[:, GLA_N:GLA_N + 1], yT[3], s2)
                dump("ygla", yT[3][:, :, :])

            with ExitStack() as s2:
                m = sb("mixer_sum", [P, TILES, D], s2)
                part = sb("mixer_part", [P, 512], s2)
                step = Count(nc, "mixer_step")
                jobs = []
                for n in range(4):
                    for nb in range(2):
                        for t in range(TILES):
                            def out(src, n=n, nb=nb, t=t):
                                gate = merge_gates[:, t, n * D + nb * 512:n * D + nb * 512 + 512]
                                dst = m[:, t, nb * 512:nb * 512 + 512]
                                if n == 0:
                                    return v.tensor_tensor(dst, src, gate, ALU.mult)
                                done(v, v.tensor_tensor(part[:, :], src, gate, ALU.mult), step)
                                return v.tensor_tensor(dst, dst, part[:, :], ALU.add)

                            jobs.append(Job(U_BR + n, "tok", t, 512, False, out, last=nb == 1 and t == 1, k=4, lhs=yT[n],
                                            unit_width=D, col0=512 * nb))
                project("mixer_merge", ring, jobs, U_OUT)
                transpose_block("mixer_T", m, hT)
            jobs = []
            for nb in range(2):
                for t in range(TILES):
                    cut = slice(nb * 512, nb * 512 + 512)

                    def out(src, t=t, cut=cut):
                        return v.scalar_tensor_tensor(x[:, t, cut], x[:, t, cut], ALPHA, src, ALU.mult, ALU.add)

                    jobs.append(Job(U_OUT + nb, "tok", t, 512, False, out))
            project("mixer_out", ring, jobs, U_HID)

        def cols2(name, c0, c1):
            return A[name][0, :, c0:c1].rearrange("(k p) n -> p k n", p=P)

        def lru(xc, blocks4, W, par, w_ax, y, B_A, B_X, LAM):
            v, a = nc.vector, nc.scalar
            R, I, T, M, N = 1, 2, 3, 4, 5
            summed, squashed, step, acted, coef_ready = (Count(nc, f"lru_{n}") for n in
                                                         ("summed", "squashed", "step", "acted", "coef"))
            with ExitStack() as st:
                cf = sb("lru_coef", [P, 4, 4], st)
                with nc.Block() as block:
                    @block.tensor
                    def _(pe):
                        for i in range(2):
                            for c in range(4):
                                ins = nc.tensor.matmul(ps[2 * i + c // 2][:, (c % 2) * S:(c % 2 + 1) * S],
                                                       w_ax[:, i, c, :], xc[:, c, :], start=True, stop=True)
                            ins.then_inc(summed.sem, 1)

                    @block.scalar
                    def _(act):
                        for i, (B, dst) in enumerate(((B_A, R), (B_X, I))):
                            act.wait_ge(summed.sem, i + 1)
                            for c in range(4):
                                ins = a.activation(blocks4(dst)[:, c, :], ps[2 * i + c // 2][:, (c % 2) * S:(c % 2 + 1) * S],
                                                   ACT.Sigmoid, bias=par[:, B + c:B + c + 1])
                                ins.then_inc(squashed.sem, 1)
                        act.wait_ge(step.sem, 1)
                        done(act, a.activation(cf[:, 1, :], cf[:, 0, :], ACT.Exp), coef_ready)
                        done(act, a.activation(cf[:, 2, :], cf[:, 1, :], ACT.Ln, bias=1.0), coef_ready)
                        act.wait_ge(step.sem, 8)
                        done(act, a.activation(W(M), W(T), ACT.Tanh), acted)
                        done(act, a.activation(W(R), W(T), ACT.Exp), acted)
                        act.wait_ge(step.sem, 11)
                        done(act, a.activation(W(N), W(T), ACT.Sqrt), acted)

                    @block.vector
                    def _(dve):
                        def do(ins):
                            done(dve, ins, step)
                        lam = par[:, LAM:LAM + 4]
                        do(v.scalar_tensor_tensor(cf[:, 0, :], lam, -1.0, lam, ALU.mult, ALU.min))
                        do(v.tensor_scalar(cf[:, 3, :], lam, -1.0, 0.0, ALU.mult, ALU.max))
                        dve.wait_ge(coef_ready.sem, 2)
                        do(v.tensor_tensor(cf[:, 3, :], cf[:, 3, :], cf[:, 2, :], ALU.add))
                        do(v.tensor_scalar(cf[:, 3, :], cf[:, 3, :], -8.0, None, ALU.mult))
                        dve.wait_ge(squashed.sem, 8)
                        for c in range(4):
                            do(v.tensor_scalar(blocks4(T)[:, c, :], blocks4(R)[:, c, :], cf[:, 3, c:c + 1], None, ALU.mult))
                        dve.wait_ge(acted.sem, 2)
                        do(v.tensor_scalar(W(T), W(M), -1.0, 1.0, ALU.mult, ALU.add))
                        do(v.reciprocal(W(N), W(T)))
                        do(v.scalar_tensor_tensor(W(T), W(M), -2.0, W(N), ALU.mult, ALU.mult))
                        dve.wait_ge(acted.sem, 3)
                        do(v.memset(blocks4(N)[:, :, 0:1], 1.0))
                        do(v.tensor_tensor(W(N), W(N), W(I), ALU.mult))
                        do(v.tensor_tensor(W(N), W(N), W(0), ALU.mult))
                        for c in range(4):
                            do(v.tensor_tensor_scan(y[:, c, :], blocks4(R)[:, c, :], blocks4(N)[:, c, :], 0.0,
                                                    ALU.mult, ALU.add))

        def head_norm(tag, oT, sqT, rsT, gain, gate, y):
            v, a = nc.vector, nc.scalar
            squared, summed, rooted, step = (Count(nc, f"{tag}_{n}") for n in ("squared", "summed", "rooted", "step"))
            with nc.Block() as block:
                @block.vector
                def _(dve):
                    done(dve, v.tensor_tensor(sqT, oT, oT, ALU.mult), squared)
                    for b in range(2):
                        cut = slice(512 * b, 512 * b + 512)
                        dve.wait_ge(summed.sem, b + 1)
                        done(dve, v.tensor_scalar(rsT[:, cut], ps[b][:, :], 1.0 / P, EPS, ALU.mult, ALU.add), step)
                    dve.wait_ge(rooted.sem, 1)
                    done(dve, v.reciprocal(rsT, rsT), step)
                    done(dve, v.scalar_tensor_tensor(y, oT, gain, gate, ALU.mult, ALU.mult), step)
                    done(dve, v.tensor_tensor(y, y, rsT, ALU.mult), step)

                @block.tensor
                def _(pe):
                    pe.wait_ge(squared.sem, 1)
                    for b in range(2):
                        nc.tensor.matmul(ps[b][:, :], ones, sqT[:, 512 * b:512 * b + 512], start=True,
                                         stop=True).then_inc(summed.sem, 1)

                @block.scalar
                def _(act):
                    act.wait_ge(step.sem, 2)
                    a.activation(rsT, rsT, ACT.Sqrt).then_inc(rooted.sem, 1)

        def gdn(qkv, ggate, work, blocks4, tiles8, W, tok8, hrow, gain, y):
            v, a = nc.vector, nc.scalar
            qT = qkv[:, 0:4, :].rearrange("p c s -> p (c s)")
            kT = qkv[:, 4:8, :].rearrange("p c s -> p (c s)")
            vT = qkv[:, 8:12, :].rearrange("p c s -> p (c s)")
            SQ, RS = 0, 1
            ROW, BROW, DT, AT, ATT, AN, AM, U, TN, Y = 0, 1, 2, 3, 4, 5, 6, 7, 8, 9
            EXTRA = 10
            VK = qkv[:, 8:12, :]

            def g8(flat):
                return flat.rearrange("p (g s) -> p g s", g=8)

            with ExitStack() as st:
                tg = sb("gdn_tok", [P, 8, 8], st)
                BETA, G, GC, GL, BE, KD_, T1, T2 = range(8)
                tq = {i: tg[:, i, :] for i in range(8)}

                def by_tile(i):
                    return tg[:, i, :].rearrange("p (h t) -> p t h", t=2)

                step, squared, summed, rooted = (Count(nc, f"gdn_l2_{n}") for n in ("step", "squared", "summed", "rooted"))
                with nc.Block() as block:
                    @block.vector
                    def _(dve):
                        done(dve, v.tensor_tensor(W(SQ), qT, qT, ALU.mult), squared)
                        done(dve, v.tensor_tensor(W(2), kT, kT, ALU.mult), squared)
                        for i in range(2):
                            rs = W(1 + 2 * i)
                            for b in range(2):
                                dve.wait_ge(summed.sem, 2 * i + b + 1)
                                done(dve, v.tensor_scalar(rs[:, 512 * b:512 * b + 512], ps[2 * i + b][:, :], EPS, None,
                                                          ALU.add), step)
                        dve.wait_ge(rooted.sem, 2)
                        for i, z in enumerate((qT, kT)):
                            rs = W(1 + 2 * i)
                            done(dve, v.reciprocal(rs, rs), step)
                            done(dve, v.scalar_tensor_tensor(z, z, P ** -0.5 if i == 0 else 1.0, rs, ALU.mult, ALU.mult), step)
                        d = by_tile(T1)
                        bc = [P, TILES, 4]
                        done(dve, v.tensor_tensor(d, tok8[:, :, 4:8], hrow[:, 4:8].unsqueeze(1).broadcast_to(bc), ALU.add), step)
                        done(dve, v.tensor_scalar(tq[G], tq[T1], 0.0, None, ALU.max), step)
                        done(dve, v.scalar_tensor_tensor(tq[T1], tq[T1], -1.0, tq[T1], ALU.mult, ALU.min), step)
                        dve.wait_ge(rooted.sem, 6)
                        done(dve, v.tensor_tensor(tq[G], tq[G], tq[T2], ALU.add), step)
                        done(dve, v.tensor_tensor(by_tile(G), by_tile(G), hrow[:, 0:4].unsqueeze(1).broadcast_to(bc), ALU.mult), step)
                        done(dve, v.tensor_scalar(tq[G], tq[G], -1.0, None, ALU.mult), step)

                    @block.tensor
                    def _(pe):
                        for i in range(2):
                            pe.wait_ge(squared.sem, i + 1)
                            for b in range(2):
                                nc.tensor.matmul(ps[2 * i + b][:, :], ones, W(2 * i)[:, 512 * b:512 * b + 512],
                                                 start=True, stop=True).then_inc(summed.sem, 1)

                    @block.scalar
                    def _(act):
                        for i in range(2):
                            act.wait_ge(step.sem, 2 * i + 2)
                            done(act, a.activation(W(1 + 2 * i), W(1 + 2 * i), ACT.Sqrt), rooted)
                        done(act, a.activation(by_tile(BETA), tok8[:, :, 0:4], ACT.Sigmoid), rooted)
                        act.wait_ge(step.sem, 11)
                        done(act, a.activation(hrow[:, 0:4], hrow[:, 0:4], ACT.Exp), rooted)
                        done(act, a.activation(tq[T2], tq[T1], ACT.Exp), rooted)
                        done(act, a.activation(tq[T2], tq[T2], ACT.Ln, bias=1.0), rooted)

                mm = Count(nc, "gdn_a_mm")
                step, acted = Count(nc, "gdn_a_step"), Count(nc, "gdn_a_act")
                with nc.Block() as block:
                    @block.tensor
                    def _(pe):
                        nc.tensor.matmul(ps[0][:, 0:8], const("cum64"), tq[G], start=True, stop=True)
                        nc.tensor.matmul(ps[0][:, 8:16], const("blk64"), tq[G], start=True, stop=True).then_inc(mm.sem, 1)
                        pe.wait_ge(step.sem, 2)
                        for g in range(8):
                            ins = nc.tensor.matmul(ps[1 + g // 4][:, (g % 4) * P:(g % 4 + 1) * P], g8(W(AM))[:, g, :],
                                                   const("cum64"), start=True, stop=True)
                        ins.then_inc(mm.sem, 1)
                        for g in range(8):
                            ins = nc.tensor.matmul(ps[3 + g // 4][:, (g % 4) * P:(g % 4 + 1) * P], g8(W(U))[:, g, :],
                                                   ident, start=True, stop=True)
                        ins.then_inc(mm.sem, 1)
                        for g in range(8):
                            ins = nc.tensor.matmul(ps[5 + g // 4][:, (g % 4) * P:(g % 4 + 1) * P], g8(kT)[:, g, :],
                                                   g8(kT)[:, g, :], start=True, stop=True)
                        ins.then_inc(mm.sem, 1)
                        pe.wait_ge(acted.sem, 2)
                        for g in range(8):
                            ins = nc.tensor.matmul(ps[1 + g // 4][:, (g % 4) * P:(g % 4 + 1) * P], g8(kT)[:, g, :],
                                                   g8(qT)[:, g, :], start=True, stop=True)
                        ins.then_inc(mm.sem, 1)

                    @block.scalar
                    def _(act):
                        act.wait_ge(mm.sem, 2)
                        for b in range(2):
                            done(act, a.activation(W(ROW)[:, 512 * b:512 * b + 512], ps[1 + b][:, :], ACT.Copy), acted)
                        act.wait_ge(mm.sem, 3)
                        for b in range(2):
                            done(act, a.activation(W(BROW)[:, 512 * b:512 * b + 512], ps[3 + b][:, :], ACT.Copy), acted)
                        act.wait_ge(step.sem, 12)
                        done(act, a.activation(W(DT), W(DT), ACT.Exp), acted)
                        done(act, a.activation(W(ROW), W(ROW), ACT.Exp), acted)
                        done(act, a.activation(tq[BE], tq[GC], ACT.Exp), acted)
                        done(act, a.activation(tq[KD_], tq[KD_], ACT.Exp), acted)

                    @block.vector
                    def _(dve):
                        def do(ins):
                            done(dve, ins, step)
                        bc = [P, 8, P]
                        do(v.tensor_copy(g8(W(AM)), tq[G].unsqueeze(2).broadcast_to(bc)))
                        do(v.tensor_copy(g8(W(U)), tq[BETA].unsqueeze(2).broadcast_to(bc)))
                        dve.wait_ge(mm.sem, 1)
                        do(v.tensor_copy(tq[GC], ps[0][:, 0:8]))
                        do(v.tensor_tensor(tq[KD_], ps[0][:, 8:16], tq[GC], ALU.subtract))
                        dve.wait_ge(acted.sem, 2)
                        for g in range(8):
                            do(v.tensor_scalar(g8(W(DT))[:, g, :], g8(W(ROW))[:, g, :], tq[GC][:, g:g + 1], 0.0,
                                               ALU.subtract, ALU.min))
                        dve.wait_ge(acted.sem, 7)
                        do(v.tensor_tensor(tq[BE], tq[BE], tq[BETA], ALU.mult))
                        do(v.tensor_tensor(g8(W(AN)), g8(W(DT)), const("strict64").unsqueeze(1).broadcast_to(bc), ALU.mult))
                        do(v.tensor_tensor(W(AN), W(AN), W(BROW), ALU.mult))
                        do(v.tensor_tensor(g8(W(DT)), g8(W(DT)), const("cum64").unsqueeze(1).broadcast_to(bc), ALU.mult))
                        dve.wait_ge(mm.sem, 5)
                        for b in range(2):
                            cut = slice(512 * b, 512 * b + 512)
                            do(v.tensor_tensor(W(AT)[:, cut], W(AN)[:, cut], ps[5 + b][:, :], ALU.mult))
                            do(v.tensor_tensor(W(ATT)[:, cut], W(DT)[:, cut], ps[1 + b][:, :], ALU.mult))

                step, mm, yout = Count(nc, "gdn_inv_step"), Count(nc, "gdn_inv_mm"), Count(nc, "gdn_inv_y")
                base = {}
                levels = (2, 4, 8, 16, 32)
                with nc.Block() as block:
                    bc = [P, 8, P]

                    @block.vector
                    def _(dve):
                        def do(ins):
                            done(dve, ins, step)
                        dve.wait_ge(mm.sem, 1)
                        for b in range(2):
                            do(v.tensor_copy(W(AN)[:, 512 * b:512 * b + 512], ps[b][:, :]))
                        for dst, src, mask in ((U, AT, "level1_t"), (TN, AN, "level1")):
                            do(v.tensor_tensor(g8(W(dst)), g8(W(src)), const(mask).unsqueeze(1).broadcast_to(bc), ALU.mult))
                            do(v.tensor_tensor(g8(W(dst)), ident.unsqueeze(1).broadcast_to(bc), g8(W(dst)), ALU.subtract))
                        for n, s in enumerate(levels):
                            do(v.tensor_tensor(g8(W(AM)), g8(W(AN)), const(f"level{s}").unsqueeze(1).broadcast_to(bc), ALU.mult))
                            dve.wait_ge(mm.sem, 3 + 2 * n)
                            for b in range(2):
                                cut = slice(512 * b, 512 * b + 512)
                                do(v.tensor_tensor(W(U)[:, cut], W(U)[:, cut], ps[4 + b][:, :], ALU.subtract))
                                do(v.tensor_tensor(W(TN)[:, cut], W(TN)[:, cut], ps[6 + b][:, :], ALU.subtract))

                    @block.tensor
                    def _(pe):
                        for g in range(8):
                            ins = nc.tensor.transpose(ps[g // 4][:, (g % 4) * P:(g % 4 + 1) * P], g8(W(AT))[:, g, :], ident)
                        ins.then_inc(mm.sem, 1)
                        for n in range(5):
                            pe.wait_ge(step.sem, 7 + 5 * n)
                            for g in range(8):
                                ins = nc.tensor.matmul(ps[2 + g // 4][:, (g % 4) * P:(g % 4 + 1) * P], g8(W(AM))[:, g, :],
                                                       g8(W(U))[:, g, :], start=True, stop=True)
                            ins.then_inc(mm.sem, 1)
                            pe.wait_ge(yout.sem, 2 * n + 2)
                            for g in range(8):
                                nc.tensor.matmul(ps[4 + g // 4][:, (g % 4) * P:(g % 4 + 1) * P], g8(W(TN))[:, g, :],
                                                 g8(W(Y))[:, g, :], start=True, stop=True)
                            for g in range(8):
                                ins = nc.tensor.matmul(ps[6 + g // 4][:, (g % 4) * P:(g % 4 + 1) * P], g8(W(Y))[:, g, :],
                                                       g8(W(TN))[:, g, :], start=True, stop=True)
                            ins.then_inc(mm.sem, 1)

                    @block.scalar
                    def _(act):
                        for n in range(5):
                            act.wait_ge(mm.sem, 2 + 2 * n)
                            for b in range(2):
                                done(act, a.activation(W(Y)[:, 512 * b:512 * b + 512], ps[2 + b][:, :], ACT.Copy), yout)
                dump("gdnU", W(U))

                KBE, KDEC, VB, WT, UU, QD = 5, 6, 2, 8, 9, 3
                step, mm, acted = Count(nc, "gdn_w_step"), Count(nc, "gdn_w_mm"), Count(nc, "gdn_w_act")
                with nc.Block() as block:
                    @block.tensor
                    def _(pe):
                        for i, z in enumerate((kT, vT)):
                            for g in range(8):
                                ins = nc.tensor.transpose(ps[2 * i + g // 4][:, (g % 4) * P:(g % 4 + 1) * P], g8(z)[:, g, :], ident)
                            ins.then_inc(mm.sem, 1)
                        pe.wait_ge(acted.sem, 16)
                        for g in range(8):
                            ins = nc.tensor.matmul(ps[4 + g // 4][:, (g % 4) * P:(g % 4 + 1) * P], g8(W(KBE))[:, g, :],
                                                   g8(W(U))[:, g, :], start=True, stop=True)
                        ins.then_inc(mm.sem, 1)
                        for g in range(8):
                            ins = nc.tensor.matmul(ps[6 + g // 4][:, (g % 4) * P:(g % 4 + 1) * P], g8(W(U))[:, g, :],
                                                   g8(W(VB))[:, g, :], start=True, stop=True)
                        ins.then_inc(mm.sem, 1)

                    @block.scalar
                    def _(act):
                        for n, (dst, bank, colq) in enumerate(((KBE, 0, BE), (VB, 2, BETA))):
                            act.wait_ge(mm.sem, n + 1)
                            for g in range(8):
                                done(act, a.activation(g8(W(dst))[:, g, :], ps[bank + g // 4][:, (g % 4) * P:(g % 4 + 1) * P],
                                                       ACT.Copy, scale=tq[colq][:, g:g + 1]), acted)
                        act.wait_ge(mm.sem, 3)
                        for b in range(2):
                            done(act, a.activation(W(WT)[:, 512 * b:512 * b + 512], ps[4 + b][:, :], ACT.Copy), acted)

                    @block.vector
                    def _(dve):
                        def do(ins):
                            done(dve, ins, step)
                        do(v.tensor_tensor(W(QD), qT, W(ROW), ALU.mult))
                        dve.wait_ge(acted.sem, 8)
                        for g in range(8):
                            do(v.tensor_scalar(g8(W(KDEC))[:, g, :], ps[g // 4][:, (g % 4) * P:(g % 4 + 1) * P],
                                               tq[KD_][:, g:g + 1], None, ALU.mult))
                        dve.wait_ge(mm.sem, 4)
                        for b in range(2):
                            do(v.tensor_copy(W(UU)[:, 512 * b:512 * b + 512], ps[6 + b][:, :]))

                step, mm = Count(nc, "gdn_scan_step"), Count(nc, "gdn_scan_mm")
                oT = W(5)
                with ExitStack() as s5:
                    state = W(10)[:, 0:512].rearrange("p (h d) -> p h d", h=4)
                    new = W(10)[:, 512:1024].rearrange("p (h d) -> p h d", h=4)
                    with nc.Block() as block:
                        @block.vector
                        def _(dve):
                            def do(ins):
                                done(dve, ins, step)
                            do(v.memset(state, 0.0))
                            uu = W(UU).rearrange("p (h t d) -> p h t d", h=4, t=2)
                            for n in range(4):
                                t, b0 = n // 2, 64 * (n % 2)
                                dve.wait_ge(mm.sem, 2 * n + 1)
                                do(v.tensor_tensor(new[b0:b0 + 64, :, :], uu[b0:b0 + 64, :, t, :],
                                                   ps[0][b0:b0 + 64, :].rearrange("p (h d) -> p h d", h=4), ALU.subtract))
                                dve.wait_ge(mm.sem, 2 * n + 2)
                                for h in range(4):
                                    do(v.scalar_tensor_tensor(state[:, h, :], state[:, h, :],
                                                              blocks4(ROW)[:, h, 64 * n + 63:64 * n + 64],
                                                              ps[1][:, h * P:(h + 1) * P], ALU.mult, ALU.add))

                        @block.tensor
                        def _(pe):
                            for n in range(4):
                                t, b0 = n // 2, 64 * (n % 2)
                                cut = slice(64 * n, 64 * n + 64)
                                pe.wait_ge(step.sem, 1 + 5 * n)
                                for h in range(4):
                                    ins = nc.tensor.matmul(ps[0][b0:b0 + 64, h * P:(h + 1) * P], blocks4(WT)[:, h, cut],
                                                           state[:, h, :], start=True, stop=True)
                                ins.then_inc(mm.sem, 1)
                                pe.wait_ge(step.sem, 2 + 5 * n)
                                for h in range(4):
                                    g = 2 * h + t
                                    out = ps[2 + h][:, cut]
                                    nc.tensor.matmul(out, state[:, h, :], blocks4(QD)[:, h, cut], start=True, stop=False)
                                    nc.tensor.matmul(out, new[b0:b0 + 64, h, :],
                                                     g8(W(ATT))[b0:b0 + 64, g, b0:b0 + 64], start=False, stop=True)
                                for h in range(4):
                                    g = 2 * h + t
                                    ins = nc.tensor.matmul(ps[1][:, h * P:(h + 1) * P], g8(W(KDEC))[b0:b0 + 64, g, :],
                                                           new[b0:b0 + 64, h, :], start=True, stop=True)
                                ins.then_inc(mm.sem, 1)
                    o_out = Count(nc, "gdn_o_out")
                    with nc.Block() as block:
                        @block.scalar
                        def _(act):
                            for h in range(4):
                                done(act, a.activation(blocks4(5)[:, h, :], ps[2 + h][:, 0:S], ACT.Copy), o_out)
                dump("gdnO", W(5))
            head_norm("gdn_norm", W(5), W(6), W(7), gain, ggate[:, :, :].rearrange("p c s -> p (c s)"),
                      y[:, :, :].rearrange("p c s -> p (c s)"))

        def stick_breaking(q, k, sv, y, s3):
            v, a = nc.vector, nc.scalar
            scale = 64 ** -0.5
            Wd = S + P
            with ExitStack() as st:
                ab = sb("sb_abs", [P, 2, Wd], st)
                score = sb("sb_score", [P, 2, Wd], st)
                keep = sb("sb_keep", [P, 2, Wd], st)
                wt = sb("sb_weights", [P, 2, Wd], st)
                scored, prepped, logged, kept, cumed, added, expd, masked, mixed, out, step = (
                    Count(nc, f"sb_{n}") for n in ("scored", "prepped", "logged", "kept", "cumed", "added", "expd",
                                                   "masked", "mixed", "out", "step"))
                exped = Count(nc, "sb_exped")
                strict = const("sb_strict")
                H = 8
                with nc.Block() as block:
                    @block.tensor
                    def _(pe):
                        for i in range(H + 2):
                            if i < H:
                                b0, c = 64 * (i % 2), i // 2
                                if i >= 2:
                                    pe.wait_ge(added.sem, i - 1)
                                kk, qq = k[b0:b0 + 64, c, :], q[b0:b0 + 64, c, :]
                                nc.tensor.matmul(ps[i % 2][:, 0:S], kk[:, 0:P], qq, start=True, stop=True)
                                nc.tensor.matmul(ps[i % 2][:, S:Wd], kk[:, P:S], qq[:, P:S], start=True,
                                                 stop=True).then_inc(scored.sem, 1)
                            if 1 <= i <= H:
                                n = i - 1
                                pe.wait_ge(kept.sem, n + 1)
                                if n >= 2:
                                    pe.wait_ge(added.sem, n - 1)
                                kp = keep[:, n % 2, :]
                                bank = ps[2 + n % 2]
                                nc.tensor.matmul(bank[:, 0:S], const("sb_incl"), kp[:, 0:S], start=True, stop=False)
                                nc.tensor.matmul(bank[:, P:S], ones, kp[:, S:Wd], start=False, stop=True)
                                nc.tensor.matmul(bank[:, S:Wd], const("sb_incl"), kp[:, S:Wd], start=True,
                                                 stop=True).then_inc(cumed.sem, 1)
                            if i >= 2:
                                n = i - 2
                                pe.wait_ge(masked.sem, n + 1)
                                if n >= 2:
                                    pe.wait_ge(out.sem, n - 1)
                                b0 = 64 * (n % 2)
                                o = ps[4 + n % 2][b0:b0 + 64, :]
                                nc.tensor.matmul(o[:, 0:S], sv[:, 0, 64 * n:64 * n + 64], wt[:, n % 2, 0:S], start=True, stop=False)
                                nc.tensor.matmul(o[:, P:S], sv[:, 1, 64 * n:64 * n + 64], wt[:, n % 2, S:Wd], start=False,
                                                 stop=True).then_inc(mixed.sem, 1)

                    @block.vector
                    def _(dve):
                        for i in range(H + 2):
                            if i < H:
                                dve.wait_ge(scored.sem, i + 1)
                                z = ps[i % 2][:, 0:Wd]
                                if i >= 2:
                                    dve.wait_ge(cumed.sem, i - 1)
                                zs = score[:, i % 2, :]
                                done(dve, v.tensor_scalar(zs, z, scale, None, ALU.mult), step)
                                v.scalar_tensor_tensor(ab[:, i % 2, :], zs, -1.0, zs, ALU.mult, ALU.min) \
                                    .then_inc(prepped.sem, 1)
                            if 1 <= i <= H:
                                n = i - 1
                                dve.wait_ge(cumed.sem, n + 1)
                                if n >= 2:
                                    dve.wait_ge(mixed.sem, n - 1)
                                v.tensor_tensor(wt[:, n % 2, :], score[:, n % 2, :], ps[2 + n % 2][:, 0:Wd],
                                                ALU.add).then_inc(added.sem, 1)
                            if i < H:
                                dve.wait_ge(logged.sem, i + 1)
                                kp, lg = keep[:, i % 2, :], ab[:, i % 2, :]
                                done(dve, v.scalar_tensor_tensor(lg, score[:, i % 2, :], 0.0, lg, ALU.max, ALU.add), step)
                                v3 = v.scalar_tensor_tensor
                                done(dve, v3(kp[:, 0:P], lg[:, 0:P], -1.0, strict, ALU.mult, ALU.mult), step)
                                done(dve, v.tensor_scalar(kp[:, P:S], lg[:, P:S], -1.0, None, ALU.mult), step)
                                v3(kp[:, S:Wd], lg[:, S:Wd], -1.0, strict, ALU.mult, ALU.mult).then_inc(kept.sem, 1)
                            if 1 <= i <= H:
                                n = i - 1
                                dve.wait_ge(expd.sem, n + 1)
                                done(dve, v.tensor_tensor(wt[:, n % 2, 0:P], wt[:, n % 2, 0:P], strict, ALU.mult), step)
                                v.tensor_tensor(wt[:, n % 2, S:Wd], wt[:, n % 2, S:Wd], strict, ALU.mult).then_inc(masked.sem, 1)
                            if i >= 2:
                                n = i - 2
                                b0 = 64 * (n % 2)
                                dve.wait_ge(mixed.sem, n + 1)
                                v.tensor_copy(y[b0:b0 + 64, n // 2, :], ps[4 + n % 2][b0:b0 + 64, 0:S]).then_inc(out.sem, 1)

                    @block.scalar
                    def _(act):
                        for i in range(H + 1):
                            if i < H:
                                act.wait_ge(prepped.sem, i + 1)
                                z = ab[:, i % 2, :]
                                done(act, a.activation(z, z, ACT.Exp), exped)
                                a.activation(z, z, ACT.Ln, bias=1.0).then_inc(logged.sem, 1)
                            if i >= 1:
                                n = i - 1
                                act.wait_ge(added.sem, n + 1)
                                w = wt[:, n % 2, :]
                                a.activation(w, w, ACT.Exp).then_inc(expd.sem, 1)

        def gla(q, k, vt, lgate, lrT, w_up, par, GLA_B, gain, y, s2):
            v, a = nc.vector, nc.scalar
            with ExitStack() as st:
                bc_ = sb("gla_bcum", [P, 4 * S], st)
                eb = sb("gla_exp", [P, 4 * S], st)
                kd = sb("gla_kdT", [P, 4 * S], st)
                at = hT[:, 0:4, :].rearrange("p c (t s) -> p (c t) s", t=2)
                kt = hT[:, 4:8, :].rearrange("p c (t s) -> p (c t) s", t=2)
                vx = sb("gla_v_pairs", [P, TILES, 4, 2, P], st)
                states = sb("gla_states", [P, 2, 16, P], st)
                flat = "p c s -> p (c s)"
                qf, kf = q[:, :, :].rearrange(flat), k[:, :, :].rearrange(flat)
                mm, step, acted = (Count(nc, f"gla_{n}") for n in ("mm", "step", "acted"))
                with nc.Block() as block:
                    @block.tensor
                    def _(pe):
                        for c in range(4):
                            ins = nc.tensor.matmul(ps[c // 2][:, (c % 2) * S:(c % 2 + 1) * S], w_up[:, c * P:(c + 1) * P],
                                                   lrT[:, :], start=True, stop=True)
                        ins.then_inc(mm.sem, 1)
                        pe.wait_ge(step.sem, 9)
                        for g in range(8):
                            ins = nc.tensor.matmul(ps[2 + g // 4][:, (g % 4) * P:(g % 4 + 1) * P], kf[:, g * P:(g + 1) * P],
                                                   qf[:, g * P:(g + 1) * P], start=True, stop=True)
                        ins.then_inc(mm.sem, 1)
                        for g in range(8):
                            ins = nc.tensor.transpose(ps[4 + g // 4][:, (g % 4) * P:(g % 4 + 1) * P], kd[:, g * P:(g + 1) * P], ident)
                        ins.then_inc(mm.sem, 1)

                    @block.scalar
                    def _(act):
                        act.wait_ge(mm.sem, 1)
                        for c in range(4):
                            done(act, a.activation(bc_[:, c * S:(c + 1) * S], ps[c // 2][:, (c % 2) * S:(c % 2 + 1) * S],
                                                   ACT.Identity, bias=par[:, GLA_B + c:GLA_B + c + 1]), acted)
                        act.wait_ge(step.sem, 2)
                        done(act, a.activation(eb[:, :], eb[:, :], ACT.Exp), acted)
                        done(act, a.activation(eb[:, :], eb[:, :], ACT.Ln, bias=1.0), acted)
                        act.wait_ge(step.sem, 4)
                        done(act, a.activation(eb[:, :], bc_[:, :], ACT.Exp, scale=1.0 / 16), acted)
                        act.wait_ge(step.sem, 5)
                        done(act, a.activation(kd[:, :], kd[:, :], ACT.Exp, scale=1.0 / 16), acted)
                        done(act, a.activation(bc_[:, :], bc_[:, :], ACT.Exp, scale=-1.0 / 16), acted)
                        act.wait_ge(mm.sem, 3)
                        for b in range(2):
                            done(act, a.activation(kt[:, 4 * b:4 * b + 4, :].rearrange("p g d -> p (g d)"), ps[4 + b][:, :],
                                                   ACT.Copy), acted)

                    @block.vector
                    def _(dve):
                        def do(ins):
                            done(dve, ins, step)
                        dve.wait_ge(acted.sem, 4)
                        do(v.scalar_tensor_tensor(eb[:, :], bc_[:, :], -1.0, bc_[:, :], ALU.mult, ALU.min))
                        do(v.tensor_scalar(bc_[:, :], bc_[:, :], 0.0, None, ALU.min))
                        dve.wait_ge(acted.sem, 6)
                        do(v.tensor_tensor(bc_[:, :], bc_[:, :], eb[:, :], ALU.subtract))
                        do(v.tensor_tensor_scan(bc_[:, :], const("restart16"), bc_[:, :], 0.0, ALU.mult, ALU.add))
                        b3 = bc_[:, :].rearrange("p (n s) -> p n s", s=16)
                        do(v.tensor_tensor(kd[:, :].rearrange("p (n s) -> p n s", s=16),
                                           b3[:, :, 15:16].broadcast_to([P, 64, 16]), b3, ALU.subtract))
                        dve.wait_ge(acted.sem, 9)
                        do(v.scalar_tensor_tensor(qf, qf, P ** -0.5, eb[:, :], ALU.mult, ALU.mult))
                        do(v.tensor_tensor(kd[:, :], kd[:, :], kf, ALU.mult))
                        do(v.tensor_tensor(kf, kf, bc_[:, :], ALU.mult))
                        for par_ in range(2):
                            last = v.tensor_scalar(vx[:, :, :, par_, :], vt[:, :, :].rearrange("p t (h d) -> p t h d", h=4),
                                                   const("parity")[:, par_:par_ + 1], None, ALU.mult)
                            do(last)
                        dve.wait_ge(mm.sem, 2)
                        for b in range(2):
                            do(v.tensor_tensor(at[:, 4 * b:4 * b + 4, :], ps[2 + b][:, :].rearrange("p (g s) -> p g s", g=4),
                                               const("causal16").unsqueeze(1).broadcast_to([P, 4, P]), ALU.mult))
                dump("glab", eb[:, :])
                mm, step, acted = (Count(nc, f"gla_scan_{n}") for n in ("mm", "step", "acted"))
                oT = kd[:, :]
                with nc.Block() as block:
                    @block.tensor
                    def _(pe):
                        def updates(h):
                            if h >= 1:
                                pe.wait_ge(step.sem, 16 * h)
                            for pr in range(8):
                                t, b0 = pr // 4, 32 * (pr % 4)
                                ins = nc.tensor.matmul(ps[pr % 4][:, t * S:(t + 1) * S], kt[b0:b0 + 32, 2 * h + t, :],
                                                       vx[b0:b0 + 32, t, h, :, :].rearrange("p a d -> p (a d)"),
                                                       start=True, stop=True, tile_position=(b0, 0))
                            ins.then_inc(mm.sem, 1)

                        def outputs(h):
                            if h >= 2:
                                pe.wait_ge(acted.sem, h - 1)
                            bank = ps[4 + h % 2]
                            for t in range(TILES):
                                nc.tensor.matmul(bank[:, t * P:(t + 1) * P], vt[:, t, h * P:(h + 1) * P], at[:, 2 * h + t, :],
                                                 start=t == 0, stop=False, skip_group_check=True)
                            pe.wait_ge(step.sem, 16 * (h + 1))
                            for n in range(1, 16):
                                ins = nc.tensor.matmul(bank[:, 16 * n:16 * n + 16], states[:, h % 2, n, :],
                                                       q[:, h, 16 * n:16 * n + 16], start=False, stop=n == 15,
                                                       skip_group_check=True)
                            ins.then_inc(mm.sem, 1)

                        for h in range(5):
                            if h < 4:
                                updates(h)
                            if h >= 1:
                                outputs(h - 1)

                    @block.vector
                    def _(dve):
                        def do(ins):
                            done(dve, ins, step)
                        e4 = eb[:, :].rearrange("p (h s) -> p h s", h=4)
                        for h in range(4):
                            if h >= 2:
                                dve.wait_ge(mm.sem, 2 * h - 1)
                            dve.wait_ge(mm.sem, max(2 * h, 1))
                            for n in range(16):
                                pr = n // 2
                                kv = ps[pr % 4][:, (pr // 4) * S + (n % 2) * P:(pr // 4) * S + (n % 2 + 1) * P]
                                if n == 15:
                                    do(v.memset(states[:, h % 2, 0, 0:1], 0.0))
                                elif n == 0:
                                    do(v.tensor_copy(states[:, h % 2, 1, :], kv))
                                else:
                                    do(v.scalar_tensor_tensor(states[:, h % 2, n + 1, :], states[:, h % 2, n, :],
                                                              e4[:, h, 16 * n + 15:16 * n + 16], kv, ALU.mult, ALU.add))

                    @block.scalar
                    def _(act):
                        for h in range(4):
                            act.wait_ge(mm.sem, 2 * h + 3 if h < 3 else 8)
                            a.activation(oT[:, h * S:(h + 1) * S], ps[4 + h % 2][:, 0:S], ACT.Copy).then_inc(acted.sem, 1)
                dump("glaO", oT)
                head_norm("gla_norm", oT, bc_[:, :], eb[:, :], gain, lgate[:, :, :].rearrange(flat),
                          y[:, :, :].rearrange(flat))

        first_sem = nc.alloc_semaphore("layer_sems_from")
        with nc.Fori(0, DEPTH) as l:
            layer(l)
            last_sem = nc.alloc_semaphore("layer_sems_to")
            with nc.Block() as block:
                @block.gpsimd
                def _(pool):
                    pool.sem_clear(range(first_sem.num, last_sem.num))
        if "xl" in dbg:
            dump("xl", x[:, :, :])
            return
        nc.prepend_free_semaphores(list(range(first_sem.num, last_sem.num)))
        second_part()


NAMES = ("x", "c", "ada_w", "ada_b", "norm_mix_g", "norm_ffn_g", "w_in", "na_rpb", "mla_q_norm_g", "mla_kv_norm_g",
         "mla_w_uq", "mla_w_ukv", "gqa_q_norm_g", "gqa_k_norm_g", "w_br_na", "w_br_mla", "w_br_gqa", "w_out",
         "ffn_w_gate_up", "ffn_w_down", "final_norm_g", "w_in_2", "conv_a_w_2", "conv_a_b_2", "rg_w_a_2", "rg_b_a_2",
         "rg_w_x_2", "rg_b_x_2", "rg_lambda_2", "gdn_conv_w_2", "gdn_a_log_2", "gdn_dt_bias_2", "gdn_norm_w_2",
         "gla_w_gate_up_2", "gla_b_gate_2", "gla_norm_w_2", "w_branch_2", "w_out_2", "ln1_g_2", "ln1_b_2",
         "w_router_2", "router_bias_2", "w_gate_2", "w_up_2", "w_down_2", "ln2_g_2", "ln2_b_2")


def kernel(**inputs):
    import concourse.bacc as bacc
    from concourse.bass_utils import run_bass_kernel_spmd

    nc = bacc.Bacc("TRN2", target_bir_lowering=False, num_devices=1)
    arrays = {f"in_{name}": np.ascontiguousarray(inputs[name]) for name in NAMES}
    arrays["in_constants"] = np.ascontiguousarray(np.concatenate(list(constants().values()), axis=1))
    args = {k[3:]: nc.dram_tensor(k, a.shape, mybir.dt.from_np(a.dtype), kind="ExternalInput").ap()
            for k, a in arrays.items()}
    out = nc.dram_tensor("out", (1, S, D), FP, kind="ExternalOutput").ap()
    program(nc, args, out)
    result = run_bass_kernel_spmd(nc, [arrays], core_ids=[0])
    return result.results[0]["out"]
```

```python
import numpy as np
import concourse.bass as bass
from concourse import mybir
from contextlib import ExitStack

P = 128
D = 1024
S = 256
TILES = S // P
KD = D // P
DEPTH = 2
EPS = 1e-6
LN_EPS = 1e-5
GRID_W = 64
NEG = -1e30
FFN = 2816
IN1 = 5024
IN2 = 10264
N_EXPERTS = 16
D_EXPERT = 512
ALPHA = 2 ** 0.25
UNIT = 8 * 256
UNIT_W = 256

FP = mybir.dt.float32
FR = mybir.dt.float32r
ALU = mybir.AluOpType
ACT = mybir.ActivationFunctionType
AX = mybir.AxisListType.X


def constants():
    p = np.arange(P)
    j, i = p[:, None], p[None, :]
    c = {"ident": np.eye(P), "ones": np.ones((P, P))}
    qc, kc = (p % GRID_W)[:, None], np.arange(GRID_W)[None, :]
    start = np.clip(qc - 8, 0, GRID_W - 16)
    seen = (kc >= start) & (kc < start + 16)
    c["na_seen"] = seen
    c["na_neg"] = np.where(seen, 0.0, NEG)
    t = np.arange(S)

    def rotary(pos, half):
        inv = (1.0 / (np.float32(10000.0) ** (np.arange(half, dtype=np.float32) / half))).astype(np.float32)
        a = pos.astype(np.float32)[:, None] * inv[None, :]
        co, si = np.cos(a), np.sin(a)
        return np.stack([co, co], 1), np.stack([-si, si], 1)

    def tiled(a):
        return a.reshape(TILES, P, -1).transpose(1, 0, 2).reshape(P, -1)

    c["mla_cos"], c["mla_sin"] = (tiled(a) for a in rotary(t, 16))
    rows, cols = rotary(t // GRID_W, 16), rotary(t % GRID_W, 16)
    c["ax_cos"] = tiled(np.stack([rows[0], cols[0]], 1))
    c["ax_sin"] = tiled(np.stack([rows[1], cols[1]], 1))
    same64 = j // 64 == i // 64
    c["cum64"] = same64 & (j <= i)
    c["blk64"] = same64
    c["strict64"] = same64 & (j < i)
    for s in (1, 2, 4, 8, 16, 32):
        low = (j // (2 * s) == i // (2 * s)) & (j % (2 * s) >= s) & (i % (2 * s) < s)
        c[f"level{s}"] = low
    c["level1_t"] = c["level1"].T
    c["causal16"] = (j // 16 == i // 16) & (j <= i)
    c["sb_strict"] = j < i
    c["sb_incl"] = j >= i
    c["parity"] = np.stack([(p // 16) % 2 == 0, (p // 16) % 2 == 1], 1)
    c["restart16"] = np.broadcast_to((np.arange(4 * S) % 16 != 0)[None], (P, 4 * S))
    c["rank16"] = np.broadcast_to(np.arange(16, 0, -1)[None], (P, 16))
    c["rank4"] = np.broadcast_to(np.arange(4, 0, -1)[None], (P, 4))
    return {k: np.asarray(v, np.float32) for k, v in c.items()}


class Count:

    def __init__(self, nc, name):
        self.sem = nc.alloc_semaphore(name)
        self.n = 0


def done(eng, ins, s):
    ins.then_inc(s.sem, 1)
    s.n += 1
    eng.wait_ge(s.sem, s.n)


def signal(ins, s):
    ins.then_inc(s.sem, 1)
    s.n += 1


class Ring:

    def __init__(self, nc, name, raw, pair, units):
        self.nc, self.units, self.raw, self.pair = nc, units, raw, pair
        self.depth = raw.shape[1]
        self.landed = [nc.alloc_semaphore(f"{name}_landed{s}") for s in range(self.depth)]
        self.hi_done = nc.alloc_semaphore(f"{name}_hi_done")
        self.lo_done = nc.alloc_semaphore(f"{name}_lo_done")
        self.used = nc.alloc_semaphore(f"{name}_units_used")
        self.value, count = [], [0] * self.depth
        for n, parts in enumerate(units):
            count[n % self.depth] += 16 * len(parts)
            self.value.append(count[n % self.depth])
        self.size = [max(at + k * width for at, k, width, *_ in parts) for parts in units]
        self.issued = self.split_hi = self.split_lo = 0

    def feed(self, sp, end):
        for n in range(self.issued, min(end + self.depth + 1, len(self.units))):
            if n >= self.depth:
                sp.wait_ge(self.lo_done, n - self.depth + 1)
            for at, k, width, c0, c1, src in self.units[n]:
                dst = self.raw[:, n % self.depth, at:at + k * width].rearrange("p (k n) -> p k n", k=k)[:, :, c0:c1]
                sp.dma_start(dst, src).then_inc(self.landed[n % self.depth], 16)
            self.issued = n + 1

    def hi(self, act, through):
        for n in range(self.split_hi, min(through + 1, len(self.units))):
            act.wait_ge(self.landed[n % self.depth], self.value[n])
            if n >= 2:
                act.wait_ge(self.used, n - 1)
            self.nc.scalar.activation(self.pair[:, n % 2, 0, 0:self.size[n]], self.raw[:, n % self.depth, 0:self.size[n]],
                                      ACT.Copy).then_inc(self.hi_done, 1)
            self.split_hi = n + 1

    def lo(self, dve, through):
        for n in range(self.split_lo, min(through + 1, len(self.units))):
            dve.wait_ge(self.hi_done, n + 1)
            self.nc.vector.tensor_tensor(self.pair[:, n % 2, 1, 0:self.size[n]], self.raw[:, n % self.depth, 0:self.size[n]],
                                         self.pair[:, n % 2, 0, 0:self.size[n]].bitcast(FP),
                                         ALU.subtract).then_inc(self.lo_done, 1)
            self.split_lo = n + 1

    def arrived(self, pe, n):
        pe.wait_ge(self.lo_done, n + 1)

    def view(self, n, part, k, width, at=0):
        return self.pair[:, n % 2, part, at:at + k * width].rearrange("p (k n) -> p k n", k=k)


class Job:

    def __init__(self, unit, kind, idx, width, act, out, last=None, k=KD, lhs=None, at=0, unit_width=None, k0=0,
                 col0=0):
        self.unit, self.kind, self.idx, self.width, self.act, self.out = unit, kind, idx, width, act, out
        self.last = idx == 1 if last is None else last
        self.k, self.lhs, self.at, self.unit_width, self.k0, self.col0 = k, lhs, at, unit_width or UNIT_W, k0, col0


def program(nc, A, OUT, dbg=None):
    es = ExitStack()
    dbg = dbg or {}
    with es:
        def sb(name, shape, stack=es, dtype=FP):
            return stack.enter_context(nc.sbuf_tensor(name, shape, dtype))

        ps = [es.enter_context(nc.psum_tensor(f"bank{b}", [P, 512], FP)) for b in range(8)]
        layout, width = {}, 0
        for name, table in constants().items():
            layout[name] = (width, table.shape[1])
            width += table.shape[1]
        cst = sb("cst", [P, width])

        def const(name):
            at, n = layout[name]
            return cst[:, at:at + n]

        ident, ones = const("ident"), const("ones")
        x = sb("x", [P, TILES, D])
        hT = sb("hT", [P, KD, S])
        hP = sb("hT_pair", [P, 2, KD, S], dtype=FR)
        rstat = sb("rstat", [P, 8])
        half_neg = sb("half_neg", [P, 64])
        setup_loaded = nc.alloc_semaphore("setup_loaded")
        half_set = nc.alloc_semaphore("half_set")
        strips = nc.dram_tensor("na_bias_strips", [DEPTH, P, TILES * 4 * 256], FP, kind="Internal").ap()
        strips_written = nc.alloc_semaphore("strips_written")

        def dump(name, ap):
            if name in dbg:
                s = nc.alloc_semaphore("dbg" + name)
                with nc.Block() as block:
                    @block.sync
                    def _(sp):
                        sp.dma_start(dbg[name], ap).then_inc(s, 16)
                        sp.wait_ge(s, 16)

        with nc.Block() as block:
            @block.sync
            def _(sp):
                sp.dma_start(cst[:, :], A["constants"]).then_inc(setup_loaded, 16)
                sp.dma_start(x[:, :, :], A["x"].rearrange("o (t p) d -> p (o t) d", p=P)).then_inc(setup_loaded, 16)
                n = 0
                for l in range(DEPTH):
                    for qr in range(4):
                        for h in range(4):
                            src = bass.AP(A["na_rpb"].tensor, (l * 4 + h) * 465 + (7 - qr) * 31 + 15,
                                          [[31, 4], [-1, 64], [1, 64]])
                            at = ((qr // 2) * 4 + h) * 256
                            dst = strips[l, 64 * (qr % 2):64 * (qr % 2) + 64, at:at + 256]
                            sp.dma_start(dst.rearrange("p (r c) -> r p c", r=4), src).then_inc(strips_written, 16)
                            n += 16
                sp.wait_ge(setup_loaded, 32)
                sp.wait_ge(strips_written, n)

            @block.gpsimd
            def _(pool):
                pool.memset(half_neg[:, :], -0.5).then_inc(half_set, 1)

        def rsqrt_on_pool(pool, out, ms, n, s, mul, eps):
            done(pool, pool.tensor_scalar(ms, ms, mul, eps, ALU.mult, ALU.add), s)
            done(pool, pool.tensor_tensor(out, ms, half_neg[:, 0:n], ALU.pow), s)

        def evac(eng, act, out, in_):
            return nc.scalar.activation(out, in_, ACT.Copy) if act else nc.vector.tensor_copy(out, in_)

        def transpose_pe(pe, src, chunks, ready, s, bank0=0):
            for k in range(chunks):
                for t in range(TILES):
                    if ready is not None and k == 0:
                        pe.wait_ge(ready[0], ready[1][t])
                    ins = nc.tensor.transpose(ps[bank0 + k // 2][:, (k % 2) * S + t * P:(k % 2) * S + (t + 1) * P],
                                              src[:, t, k * P:(k + 1) * P], ident)
                if k % 2:
                    signal(ins, s)

        def rms_norm_to_fm(tag, scale=None, bias=None, row_gain=None, keep=False):
            with ExitStack() as st:
                junk = sb(f"{tag}_junk", [P, TILES, D], st)
                xn = sb(f"{tag}_xn", [P, TILES, D], st)
                squared, rooted, normed, turned, act_out, dve_out = (Count(nc, f"{tag}_{n}") for n in
                    ("squared", "rooted", "normed", "turned", "act_out", "dve_out"))
                dst = x if keep else xn
                with nc.Block() as block:
                    @block.scalar
                    def _(act):
                        for t in range(TILES):
                            done(act, nc.scalar.activation(junk[:, t, :], x[:, t, :], ACT.Square,
                                                           accum_out=rstat[:, t:t + 1]), squared)
                        for k in (0, 1, 4, 5):
                            act.wait_ge(turned.sem, k // 2 + 1)
                            src = ps[k // 2][:, (k % 2) * S:(k % 2 + 1) * S]
                            if scale is None:
                                ins = nc.scalar.activation(hT[:, k, :], src, ACT.Copy)
                            else:
                                ins = nc.scalar.activation(hT[:, k, :], src, ACT.Identity,
                                                           bias=bias[:, k:k + 1], scale=scale[:, k:k + 1])
                            signal(ins, act_out)

                    @block.gpsimd
                    def _(pool):
                        pool.wait_ge(squared.sem, 2)
                        rsqrt_on_pool(pool, rstat[:, 4:6], rstat[:, 0:2], 2, rooted, 1.0 / D, EPS)

                    @block.vector
                    def _(dve):
                        dve.wait_ge(rooted.sem, 2)
                        for t in range(TILES):
                            r = rstat[:, 4 + t:5 + t]
                            if row_gain is None:
                                ins = nc.vector.tensor_scalar(dst[:, t, :], x[:, t, :], r, None, ALU.mult)
                            else:
                                ins = nc.vector.scalar_tensor_tensor(dst[:, t, :], x[:, t, :], r, row_gain,
                                                                     ALU.mult, ALU.mult)
                            signal(ins, normed)
                        for k in (2, 3, 6, 7):
                            dve.wait_ge(turned.sem, k // 2 + 1)
                            src = ps[k // 2][:, (k % 2) * S:(k % 2 + 1) * S]
                            if scale is None:
                                ins = nc.vector.tensor_copy(hT[:, k, :], src)
                            else:
                                ins = nc.vector.tensor_scalar(hT[:, k, :], src, scale[:, k:k + 1],
                                                              bias[:, k:k + 1], ALU.mult, ALU.add)
                            signal(ins, dve_out)

                    @block.tensor
                    def _(pe):
                        transpose_pe(pe, dst, KD, (normed.sem, (1, 2)), turned)

        def products(ring, job, out):
            h = hP if job.lhs is None else job.lhs
            for c in range(job.k):
                for tp, wp in ((0, 0), (0, 1), (1, 0)):
                    tokens = h[:, tp, job.k0 + c, :]
                    weights = ring.view(job.unit, wp, job.k, job.unit_width, job.at)[:, c, :]
                    if job.kind == "tok":
                        lhs, rhs = tokens[:, job.idx * P:(job.idx + 1) * P], weights[:, job.col0:job.col0 + job.width]
                    else:
                        lhs, rhs = weights[:, job.idx * P:(job.idx + 1) * P], tokens
                    ins = nc.tensor.matmul(out, lhs, rhs, start=c == 0 and tp + wp == 0,
                                           stop=c == job.k - 1 and tp == 1)
            return ins

        def project(tag, ring, jobs, banks=8, extra=None, pace=4):
            extra = extra or {}
            summed, act_out, dve_out = (Count(nc, f"{tag}_{n}") for n in ("summed", "act_out", "dve_out"))
            n_summed, n_out = 0, {True: 0, False: 0}
            for g, job in enumerate(jobs):
                if job.last:
                    job.ready = (ring.used, job.unit + 1)
                else:
                    n_summed += 1
                    job.ready = (summed.sem, n_summed)
                n_out[job.act] += 1
                job.left = ((act_out if job.act else dve_out).sem, n_out[job.act])

            def shape(job, g):
                return ps[g % banks][:, 0:job.width if job.kind == "tok" else S]

            def drain(eng, act, s, between=None):
                for g, job in enumerate(jobs):
                    if g == 0 or jobs[g - 1].unit != job.unit:
                        (ring.hi if act else ring.lo)(eng, job.unit + 1)
                        for _ in range(pace if between is not None else 0):
                            next(between, None)
                    if job.act == act:
                        eng.wait_ge(*job.ready)
                        (signal if act else lambda ins, s: done(eng, ins, s))(job.out(shape(job, g)), s)
                for _ in between or ():
                    pass

            with nc.Block() as block:
                @block.sync
                def _(sp):
                    ring.feed(sp, jobs[-1].unit + 1)
                    if "sync" in extra:
                        extra["sync"](sp)

                @block.tensor
                def _(pe):
                    for g, job in enumerate(jobs):
                        if g == 0 or jobs[g - 1].unit != job.unit:
                            ring.arrived(pe, job.unit)
                        if g >= banks:
                            pe.wait_ge(*jobs[g - banks].left)
                        ins = products(ring, job, shape(job, g))
                        ins.then_inc(ring.used if job.last else summed.sem, 1)
                    if "tensor" in extra:
                        extra["tensor"](pe)

                @block.scalar
                def _(act):
                    drain(act, True, act_out)
                    if "scalar" in extra:
                        extra["scalar"](act)

                @block.vector
                def _(dve):
                    drain(dve, False, dve_out, extra["vector"](dve) if "vector" in extra else None)

                if "gpsimd" in extra:
                    @block.gpsimd
                    def _(pool):
                        extra["gpsimd"](pool)

        def copy_out(act, dst):
            return lambda src: nc.scalar.activation(dst, src, ACT.Copy) if act else nc.vector.tensor_copy(dst, src)

        def split_fm(tag, src, pair, chunks):
            hi_done = nc.alloc_semaphore(f"{tag}_hi")
            n = chunks // 4
            with nc.Block() as block:
                @block.scalar
                def _(act):
                    for b in range(4):
                        nc.scalar.activation(pair[:, 0, n * b:n * b + n, :], src[:, n * b:n * b + n, :],
                                             ACT.Copy).then_inc(hi_done, 1)

                @block.vector
                def _(dve):
                    for b in range(4):
                        dve.wait_ge(hi_done, b + 1)
                        nc.vector.tensor_tensor(pair[:, 1, n * b:n * b + n, :], src[:, n * b:n * b + n, :],
                                                pair[:, 0, n * b:n * b + n, :].bitcast(FP),
                                                ALU.subtract)

        def gated_hidden(tag, ring, first, blocks, gain):
            def gu(n, up):
                return first + (up if n == 0 else 3 * n - 1 + up)

            def dn(n):
                return first + (3 * n + 4 if n < blocks - 1 else 3 * n + 2)

            def flat(ap):
                return ap.rearrange("p a b -> p (a b)")

            with ExitStack() as st:
                sig = sb(f"{tag}_sig", [P, TILES, 256], st)
                a = sb(f"{tag}_a", [P, TILES, 256], st)
                aT = sb(f"{tag}_aT", [P, 2, 2, S], st, FR)
                gated, multiplied, acted, turned, hi_out, lo_out, chain = (Count(nc, f"{tag}_{n}") for n in
                    ("gated", "multiplied", "acted", "turned", "hi_out", "lo_out", "dve_step"))
                with nc.Block() as block:
                    @block.sync
                    def _(sp):
                        ring.feed(sp, len(ring.units))

                    @block.tensor
                    def _(pe):
                        def hidden(n, up):
                            ring.arrived(pe, gu(n, up))
                            if n >= 1:
                                pe.wait_ge(*((acted.sem, n) if up else (multiplied.sem, n)))
                            for t in range(TILES):
                                ins = products(ring, Job(gu(n, up), "tok", t, 256, True, None),
                                               ps[up][:, t * 256:(t + 1) * 256])
                            ins.then_inc(ring.used, 1)

                        def turn(n):
                            pe.wait_ge(acted.sem, n + 1)
                            if n >= 2:
                                pe.wait_ge(lo_out.sem, n - 1)
                            for t in range(TILES):
                                for c in range(2):
                                    ins = nc.tensor.transpose(ps[2 + n % 2][:, c * S + t * P:c * S + (t + 1) * P],
                                                              a[:, t, c * P:(c + 1) * P], ident)
                            ins.then_inc(turned.sem, 1)

                        def down(n):
                            pe.wait_ge(lo_out.sem, n + 1)
                            ring.arrived(pe, dn(n))
                            for t in range(TILES):
                                for nb in range(2):
                                    for c in range(2):
                                        for tp, wp in ((0, 0), (0, 1), (1, 0)):
                                            w = ring.view(dn(n), wp, 2, D)
                                            ins = nc.tensor.matmul(
                                                ps[4 + 2 * t + nb][:, :], aT[:, tp, c, t * P:(t + 1) * P],
                                                w[:, c, nb * 512:(nb + 1) * 512],
                                                start=n == 0 and c + tp + wp == 0,
                                                stop=n == blocks - 1 and c == 1 and tp == 1)
                            ins.then_inc(ring.used, 1)

                        for n in range(blocks):
                            hidden(n, 0)
                            hidden(n, 1)
                            if n >= 1:
                                down(n - 1)
                            turn(n)
                        down(blocks - 1)

                    @block.scalar
                    def _(act):
                        for n in range(blocks):
                            ring.hi(act, dn(n - 1) if n else gu(0, 1))
                            act.wait_ge(ring.used, gu(n, 0) + 1)
                            if n >= 1:
                                act.wait_ge(acted.sem, n)
                            nc.scalar.activation(flat(sig[:, :, :]), ps[0][:, :], ACT.Sigmoid).then_inc(gated.sem, 1)
                            if n + 1 < blocks:
                                ring.hi(act, gu(n + 1, 1))
                            else:
                                ring.hi(act, dn(n))
                            act.wait_ge(turned.sem, n + 1)
                            if n >= 1:
                                act.wait_ge(ring.used, dn(n - 1) + 1)
                            nc.scalar.activation(flat(aT[:, 0, :, :]), ps[2 + n % 2][:, :],
                                                 ACT.Copy).then_inc(hi_out.sem, 1)

                    @block.vector
                    def _(dve):
                        for n in range(blocks):
                            ring.lo(dve, dn(n - 1) if n else gu(0, 1))
                            dve.wait_ge(gated.sem, n + 1)
                            g = sig[:, :, :]
                            nc.vector.tensor_tensor(flat(g), ps[0][:, :], flat(g), ALU.mult).then_inc(multiplied.sem, 1)
                            dve.wait_ge(multiplied.sem, n + 1)
                            dve.wait_ge(ring.used, gu(n, 1) + 1)
                            if n >= 1:
                                dve.wait_ge(turned.sem, n)
                            up = ps[1][:, :].rearrange("p (t s) -> p t s", t=TILES)
                            if gain(n, 0) is None:
                                nc.vector.tensor_tensor(a[:, :, :], up, g, ALU.mult).then_inc(acted.sem, 1)
                            else:
                                for t in range(TILES):
                                    ins = nc.vector.scalar_tensor_tensor(a[:, t, :], up[:, t, :], gain(n, t), g[:, t, :],
                                                                         ALU.mult, ALU.mult)
                                    if t == 0:
                                        done(dve, ins, chain)
                                ins.then_inc(acted.sem, 1)
                            if n + 1 < blocks:
                                ring.lo(dve, gu(n + 1, 1))
                            else:
                                ring.lo(dve, dn(n))
                            dve.wait_ge(hi_out.sem, n + 1)
                            nc.vector.tensor_tensor(flat(aT[:, 1, :, :]), ps[2 + n % 2][:, :],
                                                    flat(aT[:, 0, :, :]).bitcast(FP), ALU.subtract).then_inc(lo_out.sem, 1)

        def hidden_units(blocks, gate, up, down):
            units = []
            for n in range(blocks):
                units += [[(0, 8, 256, 0, 256, gate(n))], [(0, 8, 256, 0, 256, up(n))]]
                if n:
                    units.append([(0, 2, D, 0, D, down(n - 1))])
            units.append([(0, 2, D, 0, D, down(blocks - 1))])
            return units

        def add_gated(tag, gain):
            with ExitStack() as st:
                tmp = sb(f"{tag}_tmp", [P, 4, 512], st)
                chain = Count(nc, f"{tag}_step")
                with nc.Block() as block:
                    @block.vector
                    def _(dve):
                        for q in range(4):
                            t, cut = q // 2, slice((q % 2) * 512, (q % 2) * 512 + 512)
                            done(dve, nc.vector.tensor_tensor(tmp[:, q, :], ps[4 + q][:, :], gain[:, cut], ALU.mult), chain)
                            done(dve, nc.vector.tensor_tensor(x[:, t, cut], x[:, t, cut], tmp[:, q, :], ALU.add), chain)

        def attend(tag, heads, oT, ring, ada_first, ada_lhs, ada_out, after):
            with ExitStack() as st:
                prob = sb(f"{tag}_prob", [P, 2, TILES, S], st)
                score = sb(f"{tag}_score", [P, 2, TILES, S], st)
                probT = sb(f"{tag}_probT", [P, 2, TILES, S], st)
                stat = sb(f"{tag}_stat", [P, 2, 4, TILES], st)
                scored, maxed, expd, normed, turned, copied, mixed, stored_o, chain, mod_out = (
                    Count(nc, f"{tag}_{n}") for n in ("scored", "maxed", "expd", "normed", "turned", "copied",
                                                      "mixed", "out", "step", "mod_out"))
                N = len(heads)
                with nc.Block() as block:
                    @block.sync
                    def _(sp):
                        ring.feed(sp, ada_first + N)

                    @block.tensor
                    def _(pe):
                        for i in range(N + 2):
                            if i < N:
                                qT, kT, v, scale, bias = heads[i]
                                if i >= 2:
                                    pe.wait_ge(expd.sem, 2 * (i - 1))
                                    pe.wait_ge(maxed.sem, i - 1)
                                for t in range(TILES):
                                    ins = nc.tensor.matmul(ps[i % 2][:, t * S:(t + 1) * S], qT[:, t * P:(t + 1) * P],
                                                           kT, start=True, stop=True)
                                ins.then_inc(scored.sem, 1)
                                if i >= 2:
                                    pe.wait_ge(mod_out.sem, i - 1)
                                modulation(pe, ring, ada_first + i, ps[6 + i % 2][:, 0:UNIT_W], ada_lhs)
                            if 1 <= i <= N:
                                n = i - 1
                                pe.wait_ge(normed.sem, n + 1)
                                if n >= 2:
                                    pe.wait_ge(copied.sem, n - 1)
                                for t in range(TILES):
                                    for kt in range(TILES):
                                        ins = nc.tensor.transpose(ps[2 + n % 2][:, kt * S + t * P:kt * S + (t + 1) * P],
                                                                  prob[:, n % 2, t, kt * P:(kt + 1) * P], ident)
                                ins.then_inc(turned.sem, 1)
                            if i >= 2:
                                n = i - 2
                                v = heads[n][2]
                                pe.wait_ge(copied.sem, n + 1)
                                if n >= 2:
                                    pe.wait_ge(stored_o.sem, n - 1)
                                base = 64 * (n % 2)
                                for kt in range(TILES):
                                    ins = nc.tensor.matmul(ps[4 + n % 2][base:base + 64, 0:S], v(kt),
                                                           probT[:, n % 2, kt, :], start=kt == 0, stop=kt == 1)
                                ins.then_inc(mixed.sem, 1)

                    @block.vector
                    def _(dve):
                        for i in range(N + 2):
                            if i < N:
                                scale, bias = heads[i][3:5]
                                dve.wait_ge(scored.sem, i + 1)
                                if i >= 2:
                                    dve.wait_ge(normed.sem, i - 1)
                                src = ps[i % 2][:, :].rearrange("p (t s) -> p t s", t=TILES)
                                if bias is not None:
                                    dst = score[:, i % 2, :, :]
                                    if i >= 2:
                                        dve.wait_ge(expd.sem, 2 * (i - 1))
                                    done(dve, nc.vector.scalar_tensor_tensor(dst, src, scale, bias, ALU.mult, ALU.add), chain)
                                    src = dst
                                done(dve, nc.vector.tensor_reduce(stat[:, i % 2, 1, :], src, AX, ALU.max), chain)
                                nc.vector.tensor_scalar(stat[:, i % 2, 0, :], stat[:, i % 2, 1, :],
                                                        -1.0 if bias is not None else -scale, None,
                                                        ALU.mult).then_inc(maxed.sem, 1)
                            if 1 <= i <= N:
                                n = i - 1
                                dve.wait_ge(expd.sem, 2 * n + 2)
                                done(dve, nc.vector.reciprocal(stat[:, n % 2, 3, :], stat[:, n % 2, 2, :]), chain)
                                nc.vector.tensor_tensor(
                                    prob[:, n % 2, :, :], prob[:, n % 2, :, :],
                                    stat[:, n % 2, 3, :].unsqueeze(2).broadcast_to([P, TILES, S]),
                                    ALU.mult).then_inc(normed.sem, 1)
                            if i >= 2:
                                n = i - 2
                                base = 64 * (n % 2)
                                dve.wait_ge(mixed.sem, n + 1)
                                nc.vector.tensor_copy(oT[base:base + 64, n // 2, :],
                                                      ps[4 + n % 2][base:base + 64, 0:S]).then_inc(stored_o.sem, 1)
                            if i < N:
                                ring.lo(dve, ada_first + i + 1)
                            if 1 <= i <= N:
                                n = i - 1
                                dve.wait_ge(ring.used, ada_first + n + 1)
                                done(dve, ada_out(dve, n, ps[6 + n % 2][:, 0:UNIT_W]), mod_out)
                        after(dve)

                    @block.scalar
                    def _(act):
                        for i in range(N + 1):
                            if i < N:
                                scale, bias = heads[i][3:5]
                                act.wait_ge(maxed.sem, i + 1)
                                if i >= 2:
                                    act.wait_ge(turned.sem, i - 1)
                                for t in range(TILES):
                                    src = ps[i % 2][:, t * S:(t + 1) * S] if bias is None else score[:, i % 2, t, :]
                                    nc.scalar.activation(prob[:, i % 2, t, :], src, ACT.Exp,
                                                         bias=stat[:, i % 2, 0, t:t + 1],
                                                         scale=scale if bias is None else 1.0,
                                                         accum_out=stat[:, i % 2, 2, t:t + 1]).then_inc(expd.sem, 1)
                            if i >= 1:
                                n = i - 1
                                act.wait_ge(turned.sem, n + 1)
                                if n >= 2:
                                    act.wait_ge(mixed.sem, n - 1)
                                nc.scalar.activation(probT[:, n % 2, :, :].rearrange("p k s -> p (k s)"),
                                                     ps[2 + n % 2][:, :], ACT.Copy).then_inc(copied.sem, 1)
                            if i < N:
                                ring.hi(act, ada_first + i + 1)

        def modulation(pe, ring, unit, out, lhs):
            ring.arrived(pe, unit)
            for c in range(KD):
                for tp, wp in ((0, 0), (0, 1), (1, 0)):
                    ins = nc.tensor.matmul(out, lhs[:, tp, c, :], ring.view(unit, wp, KD, UNIT_W)[:, c, :],
                                           start=c + tp + wp == 0, stop=c == KD - 1 and tp == 1)
            ins.then_inc(ring.used, 1)

        def to_columns(dve, dst, src, junk, s):
            j = junk.rearrange("p (b n) -> p b n", b=2)
            done(dve, nc.vector.tensor_tensor(j, src.rearrange("p (b n) -> p b n", b=2),
                                              ident.unsqueeze(1).broadcast_to([P, 2, P]), ALU.mult), s)
            return nc.vector.tensor_reduce(dst, j, AX, ALU.add)

        def rotate(dve, s, out, src, cos, sin, tmp, heads, parts):
            w = parts * 32
            bc = [P, TILES, heads, w]

            def table(c):
                return c.rearrange("p (t w) -> p t w", t=TILES).unsqueeze(2).broadcast_to(bc)

            for t in range(TILES):
                for half in range(2):
                    pick = "p h (a f w) -> p h a f w"
                    got = src[:, t, :, :].rearrange(pick, a=parts, f=2)[:, :, :, 1 - half, :]
                    put = tmp[:, t, :, :].rearrange(pick, a=parts, f=2)[:, :, :, half, :]
                    by = sin[:, t * w:(t + 1) * w].unsqueeze(1).broadcast_to([P, heads, w]) \
                        .rearrange(pick, a=parts, f=2)[:, :, :, half, :]
                    signal(nc.vector.tensor_tensor(put, got, by, ALU.mult), s)
            dve.wait_ge(s.sem, s.n)
            done(dve, nc.vector.tensor_tensor(out, src, table(cos), ALU.mult), s)
            done(dve, nc.vector.tensor_tensor(out, out, tmp, ALU.add), s)

        def layer(l):
            def cols(name, c0, c1):
                return A[name][bass.ds(l, 1), :, c0:c1].rearrange("o (k p) n -> p (o k) n", p=P)

            def rows(name, r0, r1):
                return A[name][bass.ds(l, 1), r0:r1, :].rearrange("o (k p) n -> p (o k) n", p=P)

            def ada(u):
                return [(0, 8, 256, 0, 256, cols("ada_w", 256 * u, 256 * u + 256))]

            units = [ada(u) for u in range(8)]
            PROJ = len(units)
            for c0 in range(0, 1952, 256):
                units.append([(0, 8, 256, 0, min(256, 1952 - c0), cols("w_in", c0, min(c0 + 256, 1952)))])
            GATES = len(units)
            for b in range(12):
                units.append([(0, 8, 256, 0, 256, cols("w_in", 1952 + 256 * b, 2208 + 256 * b))])
            ADA2 = len(units)
            units += [ada(u) for u in range(8, 24)]
            BRANCH = len(units)
            for nb in range(4):
                n0, n1 = 256 * nb, 256 * nb + 256
                units.append([(0, 2, 256, 0, 256, cols("w_br_na", n0, n1)),
                              (512, 2, 256, 0, 256, cols("w_br_mla", n0, n1)),
                              (1024, 4, 256, 0, 256, cols("w_br_gqa", n0, n1))])
            MERGED = len(units)
            for nb in range(4):
                units.append([(0, 8, 256, 0, 256, cols("w_out", 256 * nb, 256 * nb + 256))])
            HIDDEN = len(units)
            n_hidden = FFN // 256
            units += hidden_units(n_hidden, lambda n: cols("ffn_w_gate_up", 256 * n, 256 * n + 256),
                                  lambda n: cols("ffn_w_gate_up", FFN + 256 * n, FFN + 256 * n + 256),
                                  lambda n: rows("ffn_w_down", 256 * n, 256 * n + 256))
            with ExitStack() as st:
                ring = Ring(nc, "layer", sb("layer_raw", [P, 3, UNIT], st), sb("layer_split", [P, 2, 2, UNIT], st, FR), units)
                col = sb("columns", [P, 75], st)
                mod = sb("mod", [P, 48], st)
                Gm = sb("gain_mix", [P, 8], st)
                Gf = sb("gain_ffn", [P, 8], st)
                gate_rows = sb("gate_rows", [P, 2, D], st)
                small = nc.alloc_semaphore("small_loaded")
                rows_loaded = nc.alloc_semaphore("gate_rows_loaded")
                turned, copied, silud, modded, mod_out = (Count(nc, f"mod_{n}") for n in
                    ("turned", "copied", "silud", "modded", "out"))
                scP = sb("silu_c_pair", [P, 2, KD, P], st, FR)
                diag = sb("diag", [P, UNIT_W], st)

                with ExitStack() as s1:
                    raw = sb("raw_rows", [P, P], s1)
                    sg = sb("sigmoid_c", [P, 8], s1)
                    sc = sb("silu_c", [P, KD, P], s1)
                    with nc.Block() as block:
                        @block.sync
                        def _(sp):
                            def row_block(name, r, n):
                                src = A[name] if name == "c" else A[name][bass.ds(l, 1), :]
                                sp.dma_start(raw[r:r + n, :], src.rearrange("o (r p) -> (o r) p", p=P)).then_inc(small, 16)

                            row_block("ada_b", 0, 48)
                            row_block("norm_mix_g", 48, 8)
                            row_block("norm_ffn_g", 56, 8)
                            row_block("mla_q_norm_g", 64, 2)
                            row_block("mla_kv_norm_g", 66, 1)
                            row_block("c", 67, 8)
                            for i, at in enumerate((2 * D, 5 * D)):
                                sp.dma_start(gate_rows[:, i, :], A["ada_b"][bass.ds(l, 1), at:at + D].broadcast_to([P, D])) \
                                    .then_inc(rows_loaded, 16)
                            ring.feed(sp, PROJ)

                        @block.tensor
                        def _(pe):
                            pe.wait_ge(small, 16 * 6)
                            nc.tensor.transpose(ps[0][:, 0:75], raw[0:75, :], ident[0:75, 0:75]).then_inc(turned.sem, 1)
                            pe.wait_ge(silud.sem, 4)
                            for u in range(8):
                                if u >= 2:
                                    pe.wait_ge(mod_out.sem, u - 1)
                                modulation(pe, ring, u, ps[1 + u % 2][:, 0:UNIT_W], scP)

                        @block.scalar
                        def _(act):
                            act.wait_ge(turned.sem, 1)
                            done(act, nc.scalar.activation(col[:, :], ps[0][:, 0:75], ACT.Copy), copied)
                            done(act, nc.scalar.activation(sg[:, :], col[:, 67:75], ACT.Sigmoid), silud)
                            act.wait_ge(silud.sem, 2)
                            done(act, nc.scalar.activation(scP[:, 0, :, :], sc[:, :, :], ACT.Copy), copied)
                            for u in range(8):
                                ring.hi(act, u + 1)

                        @block.vector
                        def _(dve):
                            silud.n = 1
                            dve.wait_ge(silud.sem, 1)
                            bc = [P, KD, P]
                            done(dve, nc.vector.tensor_tensor(sc[:, :, :], sg[:, :].unsqueeze(2).broadcast_to(bc),
                                                              col[:, 67:75].unsqueeze(2).broadcast_to(bc), ALU.mult), silud)
                            dve.wait_ge(copied.sem, 2)
                            done(dve, nc.vector.tensor_tensor(scP[:, 1, :, :], sc[:, :, :], scP[:, 0, :, :].bitcast(FP),
                                                              ALU.subtract), silud)
                            done(dve, nc.vector.memset(mod[:, :], 0.0), silud)
                            for u in range(8):
                                ring.lo(dve, u + 1)
                                dve.wait_ge(ring.used, u + 1)
                                done(dve, to_columns(dve, mod[:, 2 * u:2 * u + 2], ps[1 + u % 2][:, 0:UNIT_W], diag[:, :],
                                                     modded), mod_out)
                            done(dve, nc.vector.tensor_tensor(mod[:, 0:16], mod[:, 0:16], col[:, 0:16], ALU.add), modded)
                            done(dve, nc.vector.scalar_tensor_tensor(Gm[:, :], mod[:, 8:16], 1.0, col[:, 48:56],
                                                                     ALU.add, ALU.mult), modded)
                dump("mod", mod[:, :])

                def ada_out(dve, n, src):
                    if n // 4 in (0, 3):
                        if n == 0:
                            dve.wait_ge(rows_loaded, 32)
                        dst = gate_rows[:, n // 12, 256 * (n % 4):256 * (n % 4) + 256]
                        return nc.vector.tensor_tensor(dst, src, dst, ALU.add)
                    return to_columns(dve, mod[:, 16 + 2 * n:18 + 2 * n], src, diag[:, :], modded)

                def ada_rest(dve):
                    done(dve, nc.vector.tensor_tensor(mod[:, 24:40], mod[:, 24:40], col[:, 24:40], ALU.add), modded)
                    done(dve, nc.vector.scalar_tensor_tensor(Gf[:, :], mod[:, 32:40], 1.0, col[:, 56:64],
                                                             ALU.add, ALU.mult), modded)

                rms_norm_to_fm("mix", Gm, mod[:, 0:8])
                split_fm("mix_split", hT, hP, KD)
                with ExitStack() as s2:
                    oT = sb("oT", [P, 8, S], s2)
                    sg3 = sb("branch_gates", [P, TILES, 3 * D], s2)
                    attention(l, ring, PROJ, GATES, ADA2, col, oT, sg3, scP, ada_out, ada_rest)
                    dump("oT", oT[:, :, :])
                    dump("gate_rows", gate_rows[:, :, :])
                    merge(ring, "merge", BRANCH, MERGED, ((0, 2), (2, 2), (4, 4)), oT, sg3, gate_rows[:, 0, :])
                dump("xmid", x[:, :, :])
                rms_norm_to_fm("ffn", Gf, mod[:, 24:32])
                split_fm("ffn_split", hT, hP, KD)
                gated_hidden("ffnh", ring, HIDDEN, n_hidden, lambda n, t: None)
                add_gated("ffn_add", gate_rows[:, 1, :])

        def attention(l, ring, PROJ, GATES, ADA2, col, oT, sg3, scP, ada_out, ada_rest):
            with ExitStack() as s3:
                VA, CQ, CKV, KR, QC, KC, VC = 0, 256, 512, 640, 672, 1184, 1312
                p1 = sb("proj_tok", [P, TILES, 1440], s3)
                na_qk = sb("na_qkT", [P, 4, S], s3)
                na_bias = sb("na_bias", [P, TILES, 4, 4, GRID_W], s3)
                gqa_g = sb("gqa_g", [P, 2, 64], s3)
                bias_loaded = nc.alloc_semaphore("na_bias_loaded")
                gains_loaded = nc.alloc_semaphore("gqa_gains_loaded")

                lora_w = sb("lora_w", [P, 1280], s3)
                lora_loaded = nc.alloc_semaphore("lora_w_loaded")
                jobs = []
                for b in range(4):
                    act = b % 2 == 0
                    jobs.append(Job(PROJ + b // 2, "fm", b % 2, S, act, copy_out(act, na_qk[:, b, :])))
                for u in range(6):
                    w = 160 if u == 5 else 256
                    for t in range(TILES):
                        act = t == 0
                        jobs.append(Job(PROJ + 2 + u, "tok", t, w, act,
                                        copy_out(act, p1[:, t, 256 * u:256 * u + w])))

                def load_small(sp):
                    for i, name in enumerate(("gqa_q_norm_g", "gqa_k_norm_g")):
                        src = A[name][bass.ds(l, 1), :].broadcast_to([P, 64])
                        sp.dma_start(gqa_g[:, i, :], src).then_inc(gains_loaded, 16)
                    sp.dma_start(na_bias[:, :, :, :, :].rearrange("p t h r c -> p (t h r c)"),
                                 strips[bass.ds(l, 1), :, :].rearrange("o p n -> (o p) n")).then_inc(bias_loaded, 16)

                    sp.dma_start(lora_w[:, 0:768].rearrange("p (k n) -> p k n", k=2),
                                 A["mla_w_uq"][bass.ds(l, 1), :, :].rearrange("o (k p) n -> p (o k) n", p=P)) \
                        .then_inc(lora_loaded, 16)
                    sp.dma_start(lora_w[:, 768:1280], A["mla_w_ukv"][bass.ds(l, 1), :, :]
                                 .rearrange("o p n -> p (o n)")).then_inc(lora_loaded, 16)

                project("proj", ring, jobs, extra={"sync": load_small})
                dump("p1", p1[:, :, :])
                dump("na_qk", na_qk[:, :, :])

                ms = sb("mean_squares", [P, TILES, 12], s3)
                rs = sb("inv_rms", [P, TILES, 12], s3)
                kpe = sb("mla_k_pe", [P, TILES, 1, 32], s3)
                gqaT = sb("gqa_T", [P, 6, S], s3)
                kvb = sb("mla_kv", [P, TILES, 4, P], s3)
                heads_scope = ExitStack()
                roped = sb("gqa_roped", [P, TILES, 12, 64], heads_scope)
                scratch = ExitStack()
                sq = sb("squares", [P, TILES, 1056], scratch)
                prep = Count(nc, "prep_step")
                rooted = Count(nc, "prep_rooted")
                summed_sq = nc.alloc_semaphore("prep_sums")

                jobs = [Job(GATES + b, "tok", t, 256, True,
                            (lambda dst: lambda src: nc.scalar.activation(dst, src, ACT.Sigmoid))(
                                sg3[:, t, 256 * b:256 * b + 256])) for b in range(12) for t in range(TILES)]

                def prepare(dve):
                    v = nc.vector
                    dve.wait_ge(bias_loaded, 16)
                    bias4 = na_bias[:, :, :, :, :].rearrange("p t h r c -> p (t h r) c")
                    for name, op in (("na_seen", ALU.mult), ("na_neg", ALU.add)):
                        done(dve, v.tensor_tensor(bias4, bias4, const(name).unsqueeze(1).broadcast_to([P, 32, 64]), op), prep)
                        yield
                    done(dve, v.tensor_tensor(sq[:, :, :], p1[:, :, CQ:VC], p1[:, :, CQ:VC], ALU.mult), prep)
                    yield
                    done(dve, v.tensor_reduce(ms[:, :, 0:1], sq[:, :, 0:256], AX, ALU.add), prep)
                    yield
                    done(dve, v.tensor_reduce(ms[:, :, 1:2], sq[:, :, 256:384], AX, ALU.add), prep)
                    yield
                    done(dve, v.tensor_reduce(ms[:, :, 2:12], sq[:, :, 416:1056].rearrange("p t (h d) -> p t h d", h=10),
                                              AX, ALU.add), prep)
                    yield
                    for c0, c1, n in ((0, 1, 256), (1, 2, 128), (2, 12, 64)):
                        ins = v.tensor_scalar(ms[:, :, c0:c1], ms[:, :, c0:c1], 1.0 / n, EPS, ALU.mult, ALU.add)
                        if c0 < 2:
                            done(dve, ins, prep)
                    ins.then_inc(summed_sq, 1)
                    rotate(dve, prep, kpe[:, :, :, :], p1[:, :, KR:KR + 32].unsqueeze(2), const("mla_cos"),
                           const("mla_sin"), sq[:, :, 0:32].unsqueeze(2), 1, 1)
                    yield
                    dve.wait_ge(rooted.sem, 1)
                    dve.wait_ge(gains_loaded, 32)
                    for at, n, j in ((CQ, 256, 0), (CKV, 128, 1)):
                        done(dve, v.tensor_tensor(p1[:, :, at:at + n], p1[:, :, at:at + n],
                                                  rs[:, :, j:j + 1].broadcast_to([P, TILES, n]), ALU.mult), prep)
                        yield
                    qk = p1[:, :, QC:VC].rearrange("p t (h d) -> p t h d", h=10)
                    done(dve, v.tensor_tensor(qk, qk, rs[:, :, 2:12].unsqueeze(3).broadcast_to([P, TILES, 10, 64]),
                                              ALU.mult), prep)
                    yield
                    for h0, h1, g in ((0, 8, 0), (8, 10, 1)):
                        by = gqa_g[:, g, :].unsqueeze(1).unsqueeze(1).broadcast_to([P, TILES, h1 - h0, 64])
                        done(dve, v.tensor_tensor(qk[:, :, h0:h1, :], qk[:, :, h0:h1, :], by, ALU.mult), prep)
                        yield
                    rotate(dve, prep, roped[:, :, 0:10, :], qk, const("ax_cos"), const("ax_sin"),
                           sq[:, :, 0:640].rearrange("p t (h d) -> p t h d", h=10), 10, 2)
                    yield
                    done(dve, v.tensor_copy(roped[:, :, 10, :], roped[:, :, 9, :]), prep)
                    yield
                    done(dve, v.tensor_copy(roped[:, :, 11, :], roped[:, :, 8, :]), prep)
                    yield

                def roots(pool):
                    pool.wait_ge(summed_sq, 1)
                    pool.tensor_tensor(rs[:, :, :].rearrange("p t c -> p (t c)"),
                                       ms[:, :, :].rearrange("p t c -> p (t c)"),
                                       half_neg[:, 0:24], ALU.pow).then_inc(rooted.sem, 1)

                project("gates", ring, jobs, extra={"vector": prepare, "gpsimd": roots}, pace=2)
                scratch.close()
                dump("roped", roped[:, :, :, :])

                lora = ExitStack()
                cT = sb("mla_cT", [P, 3, S], lora)
                qfull = sb("mla_q", [P, TILES, 4, 96], lora)
                kfull = sb("mla_k", [P, TILES, 4, 96], lora)
                rot, tmp = (hT[:, i, :].rearrange("p (t h d) -> p t h d", t=TILES, h=4) for i in (6, 7))
                turned, scaled, lifted, act_copied, gqa_turned, step = (Count(nc, f"mla_{n}") for n in
                    ("turned", "scaled", "lifted", "copied", "gqa_turned", "step"))
                with nc.Block() as block:
                    @block.tensor
                    def _(pe):
                        for c in range(3):
                            for t in range(TILES):
                                at = CQ + c * P
                                ins = nc.tensor.transpose(ps[c // 2][:, (c % 2) * S + t * P:(c % 2) * S + (t + 1) * P],
                                                          p1[:, t, at:at + P], ident)
                            ins.then_inc(turned.sem, 1)
                        for b in range(6):
                            for t in range(TILES):
                                ins = nc.tensor.transpose(ps[2 + b // 2][:, (b % 2) * S + t * P:(b % 2) * S + (t + 1) * P],
                                                          roped[:, t, 2 * b:2 * b + 2, :].rearrange("p h d -> p (h d)"), ident)
                            if b % 2:
                                ins.then_inc(gqa_turned.sem, 1)
                        pe.wait_ge(lora_loaded, 32)
                        pe.wait_ge(scaled.sem, 3)
                        pe.wait_ge(act_copied.sem, 1)
                        wq = lora_w[:, 0:768].rearrange("p (k n) -> p k n", k=2)
                        wkv = lora_w[:, 768:1280].unsqueeze(1)
                        bank = (6, 7, 0, 2)
                        for t in range(TILES):
                            for c in range(2):
                                ins = nc.tensor.matmul(ps[bank[t]][:, 0:384], cT[:, c, t * P:(t + 1) * P], wq[:, c, :],
                                                       start=c == 0, stop=c == 1)
                            ins.then_inc(lifted.sem, 1)
                        for t in range(TILES):
                            ins = nc.tensor.matmul(ps[bank[2 + t]][:, :], cT[:, 2, t * P:(t + 1) * P], wkv[:, 0, :],
                                                   start=True, stop=True)
                            ins.then_inc(lifted.sem, 1)

                    @block.scalar
                    def _(act):
                        for c in range(3):
                            act.wait_ge(turned.sem, max(c + 1, 2))
                            nc.scalar.activation(cT[:, c, :], ps[c // 2][:, (c % 2) * S:(c % 2 + 1) * S], ACT.Copy,
                                                 scale=col[:, 64 + c:65 + c]).then_inc(scaled.sem, 1)
                        for b in range(3):
                            act.wait_ge(gqa_turned.sem, b + 1)
                            nc.scalar.activation(gqaT[:, 2 * b:2 * b + 2, :].rearrange("p b s -> p (b s)"),
                                                 ps[2 + b][:, :], ACT.Copy).then_inc(act_copied.sem, 1)

                    @block.vector
                    def _(dve):
                        v = nc.vector
                        for t in range(TILES):
                            dve.wait_ge(lifted.sem, t + 1)
                            done(dve, v.tensor_copy(qfull[:, t, :, :].rearrange("p h d -> p (h d)"),
                                                    ps[6 + t][:, 0:384]), step)
                        for t in range(TILES):
                            dve.wait_ge(lifted.sem, 3 + t)
                            done(dve, v.tensor_copy(kvb[:, t, :, :].rearrange("p h d -> p (h d)"),
                                                    ps[(0, 2)[t]][:, :]), step)
                        rotate(dve, step, rot[:, :, :, :], qfull[:, :, :, 64:96], const("mla_cos"), const("mla_sin"),
                               tmp[:, :, :, :], 4, 1)
                        done(dve, v.tensor_copy(qfull[:, :, :, 64:96], rot[:, :, :, :]), step)
                        done(dve, v.tensor_copy(kfull[:, :, :, 0:64], kvb[:, :, :, 0:64]), step)
                        done(dve, v.tensor_copy(kfull[:, :, :, 64:96], kpe[:, :, :, :].broadcast_to([P, TILES, 4, 32])), step)
                dump("qfull", qfull[:, :, :, :])

                mT = hT[0:96, :, :].rearrange("p (i h) s -> p i h s", i=2)
                m_turned, m_out = nc.alloc_semaphore("mla_heads_turned"), nc.alloc_semaphore("mla_heads_out")
                with nc.Block() as block:
                    @block.tensor
                    def _(pe):
                        for i, src in enumerate((qfull, kfull)):
                            for h in range(4):
                                for t in range(TILES):
                                    ins = nc.tensor.transpose(
                                        ps[2 * i + h // 2][0:96, (h % 2) * S + t * P:(h % 2) * S + (t + 1) * P],
                                        src[:, t, h, :], ident)
                                if h % 2:
                                    ins.then_inc(m_turned, 1)

                    @block.scalar
                    def _(act):
                        for b in range(4):
                            act.wait_ge(m_turned, b + 1)
                            nc.scalar.activation(mT[:, b // 2, 2 * (b % 2):2 * (b % 2) + 2, :].rearrange("p b s -> p (b s)"),
                                                 ps[b][0:96, :], ACT.Copy).then_inc(m_out, 1)

                lora.close()
                heads_scope.close()
                heads = []
                for h in range(4):
                    base = 64 * (h % 2)
                    heads.append((na_qk[base:base + 64, h // 2, :], na_qk[base:base + 64, 2 + h // 2, :],
                                  (lambda h: lambda kt: p1[:, kt, VA + 64 * h:VA + 64 * h + 64])(h), 64 ** -0.5,
                                  na_bias[:, :, h, :, :].rearrange("p t r c -> p t (r c)")))
                for h in range(4):
                    heads.append((mT[:, 0, h, :], mT[:, 1, h, :],
                                  (lambda h: lambda kt: kvb[:, kt, h, 64:128])(h), 96 ** -0.5, None))
                for h in range(8):
                    base, kv = 64 * (h % 2), h // 4
                    block_k = 4 if kv == h % 2 else 5
                    heads.append((gqaT[base:base + 64, h // 2, :], gqaT[base:base + 64, block_k, :],
                                  (lambda kv: lambda kt: p1[:, kt, VC + 64 * kv:VC + 64 * kv + 64])(kv), 64 ** -0.5, None))
                attend("att", heads, oT, ring, ADA2, scP, ada_out, ada_rest)

        def merge(ring, tag, first, second, chunks, yT, gates, gain):
            n_br = len(chunks)
            with ExitStack() as st:
                m = sb(f"{tag}_sum", [P, TILES, D], st)
                part = sb(f"{tag}_part", [P, 2, 256], st)
                yP = sb(f"{tag}_pair", [P, 2, 8, S], st, FR)
                step = Count(nc, f"{tag}_step")
                split_fm(f"{tag}_split", yT, yP, 8)
                jobs = []
                for nb in range(4):
                    cut = slice(nb * 256, nb * 256 + 256)
                    for t in range(TILES):
                        for b, (c0, k) in enumerate(chunks):
                            def out(src, t=t, b=b, cut=cut):
                                gate = gates[:, t, b * D + cut.start:b * D + cut.stop]
                                dst = m[:, t, cut]
                                if b == 0:
                                    return nc.vector.tensor_tensor(dst, src, gate, ALU.mult)
                                done(nc.vector, nc.vector.tensor_tensor(part[:, b % 2, :], src, gate, ALU.mult), step)
                                return nc.vector.tensor_tensor(dst, dst, part[:, b % 2, :], ALU.add)

                            jobs.append(Job(first + nb, "tok", t, 256, False, out, last=t == 1 and b == n_br - 1,
                                            k=k, lhs=yP, at=256 * c0, k0=c0))
                project(tag, ring, jobs)
                transpose_block(f"{tag}_T", m, hT)
                split_fm(f"{tag}_split2", hT, hP, KD)
                jobs = []
                for nb in range(4):
                    for t in range(TILES):
                        cut = slice(nb * 256, nb * 256 + 256)

                        def out(src, t=t, cut=cut):
                            done(nc.vector, nc.vector.tensor_tensor(part[:, t, :], src, gain[:, cut], ALU.mult), step)
                            return nc.vector.tensor_tensor(x[:, t, cut], x[:, t, cut], part[:, t, :], ALU.add)

                        jobs.append(Job(second + nb, "tok", t, 256, False, out))
                project(f"{tag}_out", ring, jobs)

        def transpose_block(tag, src, dst):
            turned, out = Count(nc, f"{tag}_turned"), nc.alloc_semaphore(f"{tag}_out")
            with nc.Block() as block:
                @block.tensor
                def _(pe):
                    for b in range(4):
                        for k in (2 * b, 2 * b + 1):
                            for t in range(TILES):
                                ins = nc.tensor.transpose(ps[b][:, (k % 2) * S + t * P:(k % 2) * S + (t + 1) * P],
                                                          src[:, t, k * P:(k + 1) * P], ident)
                        ins.then_inc(turned.sem, 1)

                @block.scalar
                def _(act):
                    for b in (0, 2):
                        act.wait_ge(turned.sem, b + 1)
                        nc.scalar.activation(dst[:, 2 * b:2 * b + 2, :].rearrange("p b s -> p (b s)"), ps[b][:, :],
                                             ACT.Copy).then_inc(out, 1)

                @block.vector
                def _(dve):
                    for b in (1, 3):
                        dve.wait_ge(turned.sem, b + 1)
                        nc.vector.tensor_copy(dst[:, 2 * b:2 * b + 2, :].rearrange("p b s -> p (b s)"),
                                              ps[b][:, :]).then_inc(out, 1)

        def second_part():
            def cols(name, c0, c1):
                return A[name][0, :, c0:c1].rearrange("(k p) n -> p k n", p=P)

            units = []

            def unit(name, c0, c1, k=KD):
                units.append([(0, k, c1 - c0, 0, c1 - c0, cols(name, c0, c1))])
                return len(units) - 1

            def unit_pair(name, c0):
                return [unit(name, c0, c0 + 256), unit(name, c0 + 256, c0 + 512)]

            U_A = unit_pair("w_in_2", 0)
            U_QKV = [unit_pair("w_in_2", 512 + 512 * i) for i in range(3)]
            U_GGATE = unit_pair("w_in_2", 2056)
            U_MERGE = [unit("w_in_2", 6168 + 256 * i, 6424 + 256 * i) for i in range(16)]
            U_SB = [unit_pair("w_in_2", 2568 + 512 * i) for i in range(3)]
            U_GLA = [unit_pair("w_in_2", 4104 + 512 * i) for i in range(3)]
            U_LGATE = unit_pair("w_in_2", 5656)
            U_BR = len(units)
            for n in range(4):
                for nb in range(2):
                    units.append([(0, 4, 512, 0, 512, A["w_branch_2"][0, n, :, 512 * nb:512 * nb + 512]
                                   .rearrange("(k p) n -> p k n", p=P))])
            U_OUT = len(units)
            for nb in range(4):
                unit("w_out_2", 256 * nb, 256 * nb + 256)
            U_HID = len(units)
            n_hidden = N_EXPERTS * D_EXPERT // 256
            per = D_EXPERT // 256

            def of_expert(name, n):
                c0 = 256 * (n % per)
                return A[name][0, n // per, :, c0:c0 + 256].rearrange("(k p) n -> p k n", p=P)

            units += hidden_units(n_hidden, lambda n: of_expert("w_gate_2", n), lambda n: of_expert("w_up_2", n),
                                  lambda n: A["w_down_2"][0, n // per, 256 * (n % per):256 * (n % per) + 256, :]
                                  .rearrange("(k p) n -> p k n", p=P))
            with ExitStack() as st:
                ring = Ring(nc, "second", sb("raw_w", [P, 3, UNIT], st), sb("split_w", [P, 2, 2, UNIT], st, FR), units)
                comb = sb("combine", [P, TILES, N_EXPERTS], st)
                with ExitStack() as s1:
                    mixer(ring, s1, U_A, U_QKV, U_GGATE, U_MERGE, U_SB, U_GLA, U_LGATE, U_BR, U_OUT)
                dump("pre1", x[:, :, :])
                layer_norm("ln1", "ln1_g_2", "ln1_b_2")
                dump("x3", x[:, :, :])
                transpose_block("x3_T", x, hT)
                split_fm("x3_split", hT, hP, KD)
                router(comb)
                dump("comb", comb[:, :, :])
                gated_hidden("moe", ring, U_HID, n_hidden, lambda n, t: comb[:, t, n // per:n // per + 1])
                scaled_add()
                layer_norm("ln2", "ln2_g_2", "ln2_b_2")
            with nc.Block() as block:
                @block.sync
                def _(sp):
                    stored = nc.alloc_semaphore("stored")
                    sp.dma_start(OUT.rearrange("o (t p) d -> p (o t) d", p=P), x[:, :, :]).then_inc(stored, 16)
                    sp.wait_ge(stored, 16)

        def scaled_add():
            step = Count(nc, "moe_added")
            with nc.Block() as block:
                @block.vector
                def _(dve):
                    for q in range(4):
                        t, cut = q // 2, slice((q % 2) * 512, (q % 2) * 512 + 512)
                        signal(nc.vector.scalar_tensor_tensor(x[:, t, cut], x[:, t, cut], ALPHA, ps[4 + q][:, :],
                                                              ALU.mult, ALU.add), step)

        def layer_norm(tag, gain_name, bias_name):
            with ExitStack() as st:
                rows = sb(f"{tag}_rows", [P, 2, D], st)
                junk = sb(f"{tag}_junk", [P, TILES, D], st)
                loaded = nc.alloc_semaphore(f"{tag}_rows_loaded")
                step, squared, rooted = (Count(nc, f"{tag}_{n}") for n in ("step", "squared", "rooted"))
                with nc.Block() as block:
                    @block.sync
                    def _(sp):
                        for i, name in enumerate((gain_name, bias_name)):
                            sp.dma_start(rows[:, i, :], A[name].broadcast_to([P, D])).then_inc(loaded, 16)

                    @block.vector
                    def _(dve):
                        v = nc.vector
                        done(dve, v.tensor_reduce(rstat[:, 0:2], x[:, :, :], AX, ALU.add), step)
                        done(dve, v.tensor_scalar(rstat[:, 0:2], rstat[:, 0:2], 1.0 / D, None, ALU.mult), step)
                        for t in range(TILES):
                            done(dve, v.tensor_scalar(x[:, t, :], x[:, t, :], rstat[:, t:t + 1], None, ALU.subtract), step)
                        dve.wait_ge(rooted.sem, 2)
                        dve.wait_ge(loaded, 32)
                        for t in range(TILES):
                            done(dve, v.scalar_tensor_tensor(x[:, t, :], x[:, t, :], rstat[:, 4 + t:5 + t], rows[:, 0, :],
                                                             ALU.mult, ALU.mult), step)
                            done(dve, v.tensor_tensor(x[:, t, :], x[:, t, :], rows[:, 1, :], ALU.add), step)

                    @block.scalar
                    def _(act):
                        for t in range(TILES):
                            act.wait_ge(step.sem, 3 + t)
                            signal(nc.scalar.activation(junk[:, t, :], x[:, t, :], ACT.Square,
                                                        accum_out=rstat[:, 2 + t:3 + t]), squared)

                    @block.gpsimd
                    def _(pool):
                        pool.wait_ge(squared.sem, 2)
                        rsqrt_on_pool(pool, rstat[:, 4:6], rstat[:, 2:4], 2, rooted, 1.0 / D, LN_EPS)

        def router(comb):
            with ExitStack() as st:
                w = sb("router_w", [P, KD, N_EXPERTS], st)
                bias = sb("router_bias", [P, N_EXPERTS], st)
                sc = sb("router_scores", [P, TILES, 16], st)
                bi = sb("router_biased", [P, TILES, 16], st)
                t1 = sb("router_t1", [P, TILES, 16], st)
                t2 = sb("router_t2", [P, TILES, 16], st)
                gs = sb("router_groups", [P, TILES, 4], st)
                g1 = sb("router_g1", [P, TILES, 4], st)
                g2 = sb("router_g2", [P, TILES, 4], st)
                m = sb("router_max", [P, TILES, 1], st)
                loaded = nc.alloc_semaphore("router_loaded")
                scored, squashed, step = (Count(nc, f"router_{n}") for n in ("scored", "squashed", "step"))
                with nc.Block() as block:
                    @block.sync
                    def _(sp):
                        sp.dma_start(w[:, :, :], A["w_router_2"].rearrange("(k p) n -> p k n", p=P)).then_inc(loaded, 16)
                        sp.dma_start(bias[:, :], A["router_bias_2"].rearrange("(o n) -> o n", o=1)
                                     .broadcast_to([P, 16])).then_inc(loaded, 16)

                    @block.tensor
                    def _(pe):
                        pe.wait_ge(loaded, 32)
                        for t in range(TILES):
                            for k in range(KD):
                                ins = nc.tensor.matmul(ps[t][:, 0:16], hT[:, k, t * P:(t + 1) * P], w[:, k, :],
                                                       start=k == 0, stop=k == KD - 1)
                            ins.then_inc(scored.sem, 1)

                    @block.scalar
                    def _(act):
                        for t in range(TILES):
                            act.wait_ge(scored.sem, t + 1)
                            nc.scalar.activation(sc[:, t, :], ps[t][:, 0:16], ACT.Sigmoid).then_inc(squashed.sem, 1)

                    @block.vector
                    def _(dve):
                        v = nc.vector

                        def do(ins):
                            done(dve, ins, step)

                        def first_max(onehot, values, key, rank, n):
                            bc = [P, TILES, n]
                            do(v.tensor_reduce(m[:, :, :], values, AX, ALU.max))
                            do(v.tensor_tensor(key, values, m[:, :, :].broadcast_to(bc), ALU.is_equal))
                            do(v.tensor_tensor(key, key, rank.unsqueeze(1).broadcast_to(bc), ALU.mult))
                            do(v.tensor_reduce(m[:, :, :], key, AX, ALU.max))
                            do(v.tensor_tensor(onehot, key, m[:, :, :].broadcast_to(bc), ALU.is_equal))

                        dve.wait_ge(loaded, 32)
                        dve.wait_ge(squashed.sem, 2)
                        S16, B16, T1, T2 = (a[:, :, :] for a in (sc, bi, t1, t2))
                        do(v.tensor_tensor(B16, S16, bias[:, :].unsqueeze(1).broadcast_to([P, TILES, 16]), ALU.add))
                        e = B16.rearrange("p t (g e) -> p t g e", e=4)
                        pairs = [(a, b) for a in range(4) for b in range(a + 1, 4)]
                        for i, (a, b) in enumerate(pairs):
                            dst = gs[:, :, :] if i == 0 else g1[:, :, :]
                            do(v.tensor_tensor(dst, e[:, :, :, a], e[:, :, :, b], ALU.add))
                            if i:
                                do(v.tensor_tensor(gs[:, :, :], gs[:, :, :], g1[:, :, :], ALU.max))
                        first_max(g2[:, :, :], gs[:, :, :], g1[:, :, :], const("rank4"), 4)
                        inside = g2[:, :, :].unsqueeze(3).broadcast_to([P, TILES, 4, 4])
                        do(v.tensor_tensor(e, e, inside, ALU.mult))
                        do(v.tensor_scalar(g1[:, :, :], g2[:, :, :], -1.0, -NEG, ALU.add, ALU.mult))
                        do(v.tensor_tensor(e, e, g1[:, :, :].unsqueeze(3).broadcast_to([P, TILES, 4, 4]), ALU.add))
                        first_max(T1, B16, T2, const("rank16"), 16)
                        do(v.scalar_tensor_tensor(B16.rearrange("p t e -> p (t e)"), T1.rearrange("p t e -> p (t e)"),
                                                  4 * NEG, B16.rearrange("p t e -> p (t e)"), ALU.mult, ALU.add))
                        first_max(comb[:, :, :], B16, T2, const("rank16"), 16)
                        do(v.tensor_tensor(comb[:, :, :], comb[:, :, :], T1, ALU.add))
                        do(v.tensor_tensor(comb[:, :, :], comb[:, :, :], S16, ALU.mult))
                        do(v.tensor_reduce(m[:, :, :], comb[:, :, :], AX, ALU.add))
                        do(v.reciprocal(m[:, :, :], m[:, :, :]))
                        do(v.tensor_tensor(comb[:, :, :], comb[:, :, :], m[:, :, :].broadcast_to([P, TILES, 16]), ALU.mult))

        def mixer(ring, s1, U_A, U_QKV, U_GGATE, U_MERGE, U_SB, U_GLA, U_LGATE, U_BR, U_OUT):
            v, a = nc.vector, nc.scalar
            yT = [None] * 4
            yT[0] = sb("y_lru", [P, 4, S], s1)
            yT[1] = sb("y_gdn", [P, 4, S], s1)
            par = sb("mixer_columns", [P, 86], s1)
            CONV_A, CONV_B, B_A, B_X, LAM, CONV_G, GDN_N, GLA_B, GLA_N = 0, 16, 20, 24, 28, 32, 80, 81, 85
            merge_gates = sb("merge_gates", [P, TILES, 4 * D], s1)
            small = sb("small_w", [P, KD, 24], s1)
            w_up = sb("gla_up", [16, 512], s1)
            tok8 = sb("beta_decay", [P, TILES, 8], s1)
            hrow = sb("head_rows", [P, 8], s1)
            lrT = sb("low_rank_T", [16, S], s1)

            with ExitStack() as s2:
                raw = sb("raw_2", [P, P], s2)
                gain = sb("final_gain", [P, D], s2)
                raw_loaded, gain_loaded = nc.alloc_semaphore("raw_2_loaded"), nc.alloc_semaphore("final_gain_loaded")
                turned, out = nc.alloc_semaphore("raw_2_turned"), nc.alloc_semaphore("raw_2_out")
                with nc.Block() as block:
                    @block.sync
                    def _(sp):
                        sp.dma_start(gain[:, :], A["final_norm_g"].rearrange("(o n) -> o n", o=1).broadcast_to([P, D])) \
                            .then_inc(gain_loaded, 16)
                        n = 0
                        for name, at, rows in (("conv_a_w_2", CONV_A, 16), ("conv_a_b_2", CONV_B, 4), ("rg_b_a_2", B_A, 4),
                                               ("rg_b_x_2", B_X, 4), ("rg_lambda_2", LAM, 4), ("gdn_conv_w_2", CONV_G, 48),
                                               ("gdn_norm_w_2", GDN_N, 1), ("gla_b_gate_2", GLA_B, 4),
                                               ("gla_norm_w_2", GLA_N, 1)):
                            src = A[name]
                            src = src[0, :, :].rearrange("k (c p) -> (k c) p", p=P) if len(src.shape) == 3 else \
                                src.rearrange("o (c p) -> (o c) p", p=P)
                            sp.dma_start(raw[at:at + rows, :], src).then_inc(raw_loaded, 16)
                        sp.dma_start(small[:, :, 0:8], cols2("w_in_2", 2048, 2056)).then_inc(gain_loaded, 16)
                        sp.dma_start(small[:, :, 8:24], cols2("w_in_2", 5640, 5656)).then_inc(gain_loaded, 16)
                        sp.dma_start(w_up[:, :], A["gla_w_gate_up_2"][0, :, :]).then_inc(gain_loaded, 16)
                        sp.dma_start(hrow[:, 0:4], A["gdn_a_log_2"].broadcast_to([P, 4])).then_inc(gain_loaded, 16)
                        sp.dma_start(hrow[:, 4:8], A["gdn_dt_bias_2"].broadcast_to([P, 4])).then_inc(gain_loaded, 16)
                        ring.feed(sp, -1)
                        sp.wait_ge(gain_loaded, 16 * 6)

                    @block.tensor
                    def _(pe):
                        pe.wait_ge(raw_loaded, 16 * 9)
                        nc.tensor.transpose(ps[0][:, 0:86], raw[0:86, :], ident[0:86, 0:86]).then_inc(turned, 1)

                    @block.scalar
                    def _(act):
                        act.wait_ge(turned, 1)
                        a.activation(par[:, :], ps[0][:, 0:86], ACT.Copy).then_inc(out, 1)
                rms_norm_to_fm("final", row_gain=gain[:, :], keep=True)
                split_fm("final_split", hT, hP, KD)
            dump("x2", x[:, :, :])

            def fm_jobs(pair, dst, at=0, func=None):
                def out(b, act):
                    d = dst[:, at + b, :]
                    return copy_out(act, d) if func is None else (lambda src: a.activation(d, src, func))
                return [Job(pair[b // 2], "fm", b % 2, S, b % 2 == 0 or func is not None,
                            out(b, b % 2 == 0 or func is not None)) for b in range(4)]

            def tok_jobs(pair, dst):
                return [Job(pair[i], "tok", t, 256, t == 0, copy_out(t == 0, dst[:, t, 256 * i:256 * i + 256]))
                        for i in range(2) for t in range(TILES)]

            with ExitStack() as s2:
                qkv = sb("gdn_qkv", [P, 12, S], s2)
                ggate = sb("gdn_gate", [P, 4, S], s2)
                w_ax = sb("lru_w", [P, 2, 4, P], s2)
                work_ = sb("work", [P, 9, 4 * S], s2)
                work = [work_[:, i, :] for i in range(9)] + [hT[:, 4 * i:4 * i + 4, :].rearrange("p c s -> p (c s)")
                                                             for i in range(2)]
                ain = work[4].rearrange("p (c s) -> p c s", c=4)
                cleared, w_ax_loaded = nc.alloc_semaphore("lru_w_cleared"), nc.alloc_semaphore("lru_w_loaded")

                def clear(pool):
                    pool.memset(w_ax[:, :, :, :], 0.0).then_inc(cleared, 1)

                def load_lru(sp):
                    sp.wait_ge(cleared, 1)
                    for i, name in enumerate(("rg_w_a_2", "rg_w_x_2")):
                        for half in range(2):
                            src = A[name][0, half:8:2, :, :].rearrange("c i j -> i c j")
                            sp.dma_start(w_ax[64 * half:64 * half + 64, i, :, 64 * half:64 * half + 64], src) \
                                .then_inc(w_ax_loaded, 16)
                    sp.wait_ge(w_ax_loaded, 64)

                jobs = fm_jobs(U_A, ain)
                for i in range(3):
                    jobs += fm_jobs(U_QKV[i], qkv, 4 * i)
                jobs += fm_jobs(U_GGATE, ggate, 0, ACT.Silu)
                small_done, small_out = nc.alloc_semaphore("small_summed"), nc.alloc_semaphore("small_out")

                def small_copy(act):
                    act.wait_ge(small_done, 1)
                    a.activation(tok8[:, :, :].rearrange("p t c -> p (t c)"), ps[7][:, 0:16], ACT.Copy).then_inc(small_out, 1)
                    a.activation(lrT[:, :], ps[7][0:16, S:2 * S], ACT.Copy).then_inc(small_out, 1)

                def small_products(pe):
                    for t in range(TILES):
                        for k in range(KD):
                            nc.tensor.matmul(ps[7][:, 8 * t:8 * t + 8], hT[:, k, t * P:(t + 1) * P], small[:, k, 0:8],
                                             start=k == 0, stop=k == KD - 1)
                    for k in range(KD):
                        ins = nc.tensor.matmul(ps[7][0:16, S:2 * S], small[:, k, 8:24], hT[:, k, :],
                                               start=k == 0, stop=k == KD - 1)
                    ins.then_inc(small_done, 1)

                project("mix_in", ring, jobs, banks=7, extra={"tensor": small_products, "scalar": small_copy,
                                                              "gpsimd": clear, "sync": load_lru})
                dump("ain", ain[:, :, :])
                dump("tok8", tok8[:, :, :])

                def W(i):
                    return work[i]

                def blocks4(i):
                    return work[i].rearrange("p (c s) -> p c s", c=4)

                conv = Count(nc, "conv_step")
                xc = blocks4(0)
                silu_out = nc.alloc_semaphore("gdn_silu")
                gdn_conv = [blocks4(i) for i in (1, 2, 3)]

                def convolve(dve):
                    def one(dst, src, w_cols, bias):
                        w3 = par[:, w_cols[3]:w_cols[3] + 1]
                        if bias is None:
                            ins = v.tensor_scalar(dst, src, w3, None, ALU.mult)
                        else:
                            ins = v.tensor_scalar(dst, src, w3, bias, ALU.mult, ALU.add)
                        done(dve, ins, conv)
                        yield
                        for k in range(3):
                            back = 3 - k
                            done(dve, v.scalar_tensor_tensor(dst[:, back:S], src[:, 0:S - back],
                                                             par[:, w_cols[k]:w_cols[k] + 1], dst[:, back:S],
                                                             ALU.mult, ALU.add), conv)
                            yield
                    for c in range(4):
                        yield from one(xc[:, c, :], ain[:, c, :], [CONV_A + 4 * k + c for k in range(4)],
                            par[:, CONV_B + c:CONV_B + c + 1])
                    for c in range(12):
                        yield from one(gdn_conv[c // 4][:, c % 4, :], qkv[:, c, :], [CONV_G + 12 * k + c for k in range(4)], None)

                def silus(act):
                    for i in range(3):
                        act.wait_ge(conv.sem, 4 * 4 * (i + 2))
                        a.activation(qkv[:, 4 * i:4 * i + 4, :].rearrange("p c s -> p (c s)"), W(1 + i),
                                     ACT.Silu).then_inc(silu_out, 1)

                jobs = [Job(U_MERGE[b], "tok", t, 256, True,
                            (lambda dst: lambda src: a.activation(dst, src, ACT.Sigmoid))(
                                merge_gates[:, t, 256 * b:256 * b + 256])) for b in range(16) for t in range(TILES)]
                project("merge_gates", ring, jobs, extra={"vector": convolve, "scalar": silus}, pace=5)
                dump("xc", xc)
                dump("qkv", qkv[:, :, :])

                lru(xc, blocks4, W, par, w_ax, yT[0], B_A, B_X, LAM)
                dump("ylru", yT[0][:, :, :])
                gdn(qkv, ggate, blocks4, W, tok8, hrow, par[:, GDN_N:GDN_N + 1], yT[1])
                dump("ygdn", yT[1][:, :, :])

            yT[2] = sb("y_sb", [P, 4, S], s1)
            yT[3] = sb("y_gla", [P, 4, S], s1)
            with ExitStack() as s2:
                q = sb("gla_q", [P, 4, S], s2)
                k = sb("gla_k", [P, 4, S], s2)
                vt = sb("gla_v", [P, TILES, 512], s2)
                lgate = sb("gla_gate", [P, 4, S], s2)
                with ExitStack() as s3:
                    sq = sb("sb_q", [P, 4, S], s3)
                    sk = sb("sb_k", [P, 4, S], s3)
                    sv = sb("sb_v", [P, TILES, 512], s3)
                    jobs = []
                    for (uq, uk, uv), (dq, dk, dv) in ((U_SB, (sq, sk, sv)), (U_GLA, (q, k, vt))):
                        jobs += fm_jobs(uq, dq) + fm_jobs(uk, dk) + tok_jobs(uv, dv)
                    jobs += fm_jobs(U_LGATE, lgate, 0, ACT.Silu)
                    project("mix_in_2", ring, jobs)
                    stick_breaking(sq, sk, sv, yT[2], s3)
                    dump("ysb", yT[2][:, :, :])
                gla(q, k, vt, lgate, lrT, w_up, par, GLA_B, par[:, GLA_N:GLA_N + 1], yT[3], s2)
                dump("ygla", yT[3][:, :, :])

            with ExitStack() as s2:
                m = sb("mixer_sum", [P, TILES, D], s2)
                part = sb("mixer_part", [P, 512], s2)
                step = Count(nc, "mixer_step")
                yP = sb("mixer_pair", [P, 4, 2, 4, S], s2, FR)
                for n in range(4):
                    split_fm(f"mixer_split{n}", yT[n], yP[:, n, :, :, :], 4)
                jobs = []
                for n in range(4):
                    for nb in range(2):
                        for t in range(TILES):
                            def out(src, n=n, nb=nb, t=t):
                                gate = merge_gates[:, t, n * D + nb * 512:n * D + nb * 512 + 512]
                                dst = m[:, t, nb * 512:nb * 512 + 512]
                                if n == 0:
                                    return v.tensor_tensor(dst, src, gate, ALU.mult)
                                done(v, v.tensor_tensor(part[:, :], src, gate, ALU.mult), step)
                                return v.tensor_tensor(dst, dst, part[:, :], ALU.add)

                            jobs.append(Job(U_BR + 2 * n + nb, "tok", t, 512, False, out, k=4, lhs=yP[:, n, :, :, :],
                                            unit_width=512))
                project("mixer_merge", ring, jobs)
                transpose_block("mixer_T", m, hT)
                split_fm("mixer_T_split", hT, hP, KD)
            jobs = []
            for nb in range(4):
                for t in range(TILES):
                    cut = slice(nb * 256, nb * 256 + 256)

                    def out(src, t=t, cut=cut):
                        return v.scalar_tensor_tensor(x[:, t, cut], x[:, t, cut], ALPHA, src, ALU.mult, ALU.add)

                    jobs.append(Job(U_OUT + nb, "tok", t, 256, False, out))
            project("mixer_out", ring, jobs)

        def cols2(name, c0, c1):
            return A[name][0, :, c0:c1].rearrange("(k p) n -> p k n", p=P)

        def lru(xc, blocks4, W, par, w_ax, y, B_A, B_X, LAM):
            v, a = nc.vector, nc.scalar
            R, I, T, M, N = 1, 2, 3, 4, 5
            summed, squashed, step, acted, coef_ready = (Count(nc, f"lru_{n}") for n in
                                                         ("summed", "squashed", "step", "acted", "coef"))
            with ExitStack() as st:
                cf = sb("lru_coef", [P, 4, 4], st)
                with nc.Block() as block:
                    @block.tensor
                    def _(pe):
                        for i in range(2):
                            for c in range(4):
                                ins = nc.tensor.matmul(ps[2 * i + c // 2][:, (c % 2) * S:(c % 2 + 1) * S],
                                                       w_ax[:, i, c, :], xc[:, c, :], start=True, stop=True)
                            ins.then_inc(summed.sem, 1)

                    @block.scalar
                    def _(act):
                        for i, (B, dst) in enumerate(((B_A, R), (B_X, I))):
                            act.wait_ge(summed.sem, i + 1)
                            for c in range(4):
                                ins = a.activation(blocks4(dst)[:, c, :], ps[2 * i + c // 2][:, (c % 2) * S:(c % 2 + 1) * S],
                                                   ACT.Sigmoid, bias=par[:, B + c:B + c + 1])
                                ins.then_inc(squashed.sem, 1)
                        act.wait_ge(step.sem, 1)
                        done(act, a.activation(cf[:, 1, :], cf[:, 0, :], ACT.Exp), coef_ready)
                        done(act, a.activation(cf[:, 2, :], cf[:, 1, :], ACT.Ln, bias=1.0), coef_ready)
                        act.wait_ge(step.sem, 8)
                        done(act, a.activation(W(M), W(T), ACT.Tanh), acted)
                        done(act, a.activation(W(R), W(T), ACT.Exp), acted)
                        act.wait_ge(step.sem, 11)
                        done(act, a.activation(W(N), W(T), ACT.Sqrt), acted)

                    @block.vector
                    def _(dve):
                        def do(ins):
                            done(dve, ins, step)
                        lam = par[:, LAM:LAM + 4]
                        do(v.scalar_tensor_tensor(cf[:, 0, :], lam, -1.0, lam, ALU.mult, ALU.min))
                        do(v.tensor_scalar(cf[:, 3, :], lam, -1.0, 0.0, ALU.mult, ALU.max))
                        dve.wait_ge(coef_ready.sem, 2)
                        do(v.tensor_tensor(cf[:, 3, :], cf[:, 3, :], cf[:, 2, :], ALU.add))
                        do(v.tensor_scalar(cf[:, 3, :], cf[:, 3, :], -8.0, None, ALU.mult))
                        dve.wait_ge(squashed.sem, 8)
                        for c in range(4):
                            do(v.tensor_scalar(blocks4(T)[:, c, :], blocks4(R)[:, c, :], cf[:, 3, c:c + 1], None, ALU.mult))
                        dve.wait_ge(acted.sem, 2)
                        do(v.tensor_scalar(W(T), W(M), -1.0, 1.0, ALU.mult, ALU.add))
                        do(v.reciprocal(W(N), W(T)))
                        do(v.scalar_tensor_tensor(W(T), W(M), -2.0, W(N), ALU.mult, ALU.mult))
                        dve.wait_ge(acted.sem, 3)
                        do(v.memset(blocks4(N)[:, :, 0:1], 1.0))
                        do(v.tensor_tensor(W(N), W(N), W(I), ALU.mult))
                        do(v.tensor_tensor(W(N), W(N), W(0), ALU.mult))
                        for c in range(4):
                            do(v.tensor_tensor_scan(y[:, c, :], blocks4(R)[:, c, :], blocks4(N)[:, c, :], 0.0,
                                                    ALU.mult, ALU.add))

        def head_norm(tag, oT, sqT, rsT, gain, gate, y):
            v, a = nc.vector, nc.scalar
            squared, summed, rooted, step = (Count(nc, f"{tag}_{n}") for n in ("squared", "summed", "rooted", "step"))
            with nc.Block() as block:
                @block.vector
                def _(dve):
                    done(dve, v.tensor_tensor(sqT, oT, oT, ALU.mult), squared)
                    for b in range(2):
                        cut = slice(512 * b, 512 * b + 512)
                        dve.wait_ge(summed.sem, b + 1)
                        done(dve, v.tensor_scalar(rsT[:, cut], ps[b][:, :], 1.0 / P, EPS, ALU.mult, ALU.add), step)
                    dve.wait_ge(rooted.sem, 1)
                    done(dve, v.reciprocal(rsT, rsT), step)
                    done(dve, v.scalar_tensor_tensor(y, oT, gain, gate, ALU.mult, ALU.mult), step)
                    done(dve, v.tensor_tensor(y, y, rsT, ALU.mult), step)

                @block.tensor
                def _(pe):
                    pe.wait_ge(squared.sem, 1)
                    for b in range(2):
                        nc.tensor.matmul(ps[b][:, :], ones, sqT[:, 512 * b:512 * b + 512], start=True,
                                         stop=True).then_inc(summed.sem, 1)

                @block.scalar
                def _(act):
                    act.wait_ge(step.sem, 2)
                    a.activation(rsT, rsT, ACT.Sqrt).then_inc(rooted.sem, 1)

        def gdn(qkv, ggate, blocks4, W, tok8, hrow, gain, y):
            v, a = nc.vector, nc.scalar
            qT = qkv[:, 0:4, :].rearrange("p c s -> p (c s)")
            kT = qkv[:, 4:8, :].rearrange("p c s -> p (c s)")
            vT = qkv[:, 8:12, :].rearrange("p c s -> p (c s)")
            SQ, RS = 0, 1
            ROW, BROW, DT, AT, ATT, AN, AM, U, TN, Y = 0, 1, 2, 3, 4, 5, 6, 7, 8, 9
            EXTRA = 10
            VK = qkv[:, 8:12, :]

            def g8(flat):
                return flat.rearrange("p (g s) -> p g s", g=8)

            with ExitStack() as st:
                tg = sb("gdn_tok", [P, 8, 8], st)
                BETA, G, GC, GL, BE, KD_, T1, T2 = range(8)
                tq = {i: tg[:, i, :] for i in range(8)}

                def by_tile(i):
                    return tg[:, i, :].rearrange("p (h t) -> p t h", t=2)

                step, squared, summed, rooted = (Count(nc, f"gdn_l2_{n}") for n in ("step", "squared", "summed", "rooted"))
                with nc.Block() as block:
                    @block.vector
                    def _(dve):
                        done(dve, v.tensor_tensor(W(SQ), qT, qT, ALU.mult), squared)
                        done(dve, v.tensor_tensor(W(2), kT, kT, ALU.mult), squared)
                        for i in range(2):
                            rs = W(1 + 2 * i)
                            for b in range(2):
                                dve.wait_ge(summed.sem, 2 * i + b + 1)
                                done(dve, v.tensor_scalar(rs[:, 512 * b:512 * b + 512], ps[2 * i + b][:, :], EPS, None,
                                                          ALU.add), step)
                        dve.wait_ge(rooted.sem, 2)
                        for i, z in enumerate((qT, kT)):
                            rs = W(1 + 2 * i)
                            done(dve, v.reciprocal(rs, rs), step)
                            done(dve, v.scalar_tensor_tensor(z, z, P ** -0.5 if i == 0 else 1.0, rs, ALU.mult, ALU.mult), step)
                        d = by_tile(T1)
                        bc = [P, TILES, 4]
                        done(dve, v.tensor_tensor(d, tok8[:, :, 4:8], hrow[:, 4:8].unsqueeze(1).broadcast_to(bc), ALU.add), step)
                        done(dve, v.tensor_scalar(tq[G], tq[T1], 0.0, None, ALU.max), step)
                        done(dve, v.scalar_tensor_tensor(tq[T1], tq[T1], -1.0, tq[T1], ALU.mult, ALU.min), step)
                        dve.wait_ge(rooted.sem, 6)
                        done(dve, v.tensor_tensor(tq[G], tq[G], tq[T2], ALU.add), step)
                        done(dve, v.tensor_tensor(by_tile(G), by_tile(G), hrow[:, 0:4].unsqueeze(1).broadcast_to(bc), ALU.mult), step)
                        done(dve, v.tensor_scalar(tq[G], tq[G], -1.0, None, ALU.mult), step)

                    @block.tensor
                    def _(pe):
                        for i in range(2):
                            pe.wait_ge(squared.sem, i + 1)
                            for b in range(2):
                                nc.tensor.matmul(ps[2 * i + b][:, :], ones, W(2 * i)[:, 512 * b:512 * b + 512],
                                                 start=True, stop=True).then_inc(summed.sem, 1)

                    @block.scalar
                    def _(act):
                        for i in range(2):
                            act.wait_ge(step.sem, 2 * i + 2)
                            done(act, a.activation(W(1 + 2 * i), W(1 + 2 * i), ACT.Sqrt), rooted)
                        done(act, a.activation(by_tile(BETA), tok8[:, :, 0:4], ACT.Sigmoid), rooted)
                        act.wait_ge(step.sem, 11)
                        done(act, a.activation(hrow[:, 0:4], hrow[:, 0:4], ACT.Exp), rooted)
                        done(act, a.activation(tq[T2], tq[T1], ACT.Exp), rooted)
                        done(act, a.activation(tq[T2], tq[T2], ACT.Ln, bias=1.0), rooted)

                mm = Count(nc, "gdn_a_mm")
                step, acted = Count(nc, "gdn_a_step"), Count(nc, "gdn_a_act")
                with nc.Block() as block:
                    @block.tensor
                    def _(pe):
                        nc.tensor.matmul(ps[0][:, 0:8], const("cum64"), tq[G], start=True, stop=True)
                        nc.tensor.matmul(ps[0][:, 8:16], const("blk64"), tq[G], start=True, stop=True).then_inc(mm.sem, 1)
                        pe.wait_ge(step.sem, 2)
                        for g in range(8):
                            ins = nc.tensor.matmul(ps[1 + g // 4][:, (g % 4) * P:(g % 4 + 1) * P], g8(W(AM))[:, g, :],
                                                   const("cum64"), start=True, stop=True)
                        ins.then_inc(mm.sem, 1)
                        for g in range(8):
                            ins = nc.tensor.matmul(ps[3 + g // 4][:, (g % 4) * P:(g % 4 + 1) * P], g8(W(U))[:, g, :],
                                                   ident, start=True, stop=True)
                        ins.then_inc(mm.sem, 1)
                        for g in range(8):
                            ins = nc.tensor.matmul(ps[5 + g // 4][:, (g % 4) * P:(g % 4 + 1) * P], g8(kT)[:, g, :],
                                                   g8(kT)[:, g, :], start=True, stop=True)
                        ins.then_inc(mm.sem, 1)
                        pe.wait_ge(acted.sem, 2)
                        for g in range(8):
                            ins = nc.tensor.matmul(ps[1 + g // 4][:, (g % 4) * P:(g % 4 + 1) * P], g8(kT)[:, g, :],
                                                   g8(qT)[:, g, :], start=True, stop=True)
                        ins.then_inc(mm.sem, 1)

                    @block.scalar
                    def _(act):
                        act.wait_ge(mm.sem, 2)
                        for b in range(2):
                            done(act, a.activation(W(ROW)[:, 512 * b:512 * b + 512], ps[1 + b][:, :], ACT.Copy), acted)
                        act.wait_ge(mm.sem, 3)
                        for b in range(2):
                            done(act, a.activation(W(BROW)[:, 512 * b:512 * b + 512], ps[3 + b][:, :], ACT.Copy), acted)
                        act.wait_ge(step.sem, 12)
                        done(act, a.activation(W(DT), W(DT), ACT.Exp), acted)
                        done(act, a.activation(W(ROW), W(ROW), ACT.Exp), acted)
                        done(act, a.activation(tq[BE], tq[GC], ACT.Exp), acted)
                        done(act, a.activation(tq[KD_], tq[KD_], ACT.Exp), acted)

                    @block.vector
                    def _(dve):
                        def do(ins):
                            done(dve, ins, step)
                        bc = [P, 8, P]
                        do(v.tensor_copy(g8(W(AM)), tq[G].unsqueeze(2).broadcast_to(bc)))
                        do(v.tensor_copy(g8(W(U)), tq[BETA].unsqueeze(2).broadcast_to(bc)))
                        dve.wait_ge(mm.sem, 1)
                        do(v.tensor_copy(tq[GC], ps[0][:, 0:8]))
                        do(v.tensor_tensor(tq[KD_], ps[0][:, 8:16], tq[GC], ALU.subtract))
                        dve.wait_ge(acted.sem, 2)
                        for g in range(8):
                            do(v.tensor_scalar(g8(W(DT))[:, g, :], g8(W(ROW))[:, g, :], tq[GC][:, g:g + 1], 0.0,
                                               ALU.subtract, ALU.min))
                        dve.wait_ge(acted.sem, 7)
                        do(v.tensor_tensor(tq[BE], tq[BE], tq[BETA], ALU.mult))
                        do(v.tensor_tensor(g8(W(AN)), g8(W(DT)), const("strict64").unsqueeze(1).broadcast_to(bc), ALU.mult))
                        do(v.tensor_tensor(W(AN), W(AN), W(BROW), ALU.mult))
                        do(v.tensor_tensor(g8(W(DT)), g8(W(DT)), const("cum64").unsqueeze(1).broadcast_to(bc), ALU.mult))
                        dve.wait_ge(mm.sem, 5)
                        for b in range(2):
                            cut = slice(512 * b, 512 * b + 512)
                            do(v.tensor_tensor(W(AT)[:, cut], W(AN)[:, cut], ps[5 + b][:, :], ALU.mult))
                            do(v.tensor_tensor(W(ATT)[:, cut], W(DT)[:, cut], ps[1 + b][:, :], ALU.mult))

                step, mm, yout = Count(nc, "gdn_inv_step"), Count(nc, "gdn_inv_mm"), Count(nc, "gdn_inv_y")
                base = {}
                levels = (2, 4, 8, 16, 32)
                with nc.Block() as block:
                    bc = [P, 8, P]

                    @block.vector
                    def _(dve):
                        def do(ins):
                            done(dve, ins, step)
                        dve.wait_ge(mm.sem, 1)
                        for b in range(2):
                            do(v.tensor_copy(W(AN)[:, 512 * b:512 * b + 512], ps[b][:, :]))
                        for dst, src, mask in ((U, AT, "level1_t"), (TN, AN, "level1")):
                            do(v.tensor_tensor(g8(W(dst)), g8(W(src)), const(mask).unsqueeze(1).broadcast_to(bc), ALU.mult))
                            do(v.tensor_tensor(g8(W(dst)), ident.unsqueeze(1).broadcast_to(bc), g8(W(dst)), ALU.subtract))
                        for n, s in enumerate(levels):
                            do(v.tensor_tensor(g8(W(AM)), g8(W(AN)), const(f"level{s}").unsqueeze(1).broadcast_to(bc), ALU.mult))
                            dve.wait_ge(mm.sem, 3 + 2 * n)
                            for b in range(2):
                                cut = slice(512 * b, 512 * b + 512)
                                do(v.tensor_tensor(W(U)[:, cut], W(U)[:, cut], ps[4 + b][:, :], ALU.subtract))
                                do(v.tensor_tensor(W(TN)[:, cut], W(TN)[:, cut], ps[6 + b][:, :], ALU.subtract))

                    @block.tensor
                    def _(pe):
                        for g in range(8):
                            ins = nc.tensor.transpose(ps[g // 4][:, (g % 4) * P:(g % 4 + 1) * P], g8(W(AT))[:, g, :], ident)
                        ins.then_inc(mm.sem, 1)
                        for n in range(5):
                            pe.wait_ge(step.sem, 7 + 5 * n)
                            for g in range(8):
                                ins = nc.tensor.matmul(ps[2 + g // 4][:, (g % 4) * P:(g % 4 + 1) * P], g8(W(AM))[:, g, :],
                                                       g8(W(U))[:, g, :], start=True, stop=True)
                            ins.then_inc(mm.sem, 1)
                            pe.wait_ge(yout.sem, 2 * n + 2)
                            for g in range(8):
                                nc.tensor.matmul(ps[4 + g // 4][:, (g % 4) * P:(g % 4 + 1) * P], g8(W(TN))[:, g, :],
                                                 g8(W(Y))[:, g, :], start=True, stop=True)
                            for g in range(8):
                                ins = nc.tensor.matmul(ps[6 + g // 4][:, (g % 4) * P:(g % 4 + 1) * P], g8(W(Y))[:, g, :],
                                                       g8(W(TN))[:, g, :], start=True, stop=True)
                            ins.then_inc(mm.sem, 1)

                    @block.scalar
                    def _(act):
                        for n in range(5):
                            act.wait_ge(mm.sem, 2 + 2 * n)
                            for b in range(2):
                                done(act, a.activation(W(Y)[:, 512 * b:512 * b + 512], ps[2 + b][:, :], ACT.Copy), yout)
                dump("gdnU", W(U))

                KBE, KDEC, VB, WT, UU, QD = 5, 6, 2, 8, 9, 3
                step, mm, acted = Count(nc, "gdn_w_step"), Count(nc, "gdn_w_mm"), Count(nc, "gdn_w_act")
                with nc.Block() as block:
                    @block.tensor
                    def _(pe):
                        for i, z in enumerate((kT, vT)):
                            for g in range(8):
                                ins = nc.tensor.transpose(ps[2 * i + g // 4][:, (g % 4) * P:(g % 4 + 1) * P], g8(z)[:, g, :], ident)
                            ins.then_inc(mm.sem, 1)
                        pe.wait_ge(acted.sem, 16)
                        for g in range(8):
                            ins = nc.tensor.matmul(ps[4 + g // 4][:, (g % 4) * P:(g % 4 + 1) * P], g8(W(KBE))[:, g, :],
                                                   g8(W(U))[:, g, :], start=True, stop=True)
                        ins.then_inc(mm.sem, 1)
                        for g in range(8):
                            ins = nc.tensor.matmul(ps[6 + g // 4][:, (g % 4) * P:(g % 4 + 1) * P], g8(W(U))[:, g, :],
                                                   g8(W(VB))[:, g, :], start=True, stop=True)
                        ins.then_inc(mm.sem, 1)

                    @block.scalar
                    def _(act):
                        for n, (dst, bank, colq) in enumerate(((KBE, 0, BE), (VB, 2, BETA))):
                            act.wait_ge(mm.sem, n + 1)
                            for g in range(8):
                                done(act, a.activation(g8(W(dst))[:, g, :], ps[bank + g // 4][:, (g % 4) * P:(g % 4 + 1) * P],
                                                       ACT.Copy, scale=tq[colq][:, g:g + 1]), acted)
                        act.wait_ge(mm.sem, 3)
                        for b in range(2):
                            done(act, a.activation(W(WT)[:, 512 * b:512 * b + 512], ps[4 + b][:, :], ACT.Copy), acted)

                    @block.vector
                    def _(dve):
                        def do(ins):
                            done(dve, ins, step)
                        do(v.tensor_tensor(W(QD), qT, W(ROW), ALU.mult))
                        dve.wait_ge(acted.sem, 8)
                        for g in range(8):
                            do(v.tensor_scalar(g8(W(KDEC))[:, g, :], ps[g // 4][:, (g % 4) * P:(g % 4 + 1) * P],
                                               tq[KD_][:, g:g + 1], None, ALU.mult))
                        dve.wait_ge(mm.sem, 4)
                        for b in range(2):
                            do(v.tensor_copy(W(UU)[:, 512 * b:512 * b + 512], ps[6 + b][:, :]))

                step, mm = Count(nc, "gdn_scan_step"), Count(nc, "gdn_scan_mm")
                oT = W(5)
                with ExitStack() as s5:
                    state = W(10)[:, 0:512].rearrange("p (h d) -> p h d", h=4)
                    new = W(10)[:, 512:1024].rearrange("p (h d) -> p h d", h=4)
                    with nc.Block() as block:
                        @block.vector
                        def _(dve):
                            def do(ins):
                                done(dve, ins, step)
                            do(v.memset(state, 0.0))
                            uu = W(UU).rearrange("p (h t d) -> p h t d", h=4, t=2)
                            for n in range(4):
                                t, b0 = n // 2, 64 * (n % 2)
                                dve.wait_ge(mm.sem, 2 * n + 1)
                                do(v.tensor_tensor(new[b0:b0 + 64, :, :], uu[b0:b0 + 64, :, t, :],
                                                   ps[0][b0:b0 + 64, :].rearrange("p (h d) -> p h d", h=4), ALU.subtract))
                                dve.wait_ge(mm.sem, 2 * n + 2)
                                for h in range(4):
                                    do(v.scalar_tensor_tensor(state[:, h, :], state[:, h, :],
                                                              blocks4(ROW)[:, h, 64 * n + 63:64 * n + 64],
                                                              ps[1][:, h * P:(h + 1) * P], ALU.mult, ALU.add))

                        @block.tensor
                        def _(pe):
                            for n in range(4):
                                t, b0 = n // 2, 64 * (n % 2)
                                cut = slice(64 * n, 64 * n + 64)
                                pe.wait_ge(step.sem, 1 + 5 * n)
                                for h in range(4):
                                    ins = nc.tensor.matmul(ps[0][b0:b0 + 64, h * P:(h + 1) * P], blocks4(WT)[:, h, cut],
                                                           state[:, h, :], start=True, stop=True)
                                ins.then_inc(mm.sem, 1)
                                pe.wait_ge(step.sem, 2 + 5 * n)
                                for h in range(4):
                                    g = 2 * h + t
                                    out = ps[2 + h][:, cut]
                                    nc.tensor.matmul(out, state[:, h, :], blocks4(QD)[:, h, cut], start=True, stop=False)
                                    nc.tensor.matmul(out, new[b0:b0 + 64, h, :],
                                                     g8(W(ATT))[b0:b0 + 64, g, b0:b0 + 64], start=False, stop=True)
                                for h in range(4):
                                    g = 2 * h + t
                                    ins = nc.tensor.matmul(ps[1][:, h * P:(h + 1) * P], g8(W(KDEC))[b0:b0 + 64, g, :],
                                                           new[b0:b0 + 64, h, :], start=True, stop=True)
                                ins.then_inc(mm.sem, 1)
                    o_out = Count(nc, "gdn_o_out")
                    with nc.Block() as block:
                        @block.scalar
                        def _(act):
                            for h in range(4):
                                done(act, a.activation(blocks4(5)[:, h, :], ps[2 + h][:, 0:S], ACT.Copy), o_out)
                dump("gdnO", W(5))
            head_norm("gdn_norm", W(5), W(6), W(7), gain, ggate[:, :, :].rearrange("p c s -> p (c s)"),
                      y[:, :, :].rearrange("p c s -> p (c s)"))

        def stick_breaking(q, k, sv, y, s3):
            v, a = nc.vector, nc.scalar
            scale = 64 ** -0.5
            Wd = S + P
            with ExitStack() as st:
                ab = sb("sb_abs", [P, 2, Wd], st)
                score = sb("sb_score", [P, 2, Wd], st)
                keep = sb("sb_keep", [P, 2, Wd], st)
                wt = sb("sb_weights", [P, 2, Wd], st)
                scored, prepped, logged, kept, cumed, added, expd, masked, mixed, out, step = (
                    Count(nc, f"sb_{n}") for n in ("scored", "prepped", "logged", "kept", "cumed", "added", "expd",
                                                   "masked", "mixed", "out", "step"))
                exped = Count(nc, "sb_exped")
                strict = const("sb_strict")
                H = 8
                with nc.Block() as block:
                    @block.tensor
                    def _(pe):
                        for i in range(H + 2):
                            if i < H:
                                b0, c = 64 * (i % 2), i // 2
                                if i >= 2:
                                    pe.wait_ge(added.sem, i - 1)
                                kk, qq = k[b0:b0 + 64, c, :], q[b0:b0 + 64, c, :]
                                nc.tensor.matmul(ps[i % 2][:, 0:S], kk[:, 0:P], qq, start=True, stop=True)
                                nc.tensor.matmul(ps[i % 2][:, S:Wd], kk[:, P:S], qq[:, P:S], start=True,
                                                 stop=True).then_inc(scored.sem, 1)
                            if 1 <= i <= H:
                                n = i - 1
                                pe.wait_ge(kept.sem, n + 1)
                                if n >= 2:
                                    pe.wait_ge(added.sem, n - 1)
                                kp = keep[:, n % 2, :]
                                bank = ps[2 + n % 2]
                                nc.tensor.matmul(bank[:, 0:S], const("sb_incl"), kp[:, 0:S], start=True, stop=False)
                                nc.tensor.matmul(bank[:, P:S], ones, kp[:, S:Wd], start=False, stop=True)
                                nc.tensor.matmul(bank[:, S:Wd], const("sb_incl"), kp[:, S:Wd], start=True,
                                                 stop=True).then_inc(cumed.sem, 1)
                            if i >= 2:
                                n = i - 2
                                pe.wait_ge(masked.sem, n + 1)
                                if n >= 2:
                                    pe.wait_ge(out.sem, n - 1)
                                b0 = 64 * (n % 2)
                                o = ps[4 + n % 2][b0:b0 + 64, :]
                                nc.tensor.matmul(o[:, 0:S], sv[:, 0, 64 * n:64 * n + 64], wt[:, n % 2, 0:S], start=True, stop=False)
                                nc.tensor.matmul(o[:, P:S], sv[:, 1, 64 * n:64 * n + 64], wt[:, n % 2, S:Wd], start=False,
                                                 stop=True).then_inc(mixed.sem, 1)

                    @block.vector
                    def _(dve):
                        for i in range(H + 2):
                            if i < H:
                                dve.wait_ge(scored.sem, i + 1)
                                z = ps[i % 2][:, 0:Wd]
                                if i >= 2:
                                    dve.wait_ge(cumed.sem, i - 1)
                                zs = score[:, i % 2, :]
                                done(dve, v.tensor_scalar(zs, z, scale, None, ALU.mult), step)
                                v.scalar_tensor_tensor(ab[:, i % 2, :], zs, -1.0, zs, ALU.mult, ALU.min) \
                                    .then_inc(prepped.sem, 1)
                            if 1 <= i <= H:
                                n = i - 1
                                dve.wait_ge(cumed.sem, n + 1)
                                if n >= 2:
                                    dve.wait_ge(mixed.sem, n - 1)
                                v.tensor_tensor(wt[:, n % 2, :], score[:, n % 2, :], ps[2 + n % 2][:, 0:Wd],
                                                ALU.add).then_inc(added.sem, 1)
                            if i < H:
                                dve.wait_ge(logged.sem, i + 1)
                                kp, lg = keep[:, i % 2, :], ab[:, i % 2, :]
                                done(dve, v.scalar_tensor_tensor(lg, score[:, i % 2, :], 0.0, lg, ALU.max, ALU.add), step)
                                v3 = v.scalar_tensor_tensor
                                done(dve, v3(kp[:, 0:P], lg[:, 0:P], -1.0, strict, ALU.mult, ALU.mult), step)
                                done(dve, v.tensor_scalar(kp[:, P:S], lg[:, P:S], -1.0, None, ALU.mult), step)
                                v3(kp[:, S:Wd], lg[:, S:Wd], -1.0, strict, ALU.mult, ALU.mult).then_inc(kept.sem, 1)
                            if 1 <= i <= H:
                                n = i - 1
                                dve.wait_ge(expd.sem, n + 1)
                                done(dve, v.tensor_tensor(wt[:, n % 2, 0:P], wt[:, n % 2, 0:P], strict, ALU.mult), step)
                                v.tensor_tensor(wt[:, n % 2, S:Wd], wt[:, n % 2, S:Wd], strict, ALU.mult).then_inc(masked.sem, 1)
                            if i >= 2:
                                n = i - 2
                                b0 = 64 * (n % 2)
                                dve.wait_ge(mixed.sem, n + 1)
                                v.tensor_copy(y[b0:b0 + 64, n // 2, :], ps[4 + n % 2][b0:b0 + 64, 0:S]).then_inc(out.sem, 1)

                    @block.scalar
                    def _(act):
                        for i in range(H + 1):
                            if i < H:
                                act.wait_ge(prepped.sem, i + 1)
                                z = ab[:, i % 2, :]
                                done(act, a.activation(z, z, ACT.Exp), exped)
                                a.activation(z, z, ACT.Ln, bias=1.0).then_inc(logged.sem, 1)
                            if i >= 1:
                                n = i - 1
                                act.wait_ge(added.sem, n + 1)
                                w = wt[:, n % 2, :]
                                a.activation(w, w, ACT.Exp).then_inc(expd.sem, 1)

        def gla(q, k, vt, lgate, lrT, w_up, par, GLA_B, gain, y, s2):
            v, a = nc.vector, nc.scalar
            with ExitStack() as st:
                bc_ = sb("gla_bcum", [P, 4 * S], st)
                eb = sb("gla_exp", [P, 4 * S], st)
                kd = sb("gla_kdT", [P, 4 * S], st)
                at = hT[:, 0:4, :].rearrange("p c (t s) -> p (c t) s", t=2)
                kt = hT[:, 4:8, :].rearrange("p c (t s) -> p (c t) s", t=2)
                vx = sb("gla_v_pairs", [P, TILES, 4, 2, P], st)
                states = sb("gla_states", [P, 2, 16, P], st)
                flat = "p c s -> p (c s)"
                qf, kf = q[:, :, :].rearrange(flat), k[:, :, :].rearrange(flat)
                mm, step, acted = (Count(nc, f"gla_{n}") for n in ("mm", "step", "acted"))
                with nc.Block() as block:
                    @block.tensor
                    def _(pe):
                        for c in range(4):
                            ins = nc.tensor.matmul(ps[c // 2][:, (c % 2) * S:(c % 2 + 1) * S], w_up[:, c * P:(c + 1) * P],
                                                   lrT[:, :], start=True, stop=True)
                        ins.then_inc(mm.sem, 1)
                        pe.wait_ge(step.sem, 9)
                        for g in range(8):
                            ins = nc.tensor.matmul(ps[2 + g // 4][:, (g % 4) * P:(g % 4 + 1) * P], kf[:, g * P:(g + 1) * P],
                                                   qf[:, g * P:(g + 1) * P], start=True, stop=True)
                        ins.then_inc(mm.sem, 1)
                        for g in range(8):
                            ins = nc.tensor.transpose(ps[4 + g // 4][:, (g % 4) * P:(g % 4 + 1) * P], kd[:, g * P:(g + 1) * P], ident)
                        ins.then_inc(mm.sem, 1)

                    @block.scalar
                    def _(act):
                        act.wait_ge(mm.sem, 1)
                        for c in range(4):
                            done(act, a.activation(bc_[:, c * S:(c + 1) * S], ps[c // 2][:, (c % 2) * S:(c % 2 + 1) * S],
                                                   ACT.Identity, bias=par[:, GLA_B + c:GLA_B + c + 1]), acted)
                        act.wait_ge(step.sem, 2)
                        done(act, a.activation(eb[:, :], eb[:, :], ACT.Exp), acted)
                        done(act, a.activation(eb[:, :], eb[:, :], ACT.Ln, bias=1.0), acted)
                        act.wait_ge(step.sem, 4)
                        done(act, a.activation(eb[:, :], bc_[:, :], ACT.Exp, scale=1.0 / 16), acted)
                        act.wait_ge(step.sem, 5)
                        done(act, a.activation(kd[:, :], kd[:, :], ACT.Exp, scale=1.0 / 16), acted)
                        done(act, a.activation(bc_[:, :], bc_[:, :], ACT.Exp, scale=-1.0 / 16), acted)
                        act.wait_ge(mm.sem, 3)
                        for b in range(2):
                            done(act, a.activation(kt[:, 4 * b:4 * b + 4, :].rearrange("p g d -> p (g d)"), ps[4 + b][:, :],
                                                   ACT.Copy), acted)

                    @block.vector
                    def _(dve):
                        def do(ins):
                            done(dve, ins, step)
                        dve.wait_ge(acted.sem, 4)
                        do(v.scalar_tensor_tensor(eb[:, :], bc_[:, :], -1.0, bc_[:, :], ALU.mult, ALU.min))
                        do(v.tensor_scalar(bc_[:, :], bc_[:, :], 0.0, None, ALU.min))
                        dve.wait_ge(acted.sem, 6)
                        do(v.tensor_tensor(bc_[:, :], bc_[:, :], eb[:, :], ALU.subtract))
                        do(v.tensor_tensor_scan(bc_[:, :], const("restart16"), bc_[:, :], 0.0, ALU.mult, ALU.add))
                        b3 = bc_[:, :].rearrange("p (n s) -> p n s", s=16)
                        do(v.tensor_tensor(kd[:, :].rearrange("p (n s) -> p n s", s=16),
                                           b3[:, :, 15:16].broadcast_to([P, 64, 16]), b3, ALU.subtract))
                        dve.wait_ge(acted.sem, 9)
                        do(v.scalar_tensor_tensor(qf, qf, P ** -0.5, eb[:, :], ALU.mult, ALU.mult))
                        do(v.tensor_tensor(kd[:, :], kd[:, :], kf, ALU.mult))
                        do(v.tensor_tensor(kf, kf, bc_[:, :], ALU.mult))
                        for par_ in range(2):
                            last = v.tensor_scalar(vx[:, :, :, par_, :], vt[:, :, :].rearrange("p t (h d) -> p t h d", h=4),
                                                   const("parity")[:, par_:par_ + 1], None, ALU.mult)
                            do(last)
                        dve.wait_ge(mm.sem, 2)
                        for b in range(2):
                            do(v.tensor_tensor(at[:, 4 * b:4 * b + 4, :], ps[2 + b][:, :].rearrange("p (g s) -> p g s", g=4),
                                               const("causal16").unsqueeze(1).broadcast_to([P, 4, P]), ALU.mult))
                dump("glab", eb[:, :])
                mm, step, acted = (Count(nc, f"gla_scan_{n}") for n in ("mm", "step", "acted"))
                oT = kd[:, :]
                with nc.Block() as block:
                    @block.tensor
                    def _(pe):
                        def updates(h):
                            if h >= 1:
                                pe.wait_ge(step.sem, 16 * h)
                            for pr in range(8):
                                t, b0 = pr // 4, 32 * (pr % 4)
                                ins = nc.tensor.matmul(ps[pr % 4][:, t * S:(t + 1) * S], kt[b0:b0 + 32, 2 * h + t, :],
                                                       vx[b0:b0 + 32, t, h, :, :].rearrange("p a d -> p (a d)"),
                                                       start=True, stop=True, tile_position=(b0, 0))
                            ins.then_inc(mm.sem, 1)

                        def outputs(h):
                            if h >= 2:
                                pe.wait_ge(acted.sem, h - 1)
                            bank = ps[4 + h % 2]
                            for t in range(TILES):
                                nc.tensor.matmul(bank[:, t * P:(t + 1) * P], vt[:, t, h * P:(h + 1) * P], at[:, 2 * h + t, :],
                                                 start=t == 0, stop=False, skip_group_check=True)
                            pe.wait_ge(step.sem, 16 * (h + 1))
                            for n in range(1, 16):
                                ins = nc.tensor.matmul(bank[:, 16 * n:16 * n + 16], states[:, h % 2, n, :],
                                                       q[:, h, 16 * n:16 * n + 16], start=False, stop=n == 15,
                                                       skip_group_check=True)
                            ins.then_inc(mm.sem, 1)

                        for h in range(5):
                            if h < 4:
                                updates(h)
                            if h >= 1:
                                outputs(h - 1)

                    @block.vector
                    def _(dve):
                        def do(ins):
                            done(dve, ins, step)
                        e4 = eb[:, :].rearrange("p (h s) -> p h s", h=4)
                        for h in range(4):
                            if h >= 2:
                                dve.wait_ge(mm.sem, 2 * h - 1)
                            dve.wait_ge(mm.sem, max(2 * h, 1))
                            for n in range(16):
                                pr = n // 2
                                kv = ps[pr % 4][:, (pr // 4) * S + (n % 2) * P:(pr // 4) * S + (n % 2 + 1) * P]
                                if n == 15:
                                    do(v.memset(states[:, h % 2, 0, 0:1], 0.0))
                                elif n == 0:
                                    do(v.tensor_copy(states[:, h % 2, 1, :], kv))
                                else:
                                    do(v.scalar_tensor_tensor(states[:, h % 2, n + 1, :], states[:, h % 2, n, :],
                                                              e4[:, h, 16 * n + 15:16 * n + 16], kv, ALU.mult, ALU.add))

                    @block.scalar
                    def _(act):
                        for h in range(4):
                            act.wait_ge(mm.sem, 2 * h + 3 if h < 3 else 8)
                            a.activation(oT[:, h * S:(h + 1) * S], ps[4 + h % 2][:, 0:S], ACT.Copy).then_inc(acted.sem, 1)
                dump("glaO", oT)
                head_norm("gla_norm", oT, bc_[:, :], eb[:, :], gain, lgate[:, :, :].rearrange(flat),
                          y[:, :, :].rearrange(flat))

        first_sem = nc.alloc_semaphore("layer_sems_from")
        with nc.Fori(0, DEPTH) as l:
            layer(l)
            last_sem = nc.alloc_semaphore("layer_sems_to")
            with nc.Block() as block:
                @block.gpsimd
                def _(pool):
                    pool.sem_clear(range(first_sem.num, last_sem.num))
        if "xl" in dbg:
            dump("xl", x[:, :, :])
            return
        nc.prepend_free_semaphores(list(range(first_sem.num, last_sem.num)))
        second_part()


NAMES = ("x", "c", "ada_w", "ada_b", "norm_mix_g", "norm_ffn_g", "w_in", "na_rpb", "mla_q_norm_g", "mla_kv_norm_g",
         "mla_w_uq", "mla_w_ukv", "gqa_q_norm_g", "gqa_k_norm_g", "w_br_na", "w_br_mla", "w_br_gqa", "w_out",
         "ffn_w_gate_up", "ffn_w_down", "final_norm_g", "w_in_2", "conv_a_w_2", "conv_a_b_2", "rg_w_a_2", "rg_b_a_2",
         "rg_w_x_2", "rg_b_x_2", "rg_lambda_2", "gdn_conv_w_2", "gdn_a_log_2", "gdn_dt_bias_2", "gdn_norm_w_2",
         "gla_w_gate_up_2", "gla_b_gate_2", "gla_norm_w_2", "w_branch_2", "w_out_2", "ln1_g_2", "ln1_b_2",
         "w_router_2", "router_bias_2", "w_gate_2", "w_up_2", "w_down_2", "ln2_g_2", "ln2_b_2")


def kernel(**inputs):
    import concourse.bacc as bacc
    from concourse.bass_utils import run_bass_kernel_spmd

    nc = bacc.Bacc("TRN2", target_bir_lowering=False, num_devices=1)
    arrays = {f"in_{name}": np.ascontiguousarray(inputs[name]) for name in NAMES}
    arrays["in_constants"] = np.ascontiguousarray(np.concatenate(list(constants().values()), axis=1))
    args = {k[3:]: nc.dram_tensor(k, a.shape, mybir.dt.from_np(a.dtype), kind="ExternalInput").ap()
            for k, a in arrays.items()}
    out = nc.dram_tensor("out", (1, S, D), FP, kind="ExternalOutput").ap()
    program(nc, args, out)
    result = run_bass_kernel_spmd(nc, [arrays], core_ids=[0])
    return result.results[0]["out"]
```

```python
import numpy as np
import concourse.bass as bass
from concourse import mybir
from contextlib import ExitStack

P = 128
D = 1024
S = 256
TILES = S // P
KD = D // P
DEPTH = 2
EPS = 1e-6
LN_EPS = 1e-5
GRID_W = 64
NEG = -1e30
FFN = 2816
N_EXPERTS = 16
D_EXPERT = 512
ALPHA = 2 ** 0.25
UNIT = 8 * 256
UNIT_W = 256

FP = mybir.dt.float32
FR = mybir.dt.float32r
ALU = mybir.AluOpType
ACT = mybir.ActivationFunctionType
AX = mybir.AxisListType.X


def constants():
    p = np.arange(P)
    j, i = p[:, None], p[None, :]
    c = {"ident": np.eye(P), "ones": np.ones((P, P))}
    qc, kc = (p % GRID_W)[:, None], np.arange(GRID_W)[None, :]
    start = np.clip(qc - 8, 0, GRID_W - 16)
    seen = (kc >= start) & (kc < start + 16)
    c["na_seen"] = seen
    c["na_neg"] = np.where(seen, 0.0, NEG)
    t = np.arange(S)

    def rotary(pos, half):
        inv = (1.0 / (np.float32(10000.0) ** (np.arange(half, dtype=np.float32) / half))).astype(np.float32)
        a = pos.astype(np.float32)[:, None] * inv[None, :]
        co, si = np.cos(a), np.sin(a)
        return np.stack([co, co], 1), np.stack([-si, si], 1)

    def tiled(a):
        return a.reshape(TILES, P, -1).transpose(1, 0, 2).reshape(P, -1)

    c["mla_cos"], c["mla_sin"] = (tiled(a) for a in rotary(t, 16))
    rows, cols = rotary(t // GRID_W, 16), rotary(t % GRID_W, 16)
    c["ax_cos"] = tiled(np.stack([rows[0], cols[0]], 1))
    c["ax_sin"] = tiled(np.stack([rows[1], cols[1]], 1))
    same64 = j // 64 == i // 64
    c["cum64"] = same64 & (j <= i)
    c["blk64"] = same64
    c["strict64"] = same64 & (j < i)
    for s in (1, 2, 4, 8, 16, 32):
        low = (j // (2 * s) == i // (2 * s)) & (j % (2 * s) >= s) & (i % (2 * s) < s)
        c[f"level{s}"] = low
    c["level1_t"] = c["level1"].T
    c["causal16"] = (j // 16 == i // 16) & (j <= i)
    c["sb_strict"] = j < i
    c["sb_incl"] = j >= i
    c["parity"] = np.stack([(p // 16) % 2 == 0, (p // 16) % 2 == 1], 1)
    c["restart16"] = np.broadcast_to((np.arange(4 * S) % 16 != 0)[None], (P, 4 * S))
    c["rank16"] = np.broadcast_to(np.arange(16, 0, -1)[None], (P, 16))
    c["slot"] = np.broadcast_to(np.arange(P)[None], (P, P))
    c["rank4"] = np.broadcast_to(np.arange(4, 0, -1)[None], (P, 4))
    return {k: np.asarray(v, np.float32) for k, v in c.items()}


class Count:

    def __init__(self, nc, name):
        self.sem = nc.alloc_semaphore(name)
        self.n = 0


def done(eng, ins, s):
    ins.then_inc(s.sem, 1)
    s.n += 1
    eng.wait_ge(s.sem, s.n)


def signal(ins, s):
    ins.then_inc(s.sem, 1)
    s.n += 1


class Ring:

    def __init__(self, nc, name, raw, pair, units, scaled=(), scale=None, terms=None):
        self.nc, self.units, self.raw, self.pair = nc, units, raw, pair
        self.scaled, self.scale, self.terms = scaled, scale, terms
        self.term_step = Count(nc, f"{name}_term_step")
        self.depth, self.pairs = raw.shape[1], pair.shape[1]
        self.landed = [nc.alloc_semaphore(f"{name}_landed{s}") for s in range(self.depth)]
        self.hi_done = nc.alloc_semaphore(f"{name}_hi_done")
        self.lo_done = nc.alloc_semaphore(f"{name}_lo_done")
        self.used = nc.alloc_semaphore(f"{name}_units_used")
        self.value, count = [], [0] * self.depth
        for n, parts in enumerate(units):
            count[n % self.depth] += 16 * len(parts)
            self.value.append(count[n % self.depth])
        self.size = [max(at + k * width for at, k, width, *_ in parts) for parts in units]
        self.issued = self.split_hi = self.split_lo = 0

    def feed(self, sp, end):
        for n in range(self.issued, min(end + self.depth + 1, len(self.units))):
            if n >= self.depth:
                sp.wait_ge(self.lo_done, n - self.depth + 1)
            for at, k, width, c0, c1, src in self.units[n]:
                dst = self.raw[:, n % self.depth, at:at + k * width].rearrange("p (k n) -> p k n", k=k)[:, :, c0:c1]
                sp.dma_start(dst, src).then_inc(self.landed[n % self.depth], 16)
            self.issued = n + 1

    def hi(self, act, through):
        for n in range(self.split_hi, min(through + 1, len(self.units))):
            act.wait_ge(self.landed[n % self.depth], self.value[n])
            if n >= self.pairs:
                act.wait_ge(self.used, n - self.pairs + 1)
            if n in self.scaled:
                for k in range(5, KD):
                    ins = self.nc.scalar.activation(self.terms[:, n % 2, k - 4, :], self.row(n, k), ACT.Copy,
                                                    scale=self.scale[:, k:k + 1])
                ins.then_inc(self.hi_done, 1)
                self.split_hi = n + 1
                continue
            self.nc.scalar.activation(self.pair[:, n % self.pairs, 0, 0:self.size[n]], self.raw[:, n % self.depth, 0:self.size[n]],
                                      ACT.Copy).then_inc(self.hi_done, 1)
            self.split_hi = n + 1

    def lo(self, dve, through):
        for n in range(self.split_lo, min(through + 1, len(self.units))):
            if n in self.scaled:
                dve.wait_ge(self.landed[n % self.depth], self.value[n])
                if n >= 2:
                    dve.wait_ge(self.used, n - 1)
                acc = self.terms[:, n % 2, 0, :]
                done(dve, self.nc.vector.tensor_scalar(acc, self.row(n, 0), self.scale[:, 0:1], None, ALU.mult),
                     self.term_step)
                for k in range(1, 5):
                    if k == 4:
                        dve.wait_ge(self.hi_done, n + 1)
                    ins = self.nc.vector.scalar_tensor_tensor(acc, self.row(n, k), self.scale[:, k:k + 1], acc,
                                                              ALU.mult, ALU.add)
                    if k < 4:
                        done(dve, ins, self.term_step)
                ins.then_inc(self.lo_done, 1)
                self.split_lo = n + 1
                continue
            dve.wait_ge(self.hi_done, n + 1)
            self.nc.vector.tensor_tensor(self.pair[:, n % self.pairs, 1, 0:self.size[n]], self.raw[:, n % self.depth, 0:self.size[n]],
                                         self.pair[:, n % self.pairs, 0, 0:self.size[n]].bitcast(FP),
                                         ALU.subtract).then_inc(self.lo_done, 1)
            self.split_lo = n + 1

    def row(self, n, k):
        return self.raw[:, n % self.depth, k * UNIT_W:(k + 1) * UNIT_W]

    def arrived(self, pe, n):
        pe.wait_ge(self.lo_done, n + 1)

    def view(self, n, part, k, width, at=0):
        return self.pair[:, n % self.pairs, part, at:at + k * width].rearrange("p (k n) -> p k n", k=k)


class Job:

    def __init__(self, unit, kind, idx, width, act, out, last=None, k=KD, lhs=None, at=0, unit_width=None, k0=0,
                 col0=0):
        self.unit, self.kind, self.idx, self.width, self.act, self.out = unit, kind, idx, width, act, out
        self.last = idx == 1 if last is None else last
        self.k, self.lhs, self.at, self.unit_width, self.k0, self.col0 = k, lhs, at, unit_width or UNIT_W, k0, col0


def program(nc, A, OUT):
    es = ExitStack()
    with es:
        def sb(name, shape, stack=es, dtype=FP):
            return stack.enter_context(nc.sbuf_tensor(name, shape, dtype))

        ps = [es.enter_context(nc.psum_tensor(f"bank{b}", [P, 512], FP)) for b in range(8)]
        layout, width = {}, 0
        for name, table in constants().items():
            layout[name] = (width, table.shape[1])
            width += table.shape[1]
        cst = sb("cst", [P, width])

        def const(name):
            at, n = layout[name]
            return cst[:, at:at + n]

        ident, ones = const("ident"), const("ones")
        x = sb("x", [P, TILES, D])
        hT = sb("hT", [P, KD, S])
        hP = sb("hT_pair", [P, 2, KD, S], dtype=FR)
        rstat = sb("rstat", [P, 8])
        half_neg = sb("half_neg", [P, 64])
        setup_loaded = nc.alloc_semaphore("setup_loaded")
        half_set = nc.alloc_semaphore("half_set")
        strips = nc.dram_tensor("na_bias_strips", [DEPTH, P, TILES * 4 * 256], FP, kind="Internal").ap()
        strips_written = nc.alloc_semaphore("strips_written")

        with nc.Block() as block:
            @block.sync
            def _(sp):
                sp.dma_start(cst[:, :], A["constants"]).then_inc(setup_loaded, 16)
                sp.dma_start(x[:, :, :], A["x"].rearrange("o (t p) d -> p (o t) d", p=P)).then_inc(setup_loaded, 16)
                sp.wait_ge(setup_loaded, 32)

            @block.scalar
            def _(act):
                for l in range(DEPTH):
                    for qr in range(4):
                        for h in range(4):
                            src = bass.AP(A["na_rpb"].tensor, (l * 4 + h) * 465 + (7 - qr) * 31 + 15,
                                          [[31, 4], [-1, 64], [1, 64]])
                            at = ((qr // 2) * 4 + h) * 256
                            dst = strips[l, 64 * (qr % 2):64 * (qr % 2) + 64, at:at + 256]
                            act.dma_start(dst.rearrange("p (r c) -> r p c", r=4), src).then_inc(strips_written, 16)

            @block.gpsimd
            def _(pool):
                pool.memset(half_neg[:, :], -0.5).then_inc(half_set, 1)

        def rsqrt_on_pool(pool, out, ms, n, s, mul, eps):
            done(pool, pool.tensor_scalar(ms, ms, mul, eps, ALU.mult, ALU.add), s)
            done(pool, pool.tensor_tensor(out, ms, half_neg[:, 0:n], ALU.pow), s)

        def transpose_pe(pe, src, chunks, ready, s, bank0=0):
            for k in range(chunks):
                for t in range(TILES):
                    if ready is not None and k == 0:
                        pe.wait_ge(ready[0], ready[1][t])
                    ins = nc.tensor.transpose(ps[bank0 + k // 2][:, (k % 2) * S + t * P:(k % 2) * S + (t + 1) * P],
                                              src[:, t, k * P:(k + 1) * P], ident)
                if k % 2:
                    signal(ins, s)

        def rms_norm_to_fm(tag, scale=None, bias=None, row_gain=None, keep=False):
            with ExitStack() as st:
                junk = sb(f"{tag}_junk", [P, TILES, D], st)
                xn = sb(f"{tag}_xn", [P, TILES, D], st)
                squared, rooted, normed, turned, act_out, dve_out = (Count(nc, f"{tag}_{n}") for n in
                    ("squared", "rooted", "normed", "turned", "act_out", "dve_out"))
                dst = x if keep else xn
                with nc.Block() as block:
                    @block.scalar
                    def _(act):
                        for t in range(TILES):
                            done(act, nc.scalar.activation(junk[:, t, :], x[:, t, :], ACT.Square,
                                                           accum_out=rstat[:, t:t + 1]), squared)
                        for k in (0, 1, 4, 5):
                            act.wait_ge(turned.sem, k // 2 + 1)
                            src = ps[k // 2][:, (k % 2) * S:(k % 2 + 1) * S]
                            if scale is None:
                                ins = nc.scalar.activation(hT[:, k, :], src, ACT.Copy)
                            else:
                                ins = nc.scalar.activation(hT[:, k, :], src, ACT.Identity,
                                                           bias=bias[:, k:k + 1], scale=scale[:, k:k + 1])
                            signal(ins, act_out)

                    @block.gpsimd
                    def _(pool):
                        pool.wait_ge(squared.sem, 2)
                        rsqrt_on_pool(pool, rstat[:, 4:6], rstat[:, 0:2], 2, rooted, 1.0 / D, EPS)

                    @block.vector
                    def _(dve):
                        dve.wait_ge(rooted.sem, 2)
                        for t in range(TILES):
                            r = rstat[:, 4 + t:5 + t]
                            if row_gain is None:
                                ins = nc.vector.tensor_scalar(dst[:, t, :], x[:, t, :], r, None, ALU.mult)
                            else:
                                ins = nc.vector.scalar_tensor_tensor(dst[:, t, :], x[:, t, :], r, row_gain,
                                                                     ALU.mult, ALU.mult)
                            signal(ins, normed)
                        for k in (2, 3, 6, 7):
                            dve.wait_ge(turned.sem, k // 2 + 1)
                            src = ps[k // 2][:, (k % 2) * S:(k % 2 + 1) * S]
                            if scale is None:
                                ins = nc.vector.tensor_copy(hT[:, k, :], src)
                            else:
                                ins = nc.vector.tensor_scalar(hT[:, k, :], src, scale[:, k:k + 1],
                                                              bias[:, k:k + 1], ALU.mult, ALU.add)
                            signal(ins, dve_out)

                    @block.tensor
                    def _(pe):
                        transpose_pe(pe, dst, KD, (normed.sem, (1, 2)), turned)

        def products(ring, job, out):
            h = hP if job.lhs is None else job.lhs
            for c in range(job.k):
                for tp, wp in ((0, 0), (0, 1), (1, 0)):
                    tokens = h[:, tp, job.k0 + c, :]
                    weights = ring.view(job.unit, wp, job.k, job.unit_width, job.at)[:, c, :]
                    if job.kind == "tok":
                        lhs, rhs = tokens[:, job.idx * P:(job.idx + 1) * P], weights[:, job.col0:job.col0 + job.width]
                    else:
                        lhs, rhs = weights[:, job.idx * P:(job.idx + 1) * P], tokens
                    ins = nc.tensor.matmul(out, lhs, rhs, start=c == 0 and tp + wp == 0,
                                           stop=c == job.k - 1 and tp == 1)
            return ins

        def project(tag, ring, jobs, banks=8, extra=None, pace=4):
            extra = extra or {}
            summed, act_out, dve_out = (Count(nc, f"{tag}_{n}") for n in ("summed", "act_out", "dve_out"))
            n_summed, n_out = 0, {True: 0, False: 0}
            for g, job in enumerate(jobs):
                if job.last:
                    job.ready = (ring.used, job.unit + 1)
                else:
                    n_summed += 1
                    job.ready = (summed.sem, n_summed)
                n_out[job.act] += 1
                job.left = ((act_out if job.act else dve_out).sem, n_out[job.act])

            def shape(job, g):
                return ps[g % banks][:, 0:job.width if job.kind == "tok" else S]

            def drain(eng, act, s, between=None):
                for g, job in enumerate(jobs):
                    if g == 0 or jobs[g - 1].unit != job.unit:
                        (ring.hi if act else ring.lo)(eng, job.unit + 1)
                        for _ in range(pace if between is not None else 0):
                            next(between, None)
                    if job.act == act:
                        eng.wait_ge(*job.ready)
                        (signal if act else lambda ins, s: done(eng, ins, s))(job.out(shape(job, g)), s)
                for _ in between or ():
                    pass

            with nc.Block() as block:
                @block.sync
                def _(sp):
                    ring.feed(sp, jobs[-1].unit + 1)
                    if "sync" in extra:
                        extra["sync"](sp)

                @block.tensor
                def _(pe):
                    for g, job in enumerate(jobs):
                        if g == 0 or jobs[g - 1].unit != job.unit:
                            ring.arrived(pe, job.unit)
                        if g >= banks:
                            pe.wait_ge(*jobs[g - banks].left)
                        ins = products(ring, job, shape(job, g))
                        ins.then_inc(ring.used if job.last else summed.sem, 1)
                    if "tensor" in extra:
                        extra["tensor"](pe)

                @block.scalar
                def _(act):
                    drain(act, True, act_out)
                    if "scalar" in extra:
                        extra["scalar"](act)

                @block.vector
                def _(dve):
                    drain(dve, False, dve_out, extra["vector"](dve) if "vector" in extra else None)

                if "gpsimd" in extra:
                    @block.gpsimd
                    def _(pool):
                        extra["gpsimd"](pool)

        class Beside:

            def __init__(self, tag, ring, jobs, banks):
                self.ring, self.jobs, self.banks = ring, jobs, banks
                self.out_sem = {act: nc.alloc_semaphore(f"{tag}_{'act' if act else 'dve'}_out") for act in (True, False)}
                self.summed = nc.alloc_semaphore(f"{tag}_summed")
                self.issued, self.gone = 0, {True: 0, False: 0}
                n_summed, n_out = 0, {True: 0, False: 0}
                for job in jobs:
                    if not job.last:
                        n_summed += 1
                    job.ready = (ring.used, job.unit + 1) if job.last else (self.summed, n_summed)
                    n_out[job.act] += 1
                    job.left = (self.out_sem[job.act], n_out[job.act])

            def bank(self, g):
                job = self.jobs[g]
                return ps[self.banks[g % len(self.banks)]][:, 0:job.width if job.kind == "tok" else S]

            def multiply(self, pe, n):
                for g in range(self.issued, min(self.issued + n, len(self.jobs))):
                    job = self.jobs[g]
                    if g == 0 or self.jobs[g - 1].unit != job.unit:
                        self.ring.arrived(pe, job.unit)
                    if g >= len(self.banks):
                        pe.wait_ge(*self.jobs[g - len(self.banks)].left)
                    products(self.ring, job, self.bank(g)).then_inc(self.ring.used if job.last else self.summed, 1)
                    self.issued = g + 1

            def leave(self, eng, act, upto):
                for g in range(self.gone[act], min(upto, len(self.jobs))):
                    job = self.jobs[g]
                    if job.act == act:
                        eng.wait_ge(*job.ready)
                        job.out(self.bank(g)).then_inc(self.out_sem[act], 1)
                    self.gone[act] = g + 1

        def copy_out(act, dst):
            return lambda src: nc.scalar.activation(dst, src, ACT.Copy) if act else nc.vector.tensor_copy(dst, src)

        def split_fm(tag, src, pair, chunks):
            hi_done = nc.alloc_semaphore(f"{tag}_hi")
            n = chunks // 4
            with nc.Block() as block:
                @block.scalar
                def _(act):
                    for b in range(4):
                        nc.scalar.activation(pair[:, 0, n * b:n * b + n, :], src[:, n * b:n * b + n, :],
                                             ACT.Copy).then_inc(hi_done, 1)

                @block.vector
                def _(dve):
                    for b in range(4):
                        dve.wait_ge(hi_done, b + 1)
                        nc.vector.tensor_tensor(pair[:, 1, n * b:n * b + n, :], src[:, n * b:n * b + n, :],
                                                pair[:, 0, n * b:n * b + n, :].bitcast(FP),
                                                ALU.subtract)

        def gated_hidden(tag, ring, first, blocks, gain):
            def gu(n, up):
                return first + (up if n == 0 else 3 * n - 1 + up)

            def dn(n):
                return first + (3 * n + 4 if n < blocks - 1 else 3 * n + 2)

            def flat(ap):
                return ap.rearrange("p a b -> p (a b)")

            with ExitStack() as st:
                sig = sb(f"{tag}_sig", [P, TILES, 256], st)
                a = sb(f"{tag}_a", [P, TILES, 256], st)
                aT = sb(f"{tag}_aT", [P, 2, 2, S], st, FR)
                gated, multiplied, acted, turned, hi_out, lo_out, chain = (Count(nc, f"{tag}_{n}") for n in
                    ("gated", "multiplied", "acted", "turned", "hi_out", "lo_out", "dve_step"))
                with nc.Block() as block:
                    @block.sync
                    def _(sp):
                        ring.feed(sp, len(ring.units))

                    @block.tensor
                    def _(pe):
                        def hidden(n, up):
                            ring.arrived(pe, gu(n, up))
                            if n >= 1:
                                pe.wait_ge(*((acted.sem, n) if up else (multiplied.sem, n)))
                            for t in range(TILES):
                                ins = products(ring, Job(gu(n, up), "tok", t, 256, True, None),
                                               ps[up][:, t * 256:(t + 1) * 256])
                            ins.then_inc(ring.used, 1)

                        def turn(n):
                            pe.wait_ge(acted.sem, n + 1)
                            if n >= 2:
                                pe.wait_ge(lo_out.sem, n - 1)
                            for t in range(TILES):
                                for c in range(2):
                                    ins = nc.tensor.transpose(ps[2 + n % 2][:, c * S + t * P:c * S + (t + 1) * P],
                                                              a[:, t, c * P:(c + 1) * P], ident)
                            ins.then_inc(turned.sem, 1)

                        def down(n):
                            pe.wait_ge(lo_out.sem, n + 1)
                            ring.arrived(pe, dn(n))
                            for t in range(TILES):
                                for nb in range(2):
                                    for c in range(2):
                                        for tp, wp in ((0, 0), (0, 1), (1, 0)):
                                            w = ring.view(dn(n), wp, 2, D)
                                            ins = nc.tensor.matmul(
                                                ps[4 + 2 * t + nb][:, :], aT[:, tp, c, t * P:(t + 1) * P],
                                                w[:, c, nb * 512:(nb + 1) * 512],
                                                start=n == 0 and c + tp + wp == 0,
                                                stop=n == blocks - 1 and c == 1 and tp == 1)
                            ins.then_inc(ring.used, 1)

                        for n in range(blocks):
                            hidden(n, 0)
                            hidden(n, 1)
                            if n >= 1:
                                down(n - 1)
                            turn(n)
                        down(blocks - 1)

                    @block.scalar
                    def _(act):
                        for n in range(blocks):
                            ring.hi(act, dn(n - 1) if n else gu(0, 1))
                            act.wait_ge(ring.used, gu(n, 0) + 1)
                            if n >= 1:
                                act.wait_ge(acted.sem, n)
                            nc.scalar.activation(flat(sig[:, :, :]), ps[0][:, :], ACT.Sigmoid).then_inc(gated.sem, 1)
                            if n + 1 < blocks:
                                ring.hi(act, gu(n + 1, 1))
                            else:
                                ring.hi(act, dn(n))
                            act.wait_ge(turned.sem, n + 1)
                            if n >= 1:
                                act.wait_ge(ring.used, dn(n - 1) + 1)
                            nc.scalar.activation(flat(aT[:, 0, :, :]), ps[2 + n % 2][:, :],
                                                 ACT.Copy).then_inc(hi_out.sem, 1)

                    @block.vector
                    def _(dve):
                        for n in range(blocks):
                            ring.lo(dve, dn(n - 1) if n else gu(0, 1))
                            dve.wait_ge(gated.sem, n + 1)
                            g = sig[:, :, :]
                            nc.vector.tensor_tensor(flat(g), ps[0][:, :], flat(g), ALU.mult).then_inc(multiplied.sem, 1)
                            dve.wait_ge(multiplied.sem, n + 1)
                            dve.wait_ge(ring.used, gu(n, 1) + 1)
                            if n >= 1:
                                dve.wait_ge(turned.sem, n)
                            up = ps[1][:, :].rearrange("p (t s) -> p t s", t=TILES)
                            if gain(n, 0) is None:
                                nc.vector.tensor_tensor(a[:, :, :], up, g, ALU.mult).then_inc(acted.sem, 1)
                            else:
                                for t in range(TILES):
                                    ins = nc.vector.scalar_tensor_tensor(a[:, t, :], up[:, t, :], gain(n, t), g[:, t, :],
                                                                         ALU.mult, ALU.mult)
                                    if t == 0:
                                        done(dve, ins, chain)
                                ins.then_inc(acted.sem, 1)
                            if n + 1 < blocks:
                                ring.lo(dve, gu(n + 1, 1))
                            else:
                                ring.lo(dve, dn(n))
                            dve.wait_ge(hi_out.sem, n + 1)
                            nc.vector.tensor_tensor(flat(aT[:, 1, :, :]), ps[2 + n % 2][:, :],
                                                    flat(aT[:, 0, :, :]).bitcast(FP), ALU.subtract).then_inc(lo_out.sem, 1)

        def hidden_units(blocks, gate, up, down):
            units = []
            for n in range(blocks):
                units += [[(0, 8, 256, 0, 256, gate(n))], [(0, 8, 256, 0, 256, up(n))]]
                if n:
                    units.append([(0, 2, D, 0, D, down(n - 1))])
            units.append([(0, 2, D, 0, D, down(blocks - 1))])
            return units

        def add_gated(tag, gain):
            with ExitStack() as st:
                tmp = sb(f"{tag}_tmp", [P, 4, 512], st)
                chain = Count(nc, f"{tag}_step")
                with nc.Block() as block:
                    @block.vector
                    def _(dve):
                        for q in range(4):
                            t, cut = q // 2, slice((q % 2) * 512, (q % 2) * 512 + 512)
                            done(dve, nc.vector.tensor_tensor(tmp[:, q, :], ps[4 + q][:, :], gain[:, cut], ALU.mult), chain)
                            done(dve, nc.vector.tensor_tensor(x[:, t, cut], x[:, t, cut], tmp[:, q, :], ALU.add), chain)

        def attend(tag, heads, oT, ring, ada_first, ada_out, after):
            with ExitStack() as st:
                prob = sb(f"{tag}_prob", [P, 2, TILES, S], st)
                score = sb(f"{tag}_score", [P, 2, TILES, S], st)
                probT = sb(f"{tag}_probT", [P, 2, TILES, S], st)
                stat = sb(f"{tag}_stat", [P, 2, 4, TILES], st)
                scored, maxed, expd, normed, turned, copied, mixed, stored_o, chain, mod_out = (
                    Count(nc, f"{tag}_{n}") for n in ("scored", "maxed", "expd", "normed", "turned", "copied",
                                                      "mixed", "out", "step", "mod_out"))
                N = len(heads)
                with nc.Block() as block:
                    @block.sync
                    def _(sp):
                        ring.feed(sp, ada_first + N)

                    @block.tensor
                    def _(pe):
                        for i in range(N + 2):
                            if i < N:
                                qT, kT, v, scale, bias = heads[i]
                                if i >= 2:
                                    pe.wait_ge(expd.sem, 2 * (i - 1))
                                    pe.wait_ge(maxed.sem, i - 1)
                                for t in range(TILES):
                                    ins = nc.tensor.matmul(ps[i % 2][:, t * S:(t + 1) * S], qT[:, t * P:(t + 1) * P],
                                                           kT, start=True, stop=True)
                                ins.then_inc(scored.sem, 1)
                            if i >= 2:
                                n = i - 2
                                v = heads[n][2]
                                pe.wait_ge(copied.sem, n + 1)
                                if n >= 2:
                                    pe.wait_ge(stored_o.sem, n - 1)
                                base = 64 * (n % 2)
                                for kt in range(TILES):
                                    ins = nc.tensor.matmul(ps[4 + n % 2][base:base + 64, 0:S], v(kt),
                                                           probT[:, n % 2, kt, :], start=kt == 0, stop=kt == 1)
                                ins.then_inc(mixed.sem, 1)
                            if i < N:
                                if i >= 2:
                                    pe.wait_ge(mod_out.sem, i - 1)
                                modulation(pe, ring, ada_first + i, ps[6 + i % 2][:, 0:UNIT_W])
                            if 1 <= i <= N:
                                n = i - 1
                                pe.wait_ge(normed.sem, n + 1)
                                if n >= 2:
                                    pe.wait_ge(copied.sem, n - 1)
                                for t in range(TILES):
                                    for kt in range(TILES):
                                        ins = nc.tensor.transpose(ps[2 + n % 2][:, kt * S + t * P:kt * S + (t + 1) * P],
                                                                  prob[:, n % 2, t, kt * P:(kt + 1) * P], ident)
                                ins.then_inc(turned.sem, 1)

                    @block.vector
                    def _(dve):
                        for i in range(N + 2):
                            if i < N:
                                scale, bias = heads[i][3:5]
                                dve.wait_ge(scored.sem, i + 1)
                                if i >= 2:
                                    dve.wait_ge(normed.sem, i - 1)
                                src = ps[i % 2][:, :].rearrange("p (t s) -> p t s", t=TILES)
                                if bias is not None:
                                    dst = score[:, i % 2, :, :]
                                    if i >= 2:
                                        dve.wait_ge(expd.sem, 2 * (i - 1))
                                    done(dve, nc.vector.scalar_tensor_tensor(dst, src, scale, bias, ALU.mult, ALU.add), chain)
                                    src = dst
                                done(dve, nc.vector.tensor_reduce(stat[:, i % 2, 1, :], src, AX, ALU.max), chain)
                                nc.vector.tensor_scalar(stat[:, i % 2, 0, :], stat[:, i % 2, 1, :],
                                                        -1.0 if bias is not None else -scale, None,
                                                        ALU.mult).then_inc(maxed.sem, 1)
                            if 1 <= i <= N:
                                n = i - 1
                                dve.wait_ge(expd.sem, 2 * n + 2)
                                done(dve, nc.vector.reciprocal(stat[:, n % 2, 3, :], stat[:, n % 2, 2, :]), chain)
                                nc.vector.tensor_tensor(
                                    prob[:, n % 2, :, :], prob[:, n % 2, :, :],
                                    stat[:, n % 2, 3, :].unsqueeze(2).broadcast_to([P, TILES, S]),
                                    ALU.mult).then_inc(normed.sem, 1)
                            if i < N:
                                ring.lo(dve, ada_first + i + 1)
                            if 1 <= i <= N:
                                n = i - 1
                                dve.wait_ge(ring.used, ada_first + n + 1)
                                done(dve, ada_out(dve, n, ps[6 + n % 2][:, 0:UNIT_W]), mod_out)
                        after(dve)

                    @block.scalar
                    def _(act):
                        for i in range(N + 2):
                            if i < N:
                                ring.hi(act, ada_first + i + 1)
                                scale, bias = heads[i][3:5]
                                act.wait_ge(maxed.sem, i + 1)
                                if i >= 2:
                                    act.wait_ge(turned.sem, i - 1)
                                for t in range(TILES):
                                    src = ps[i % 2][:, t * S:(t + 1) * S] if bias is None else score[:, i % 2, t, :]
                                    nc.scalar.activation(prob[:, i % 2, t, :], src, ACT.Exp,
                                                         bias=stat[:, i % 2, 0, t:t + 1],
                                                         scale=scale if bias is None else 1.0,
                                                         accum_out=stat[:, i % 2, 2, t:t + 1]).then_inc(expd.sem, 1)
                            if i >= 2:
                                n = i - 2
                                base = 64 * (n % 2)
                                act.wait_ge(mixed.sem, n + 1)
                                nc.scalar.activation(oT[base:base + 64, n // 2, :], ps[4 + n % 2][base:base + 64, 0:S],
                                                     ACT.Copy).then_inc(stored_o.sem, 1)
                            if 1 <= i <= N:
                                n = i - 1
                                act.wait_ge(turned.sem, n + 1)
                                if n >= 2:
                                    act.wait_ge(mixed.sem, n - 1)
                                nc.scalar.activation(probT[:, n % 2, :, :].rearrange("p k s -> p (k s)"),
                                                     ps[2 + n % 2][:, :], ACT.Copy).then_inc(copied.sem, 1)

        def modulation(pe, ring, unit, out):
            ring.arrived(pe, unit)
            for i in range(4):
                ins = nc.tensor.matmul(out, ones, ring.terms[:, unit % 2, i, :], start=i == 0, stop=i == 3)
            ins.then_inc(ring.used, 1)

        def to_columns(dve, dst, src, junk, s):
            j = junk.rearrange("p (b n) -> p b n", b=2)
            done(dve, nc.vector.tensor_tensor(j, src.rearrange("p (b n) -> p b n", b=2),
                                              ident.unsqueeze(1).broadcast_to([P, 2, P]), ALU.mult), s)
            return nc.vector.tensor_reduce(dst, j, AX, ALU.add)

        def rotate(dve, s, out, src, cos, sin, tmp, heads, parts):
            w = parts * 32
            bc = [P, TILES, heads, w]

            def table(c):
                return c.rearrange("p (t w) -> p t w", t=TILES).unsqueeze(2).broadcast_to(bc)

            for t in range(TILES):
                for half in range(2):
                    pick = "p h (a f w) -> p h a f w"
                    got = src[:, t, :, :].rearrange(pick, a=parts, f=2)[:, :, :, 1 - half, :]
                    put = tmp[:, t, :, :].rearrange(pick, a=parts, f=2)[:, :, :, half, :]
                    by = sin[:, t * w:(t + 1) * w].unsqueeze(1).broadcast_to([P, heads, w]) \
                        .rearrange(pick, a=parts, f=2)[:, :, :, half, :]
                    signal(nc.vector.tensor_tensor(put, got, by, ALU.mult), s)
            dve.wait_ge(s.sem, s.n)
            done(dve, nc.vector.tensor_tensor(out, src, table(cos), ALU.mult), s)
            done(dve, nc.vector.tensor_tensor(out, out, tmp, ALU.add), s)

        def layer(l):
            def cols(name, c0, c1):
                return A[name][bass.ds(l, 1), :, c0:c1].rearrange("o (k p) n -> p (o k) n", p=P)

            def rows(name, r0, r1):
                return A[name][bass.ds(l, 1), r0:r1, :].rearrange("o (k p) n -> p (o k) n", p=P)

            def ada(u):
                return [(0, 8, 256, 0, 256, cols("ada_w", 256 * u, 256 * u + 256))]

            units = [ada(u) for u in range(8)]
            PROJ = len(units)
            for c0 in range(0, 1952, 256):
                units.append([(0, 8, 256, 0, min(256, 1952 - c0), cols("w_in", c0, min(c0 + 256, 1952)))])
            GATES = len(units)
            for b in range(12):
                units.append([(0, 8, 256, 0, 256, cols("w_in", 1952 + 256 * b, 2208 + 256 * b))])
            ADA2 = len(units)
            units += [ada(u) for u in range(8, 24)]
            BRANCH = len(units)
            for nb in range(4):
                n0, n1 = 256 * nb, 256 * nb + 256
                units.append([(0, 2, 256, 0, 256, cols("w_br_na", n0, n1)),
                              (512, 2, 256, 0, 256, cols("w_br_mla", n0, n1)),
                              (1024, 4, 256, 0, 256, cols("w_br_gqa", n0, n1))])
            MERGED = len(units)
            for nb in range(4):
                units.append([(0, 8, 256, 0, 256, cols("w_out", 256 * nb, 256 * nb + 256))])
            HIDDEN = len(units)
            n_hidden = FFN // 256
            units += hidden_units(n_hidden, lambda n: cols("ffn_w_gate_up", 256 * n, 256 * n + 256),
                                  lambda n: cols("ffn_w_gate_up", FFN + 256 * n, FFN + 256 * n + 256),
                                  lambda n: rows("ffn_w_down", 256 * n, 256 * n + 256))
            with ExitStack() as st:
                silu_c = sb("silu_c", [P, KD], st)
                ring = Ring(nc, "layer", sb("layer_raw", [P, 3, UNIT], st), sb("layer_split", [P, 2, 2, UNIT], st, FR), units,
                            scaled=(*range(8), *range(ADA2, ADA2 + 16)), scale=silu_c,
                            terms=sb("layer_terms", [P, 2, 4, UNIT_W], st))
                col = sb("columns", [P, 75], st)
                mod = sb("mod", [P, 48], st)
                Gm = sb("gain_mix", [P, 8], st)
                Gf = sb("gain_ffn", [P, 8], st)
                gate_rows = sb("gate_rows", [P, 2, D], st)
                small = nc.alloc_semaphore("small_loaded")
                rows_loaded = nc.alloc_semaphore("gate_rows_loaded")
                turned, copied, silud, modded, mod_out = (Count(nc, f"mod_{n}") for n in
                    ("turned", "copied", "silud", "modded", "out"))
                diag = sb("diag", [P, UNIT_W], st)

                squared, rooted, normed, x_turned, scaled, act_h = (Count(nc, f"mix_{n}") for n in
                    ("squared", "rooted", "normed", "turned", "scaled", "act_h"))
                with ExitStack() as s1:
                    junk = sb("mix_junk", [P, TILES, D], s1)
                    xn = sb("mix_xn", [P, TILES, D], s1)
                    raw = sb("raw_rows", [P, P], s1)
                    sg = sb("sigmoid_c", [P, 8], s1)
                    with nc.Block() as block:
                        @block.sync
                        def _(sp):
                            def row_block(name, r, n):
                                src = A[name] if name == "c" else A[name][bass.ds(l, 1), :]
                                sp.dma_start(raw[r:r + n, :], src.rearrange("o (r p) -> (o r) p", p=P)).then_inc(small, 16)

                            row_block("ada_b", 0, 48)
                            row_block("norm_mix_g", 48, 8)
                            row_block("norm_ffn_g", 56, 8)
                            row_block("mla_q_norm_g", 64, 2)
                            row_block("mla_kv_norm_g", 66, 1)
                            row_block("c", 67, 8)
                            for i, at in enumerate((2 * D, 5 * D)):
                                sp.dma_start(gate_rows[:, i, :], A["ada_b"][bass.ds(l, 1), at:at + D].broadcast_to([P, D])) \
                                    .then_inc(rows_loaded, 16)
                            ring.feed(sp, PROJ)

                        @block.tensor
                        def _(pe):
                            pe.wait_ge(small, 16 * 6)
                            nc.tensor.transpose(ps[0][:, 0:75], raw[0:75, :], ident[0:75, 0:75]).then_inc(turned.sem, 1)
                            pe.wait_ge(silud.sem, 2)
                            for u in range(8):
                                if u == 1:
                                    transpose_pe(pe, xn, KD, (normed.sem, (1, 2)), x_turned, bank0=4)
                                if u >= 2:
                                    pe.wait_ge(mod_out.sem, u - 1)
                                modulation(pe, ring, u, ps[1 + u % 2][:, 0:UNIT_W])

                        @block.scalar
                        def _(act):
                            for t in range(TILES):
                                done(act, nc.scalar.activation(junk[:, t, :], x[:, t, :], ACT.Square,
                                                               accum_out=rstat[:, t:t + 1]), squared)
                            act.wait_ge(turned.sem, 1)
                            done(act, nc.scalar.activation(col[:, :], ps[0][:, 0:75], ACT.Copy), copied)
                            done(act, nc.scalar.activation(sg[:, :], col[:, 67:75], ACT.Sigmoid), silud)
                            act.wait_ge(silud.sem, 2)
                            for u in range(8):
                                ring.hi(act, u + 1)
                            act.wait_ge(x_turned.sem, 4)
                            act.wait_ge(scaled.sem, 1)
                            for k in (0, 1, 4, 5):
                                act_ins = nc.scalar.activation(hT[:, k, :], ps[4 + k // 2][:, (k % 2) * S:(k % 2 + 1) * S],
                                                               ACT.Identity, bias=mod[:, k:k + 1], scale=Gm[:, k:k + 1])
                            signal(act_ins, act_h)

                        @block.gpsimd
                        def _(pool):
                            pool.wait_ge(squared.sem, 2)
                            rsqrt_on_pool(pool, rstat[:, 4:6], rstat[:, 0:2], 2, rooted, 1.0 / D, EPS)

                        @block.vector
                        def _(dve):
                            silud.n = 1
                            dve.wait_ge(silud.sem, 1)
                            done(dve, nc.vector.tensor_tensor(silu_c[:, :], sg[:, :], col[:, 67:75], ALU.mult), silud)
                            done(dve, nc.vector.memset(mod[:, :], 0.0), silud)
                            for u in range(8):
                                if u == 0:
                                    ring.lo(dve, 0)
                                    dve.wait_ge(rooted.sem, 2)
                                    for t in range(TILES):
                                        signal(nc.vector.tensor_scalar(xn[:, t, :], x[:, t, :], rstat[:, 4 + t:5 + t], None,
                                                                       ALU.mult), normed)
                                ring.lo(dve, u + 1)
                                dve.wait_ge(ring.used, u + 1)
                                done(dve, to_columns(dve, mod[:, 2 * u:2 * u + 2], ps[1 + u % 2][:, 0:UNIT_W], diag[:, :],
                                                     modded), mod_out)
                            done(dve, nc.vector.tensor_tensor(mod[:, 0:16], mod[:, 0:16], col[:, 0:16], ALU.add), modded)
                            done(dve, nc.vector.scalar_tensor_tensor(Gm[:, :], mod[:, 8:16], 1.0, col[:, 48:56],
                                                                     ALU.add, ALU.mult), scaled)
                            dve.wait_ge(x_turned.sem, 4)
                            for k in (2, 3, 6, 7):
                                nc.vector.tensor_scalar(hT[:, k, :], ps[4 + k // 2][:, (k % 2) * S:(k % 2 + 1) * S],
                                                        Gm[:, k:k + 1], mod[:, k:k + 1], ALU.mult, ALU.add)

                def ada_out(dve, n, src):
                    if n // 4 in (0, 3):
                        if n == 0:
                            dve.wait_ge(rows_loaded, 32)
                        dst = gate_rows[:, n // 12, 256 * (n % 4):256 * (n % 4) + 256]
                        return nc.vector.tensor_tensor(dst, src, dst, ALU.add)
                    return to_columns(dve, mod[:, 16 + 2 * n:18 + 2 * n], src, diag[:, :], modded)

                def ada_rest(dve):
                    done(dve, nc.vector.tensor_tensor(mod[:, 24:40], mod[:, 24:40], col[:, 24:40], ALU.add), modded)
                    done(dve, nc.vector.scalar_tensor_tensor(Gf[:, :], mod[:, 32:40], 1.0, col[:, 56:64],
                                                             ALU.add, ALU.mult), modded)

                split_fm("mix_split", hT, hP, KD)
                with ExitStack() as s2:
                    oT = sb("oT", [P, 8, S], s2)
                    sg3 = sb("branch_gates", [P, TILES, 3 * D], s2)
                    attention(l, ring, PROJ, GATES, ADA2, col, oT, sg3, ada_out, ada_rest)
                    merge(ring, "merge", BRANCH, MERGED, ((0, 2), (2, 2), (4, 4)), oT, sg3, gate_rows[:, 0, :])
                rms_norm_to_fm("ffn", Gf, mod[:, 24:32])
                split_fm("ffn_split", hT, hP, KD)
                gated_hidden("ffnh", ring, HIDDEN, n_hidden, lambda n, t: None)
                add_gated("ffn_add", gate_rows[:, 1, :])

        def attention(l, ring, PROJ, GATES, ADA2, col, oT, sg3, ada_out, ada_rest):
            with ExitStack() as s3:
                VA, CQ, CKV, KR, QC, KC, VC = 0, 256, 512, 640, 672, 1184, 1312
                p1 = sb("proj_tok", [P, TILES, 1440], s3)
                na_qk = sb("na_qkT", [P, 4, S], s3)
                na_bias = sb("na_bias", [P, TILES, 4, 4, GRID_W], s3)
                gqa_g = sb("gqa_g", [P, 2, 64], s3)
                bias_loaded = nc.alloc_semaphore("na_bias_loaded")
                gains_loaded = nc.alloc_semaphore("gqa_gains_loaded")

                lora_w = sb("lora_w", [P, 1280], s3)
                lora_loaded = nc.alloc_semaphore("lora_w_loaded")
                jobs = []
                for b in range(4):
                    act = b % 2 == 0
                    jobs.append(Job(PROJ + b // 2, "fm", b % 2, S, act, copy_out(act, na_qk[:, b, :])))
                for u in range(6):
                    w = 160 if u == 5 else 256
                    for t in range(TILES):
                        act = t == 0
                        jobs.append(Job(PROJ + 2 + u, "tok", t, w, act,
                                        copy_out(act, p1[:, t, 256 * u:256 * u + w])))

                def load_small(sp):
                    for i, name in enumerate(("gqa_q_norm_g", "gqa_k_norm_g")):
                        src = A[name][bass.ds(l, 1), :].broadcast_to([P, 64])
                        sp.dma_start(gqa_g[:, i, :], src).then_inc(gains_loaded, 16)
                    sp.wait_ge(strips_written, 16 * DEPTH * 16)
                    sp.dma_start(na_bias[:, :, :, :, :].rearrange("p t h r c -> p (t h r c)"),
                                 strips[bass.ds(l, 1), :, :].rearrange("o p n -> (o p) n")).then_inc(bias_loaded, 16)

                    sp.dma_start(lora_w[:, 0:768].rearrange("p (k n) -> p k n", k=2),
                                 A["mla_w_uq"][bass.ds(l, 1), :, :].rearrange("o (k p) n -> p (o k) n", p=P)) \
                        .then_inc(lora_loaded, 16)
                    sp.dma_start(lora_w[:, 768:1280], A["mla_w_ukv"][bass.ds(l, 1), :, :]
                                 .rearrange("o p n -> p (o n)")).then_inc(lora_loaded, 16)

                project("proj", ring, jobs, extra={"sync": load_small})

                ms = sb("mean_squares", [P, TILES, 12], s3)
                rs = sb("inv_rms", [P, TILES, 12], s3)
                kpe = sb("mla_k_pe", [P, TILES, 1, 32], s3)
                gqaT = sb("gqa_T", [P, 6, S], s3)
                kvb = sb("mla_kv", [P, TILES, 4, P], s3)
                heads_scope = ExitStack()
                roped = sb("gqa_roped", [P, TILES, 12, 64], heads_scope)
                scratch = ExitStack()
                sq = sb("squares", [P, TILES, 1056], scratch)
                prep = Count(nc, "prep_step")
                rooted = Count(nc, "prep_rooted")
                summed_sq = nc.alloc_semaphore("prep_sums")

                jobs = [Job(GATES + b, "tok", t, 256, True,
                            (lambda dst: lambda src: nc.scalar.activation(dst, src, ACT.Sigmoid))(
                                sg3[:, t, 256 * b:256 * b + 256])) for b in range(12) for t in range(TILES)]

                def prepare(dve):
                    v = nc.vector
                    dve.wait_ge(bias_loaded, 16)
                    bias4 = na_bias[:, :, :, :, :].rearrange("p t h r c -> p (t h r) c")
                    for name, op in (("na_seen", ALU.mult), ("na_neg", ALU.add)):
                        done(dve, v.tensor_tensor(bias4, bias4, const(name).unsqueeze(1).broadcast_to([P, 32, 64]), op), prep)
                        yield
                    done(dve, v.tensor_tensor(sq[:, :, :], p1[:, :, CQ:VC], p1[:, :, CQ:VC], ALU.mult), prep)
                    yield
                    done(dve, v.tensor_reduce(ms[:, :, 0:1], sq[:, :, 0:256], AX, ALU.add), prep)
                    yield
                    done(dve, v.tensor_reduce(ms[:, :, 1:2], sq[:, :, 256:384], AX, ALU.add), prep)
                    yield
                    done(dve, v.tensor_reduce(ms[:, :, 2:12], sq[:, :, 416:1056].rearrange("p t (h d) -> p t h d", h=10),
                                              AX, ALU.add), prep)
                    yield
                    for c0, c1, n in ((0, 1, 256), (1, 2, 128), (2, 12, 64)):
                        ins = v.tensor_scalar(ms[:, :, c0:c1], ms[:, :, c0:c1], 1.0 / n, EPS, ALU.mult, ALU.add)
                        if c0 < 2:
                            done(dve, ins, prep)
                    ins.then_inc(summed_sq, 1)
                    rotate(dve, prep, kpe[:, :, :, :], p1[:, :, KR:KR + 32].unsqueeze(2), const("mla_cos"),
                           const("mla_sin"), sq[:, :, 0:32].unsqueeze(2), 1, 1)
                    yield
                    dve.wait_ge(rooted.sem, 1)
                    dve.wait_ge(gains_loaded, 32)
                    for at, n, j in ((CQ, 256, 0), (CKV, 128, 1)):
                        done(dve, v.tensor_tensor(p1[:, :, at:at + n], p1[:, :, at:at + n],
                                                  rs[:, :, j:j + 1].broadcast_to([P, TILES, n]), ALU.mult), prep)
                        yield
                    qk = p1[:, :, QC:VC].rearrange("p t (h d) -> p t h d", h=10)
                    done(dve, v.tensor_tensor(qk, qk, rs[:, :, 2:12].unsqueeze(3).broadcast_to([P, TILES, 10, 64]),
                                              ALU.mult), prep)
                    yield
                    for h0, h1, g in ((0, 8, 0), (8, 10, 1)):
                        by = gqa_g[:, g, :].unsqueeze(1).unsqueeze(1).broadcast_to([P, TILES, h1 - h0, 64])
                        done(dve, v.tensor_tensor(qk[:, :, h0:h1, :], qk[:, :, h0:h1, :], by, ALU.mult), prep)
                        yield
                    rotate(dve, prep, roped[:, :, 0:10, :], qk, const("ax_cos"), const("ax_sin"),
                           sq[:, :, 0:640].rearrange("p t (h d) -> p t h d", h=10), 10, 2)
                    yield
                    done(dve, v.tensor_copy(roped[:, :, 10, :], roped[:, :, 9, :]), prep)
                    yield
                    done(dve, v.tensor_copy(roped[:, :, 11, :], roped[:, :, 8, :]), prep)
                    yield

                def roots(pool):
                    pool.wait_ge(summed_sq, 1)
                    pool.tensor_tensor(rs[:, :, :].rearrange("p t c -> p (t c)"),
                                       ms[:, :, :].rearrange("p t c -> p (t c)"),
                                       half_neg[:, 0:24], ALU.pow).then_inc(rooted.sem, 1)

                project("gates", ring, jobs, extra={"vector": prepare, "gpsimd": roots}, pace=2)
                scratch.close()

                lora = ExitStack()
                cT = sb("mla_cT", [P, 3, S], lora)
                qfull = sb("mla_q", [P, TILES, 4, 96], lora)
                kfull = sb("mla_k", [P, TILES, 4, 96], lora)
                rot, tmp = (hT[:, i, :].rearrange("p (t h d) -> p t h d", t=TILES, h=4) for i in (6, 7))
                turned, scaled, lifted, act_copied, gqa_turned, step = (Count(nc, f"mla_{n}") for n in
                    ("turned", "scaled", "lifted", "copied", "gqa_turned", "step"))
                with nc.Block() as block:
                    @block.tensor
                    def _(pe):
                        for c in range(3):
                            for t in range(TILES):
                                at = CQ + c * P
                                ins = nc.tensor.transpose(ps[c // 2][:, (c % 2) * S + t * P:(c % 2) * S + (t + 1) * P],
                                                          p1[:, t, at:at + P], ident)
                            ins.then_inc(turned.sem, 1)
                        for b in range(6):
                            for t in range(TILES):
                                ins = nc.tensor.transpose(ps[2 + b // 2][:, (b % 2) * S + t * P:(b % 2) * S + (t + 1) * P],
                                                          roped[:, t, 2 * b:2 * b + 2, :].rearrange("p h d -> p (h d)"), ident)
                            if b % 2:
                                ins.then_inc(gqa_turned.sem, 1)
                        pe.wait_ge(lora_loaded, 32)
                        pe.wait_ge(scaled.sem, 3)
                        pe.wait_ge(act_copied.sem, 1)
                        wq = lora_w[:, 0:768].rearrange("p (k n) -> p k n", k=2)
                        wkv = lora_w[:, 768:1280].unsqueeze(1)
                        bank = (6, 7, 0, 2)
                        for t in range(TILES):
                            for c in range(2):
                                ins = nc.tensor.matmul(ps[bank[t]][:, 0:384], cT[:, c, t * P:(t + 1) * P], wq[:, c, :],
                                                       start=c == 0, stop=c == 1)
                            ins.then_inc(lifted.sem, 1)
                        for t in range(TILES):
                            ins = nc.tensor.matmul(ps[bank[2 + t]][:, :], cT[:, 2, t * P:(t + 1) * P], wkv[:, 0, :],
                                                   start=True, stop=True)
                            ins.then_inc(lifted.sem, 1)

                    @block.scalar
                    def _(act):
                        for c in range(3):
                            act.wait_ge(turned.sem, max(c + 1, 2))
                            nc.scalar.activation(cT[:, c, :], ps[c // 2][:, (c % 2) * S:(c % 2 + 1) * S], ACT.Copy,
                                                 scale=col[:, 64 + c:65 + c]).then_inc(scaled.sem, 1)
                        for b in range(3):
                            act.wait_ge(gqa_turned.sem, b + 1)
                            nc.scalar.activation(gqaT[:, 2 * b:2 * b + 2, :].rearrange("p b s -> p (b s)"),
                                                 ps[2 + b][:, :], ACT.Copy).then_inc(act_copied.sem, 1)

                    @block.vector
                    def _(dve):
                        v = nc.vector
                        for t in range(TILES):
                            dve.wait_ge(lifted.sem, t + 1)
                            done(dve, v.tensor_copy(qfull[:, t, :, :].rearrange("p h d -> p (h d)"),
                                                    ps[6 + t][:, 0:384]), step)
                        for t in range(TILES):
                            dve.wait_ge(lifted.sem, 3 + t)
                            done(dve, v.tensor_copy(kvb[:, t, :, :].rearrange("p h d -> p (h d)"),
                                                    ps[(0, 2)[t]][:, :]), step)
                        rotate(dve, step, rot[:, :, :, :], qfull[:, :, :, 64:96], const("mla_cos"), const("mla_sin"),
                               tmp[:, :, :, :], 4, 1)
                        done(dve, v.tensor_copy(qfull[:, :, :, 64:96], rot[:, :, :, :]), step)
                        done(dve, v.tensor_copy(kfull[:, :, :, 0:64], kvb[:, :, :, 0:64]), step)
                        done(dve, v.tensor_copy(kfull[:, :, :, 64:96], kpe[:, :, :, :].broadcast_to([P, TILES, 4, 32])), step)

                mT = hT[0:96, :, :].rearrange("p (i h) s -> p i h s", i=2)
                m_turned, m_out = nc.alloc_semaphore("mla_heads_turned"), nc.alloc_semaphore("mla_heads_out")
                with nc.Block() as block:
                    @block.tensor
                    def _(pe):
                        for i, src in enumerate((qfull, kfull)):
                            for h in range(4):
                                for t in range(TILES):
                                    ins = nc.tensor.transpose(
                                        ps[2 * i + h // 2][0:96, (h % 2) * S + t * P:(h % 2) * S + (t + 1) * P],
                                        src[:, t, h, :], ident)
                                if h % 2:
                                    ins.then_inc(m_turned, 1)

                    @block.scalar
                    def _(act):
                        for b in range(4):
                            act.wait_ge(m_turned, b + 1)
                            nc.scalar.activation(mT[:, b // 2, 2 * (b % 2):2 * (b % 2) + 2, :].rearrange("p b s -> p (b s)"),
                                                 ps[b][0:96, :], ACT.Copy).then_inc(m_out, 1)

                lora.close()
                heads_scope.close()
                heads = []
                for h in range(4):
                    base = 64 * (h % 2)
                    heads.append((na_qk[base:base + 64, h // 2, :], na_qk[base:base + 64, 2 + h // 2, :],
                                  (lambda h: lambda kt: p1[:, kt, VA + 64 * h:VA + 64 * h + 64])(h), 64 ** -0.5,
                                  na_bias[:, :, h, :, :].rearrange("p t r c -> p t (r c)")))
                for h in range(4):
                    heads.append((mT[:, 0, h, :], mT[:, 1, h, :],
                                  (lambda h: lambda kt: kvb[:, kt, h, 64:128])(h), 96 ** -0.5, None))
                for h in range(8):
                    base, kv = 64 * (h % 2), h // 4
                    block_k = 4 if kv == h % 2 else 5
                    heads.append((gqaT[base:base + 64, h // 2, :], gqaT[base:base + 64, block_k, :],
                                  (lambda kv: lambda kt: p1[:, kt, VC + 64 * kv:VC + 64 * kv + 64])(kv), 64 ** -0.5, None))
                attend("att", heads, oT, ring, ADA2, ada_out, ada_rest)

        def merge(ring, tag, first, second, chunks, yT, gates, gain):
            n_br = len(chunks)
            with ExitStack() as st:
                m = sb(f"{tag}_sum", [P, TILES, D], st)
                part = sb(f"{tag}_part", [P, 2, 256], st)
                yP = sb(f"{tag}_pair", [P, 2, 8, S], st, FR)
                step = Count(nc, f"{tag}_step")
                split_fm(f"{tag}_split", yT, yP, 8)
                jobs = []
                for nb in range(4):
                    cut = slice(nb * 256, nb * 256 + 256)
                    for t in range(TILES):
                        for b, (c0, k) in enumerate(chunks):
                            def out(src, t=t, b=b, cut=cut):
                                gate = gates[:, t, b * D + cut.start:b * D + cut.stop]
                                dst = m[:, t, cut]
                                if b == 0:
                                    return nc.vector.tensor_tensor(dst, src, gate, ALU.mult)
                                done(nc.vector, nc.vector.tensor_tensor(part[:, b % 2, :], src, gate, ALU.mult), step)
                                return nc.vector.tensor_tensor(dst, dst, part[:, b % 2, :], ALU.add)

                            jobs.append(Job(first + nb, "tok", t, 256, False, out, last=t == 1 and b == n_br - 1,
                                            k=k, lhs=yP, at=256 * c0, k0=c0))
                project(tag, ring, jobs)
                transpose_split(f"{tag}_T", m, hP)
                jobs = []
                for nb in range(4):
                    for t in range(TILES):
                        cut = slice(nb * 256, nb * 256 + 256)

                        def out(src, t=t, cut=cut):
                            done(nc.vector, nc.vector.tensor_tensor(part[:, t, :], src, gain[:, cut], ALU.mult), step)
                            return nc.vector.tensor_tensor(x[:, t, cut], x[:, t, cut], part[:, t, :], ALU.add)

                        jobs.append(Job(second + nb, "tok", t, 256, False, out))
                project(f"{tag}_out", ring, jobs)

        def transpose_block(tag, src, dst):
            turned, out = Count(nc, f"{tag}_turned"), nc.alloc_semaphore(f"{tag}_out")
            with nc.Block() as block:
                @block.tensor
                def _(pe):
                    for b in range(4):
                        for k in (2 * b, 2 * b + 1):
                            for t in range(TILES):
                                ins = nc.tensor.transpose(ps[b][:, (k % 2) * S + t * P:(k % 2) * S + (t + 1) * P],
                                                          src[:, t, k * P:(k + 1) * P], ident)
                        ins.then_inc(turned.sem, 1)

                @block.scalar
                def _(act):
                    for b in (0, 2):
                        act.wait_ge(turned.sem, b + 1)
                        nc.scalar.activation(dst[:, 2 * b:2 * b + 2, :].rearrange("p b s -> p (b s)"), ps[b][:, :],
                                             ACT.Copy).then_inc(out, 1)

                @block.vector
                def _(dve):
                    for b in (1, 3):
                        dve.wait_ge(turned.sem, b + 1)
                        nc.vector.tensor_copy(dst[:, 2 * b:2 * b + 2, :].rearrange("p b s -> p (b s)"),
                                              ps[b][:, :]).then_inc(out, 1)

        def transpose_split(tag, src, pair):
            turned, hi_out, lo_out = Count(nc, f"{tag}_turned"), nc.alloc_semaphore(f"{tag}_hi"), Count(nc, f"{tag}_lo")
            with nc.Block() as block:
                @block.tensor
                def _(pe):
                    for b in range(4):
                        for k in (2 * b, 2 * b + 1):
                            for t in range(TILES):
                                ins = nc.tensor.transpose(ps[b][:, (k % 2) * S + t * P:(k % 2) * S + (t + 1) * P],
                                                          src[:, t, k * P:(k + 1) * P], ident)
                        ins.then_inc(turned.sem, 1)

                @block.scalar
                def _(act):
                    for b in range(4):
                        act.wait_ge(turned.sem, b + 1)
                        nc.scalar.activation(pair[:, 0, 2 * b:2 * b + 2, :].rearrange("p b s -> p (b s)"), ps[b][:, :],
                                             ACT.Copy).then_inc(hi_out, 1)

                @block.vector
                def _(dve):
                    for b in range(4):
                        dve.wait_ge(hi_out, b + 1)
                        hi, lo = (pair[:, i, 2 * b:2 * b + 2, :].rearrange("p b s -> p (b s)") for i in range(2))
                        signal(nc.vector.tensor_tensor(lo, ps[b][:, :], hi.bitcast(FP), ALU.subtract), lo_out)

        def second_part():
            def cols(name, c0, c1):
                return A[name][0, :, c0:c1].rearrange("(k p) n -> p k n", p=P)

            units = []

            def unit(name, c0, c1, k=KD):
                units.append([(0, k, c1 - c0, 0, c1 - c0, cols(name, c0, c1))])
                return len(units) - 1

            def unit_pair(name, c0):
                return [unit(name, c0, c0 + 256), unit(name, c0 + 256, c0 + 512)]

            U_A = unit_pair("w_in_2", 0)
            U_QKV = [unit_pair("w_in_2", 512 + 512 * i) for i in range(3)]
            U_GGATE = unit_pair("w_in_2", 2056)
            U_MERGE = [unit("w_in_2", 6168 + 256 * i, 6424 + 256 * i) for i in range(16)]
            U_SB = [unit_pair("w_in_2", 2568 + 512 * i) for i in range(3)]
            U_LGATE = unit_pair("w_in_2", 5656)
            U_GLA = [unit_pair("w_in_2", 4104 + 512 * i) for i in range(3)]
            U_BR = len(units)
            for n in range(4):
                for nb in range(2):
                    units.append([(0, 4, 512, 0, 512, A["w_branch_2"][0, n, :, 512 * nb:512 * nb + 512]
                                   .rearrange("(k p) n -> p k n", p=P))])
            U_OUT = len(units)
            for nb in range(4):
                unit("w_out_2", 256 * nb, 256 * nb + 256)
            def expert_half(name, e, n):
                return A[name][0, e, :, 256 * n:256 * n + 256].rearrange("(k p) n -> p k n", p=P)

            expert_units, dense_units = [], []
            for e in range(N_EXPERTS):
                for n in range(2):
                    expert_units += [[(0, 8, 256, 0, 256, expert_half(name, e, n))] for name in ("w_gate_2", "w_up_2")]
                for nb in range(2):
                    expert_units.append([(0, 4, 512, 0, 512, A["w_down_2"][0, e, :, 512 * nb:512 * nb + 512]
                                          .rearrange("(k p) n -> p k n", p=P))])
            n_hidden = N_EXPERTS * D_EXPERT // 256
            per = D_EXPERT // 256
            dense_units = hidden_units(n_hidden, lambda n: expert_half("w_gate_2", n // per, n % per),
                                       lambda n: expert_half("w_up_2", n // per, n % per),
                                       lambda n: A["w_down_2"][0, n // per, 256 * (n % per):256 * (n % per) + 256, :]
                                       .rearrange("(k p) n -> p k n", p=P))
            mixer_sem = nc.alloc_semaphore("mixer_sems_from")
            with ExitStack() as st:
                ring = Ring(nc, "second", sb("raw_w", [P, 3, UNIT], st), sb("split_w", [P, 2, 2, UNIT], st, FR), units)
                with ExitStack() as s1:
                    mixer(ring, s1, U_A, U_QKV, U_GGATE, U_MERGE, U_SB, U_GLA, U_LGATE, U_BR, U_OUT)
            clear_semaphores(mixer_sem, nc.alloc_semaphore("mixer_sems_to"))
            with ExitStack() as st:
                raw_w, split_w = sb("expert_raw", [P, 5, UNIT], st), sb("expert_split", [P, 4, 2, UNIT], st, FR)
                ring = Ring(nc, "experts", raw_w, split_w, expert_units)
                comb, chosen, key, rest = (sb(name, [P, TILES, N_EXPERTS], st)
                                           for name in ("combine", "chosen", "slot_key", "combine_rest"))
                most = sb("most_tokens", [P, 1], st)
                most_int = sb("most_tokens_int", [1, 1], st, mybir.dt.int32)
                router_w = sb("router_w", [P, KD, N_EXPERTS], st)
                router_bias = sb("router_bias", [P, N_EXPERTS], st)
                router_loaded = nc.alloc_semaphore("router_loaded")

                def load_ahead(sp):
                    sp.dma_start(router_w[:, :, :], A["w_router_2"].rearrange("(k p) n -> p k n", p=P)) \
                        .then_inc(router_loaded, 16)
                    sp.dma_start(router_bias[:, :], A["router_bias_2"].rearrange("(o n) -> o n", o=1)
                                 .broadcast_to([P, 16])).then_inc(router_loaded, 16)
                    ring.feed(sp, -1)

                layer_norm("ln1", "ln1_g_2", "ln1_b_2", load_ahead)
                transpose_block("x3_T", x, hT)
                router(router_w, router_bias, router_loaded, comb, chosen)
                with ExitStack() as s1:
                    sparse_experts(ring, comb, chosen, key, rest, most, most_int, s1)
                scaled_add("moe", ALPHA)
                n_most = nc.values_load(most_int[0:1, 0:1], min_val=0, max_val=S)
                with nc.If(n_most > P):
                    for engine in (nc.tensor, nc.vector, nc.scalar, nc.gpsimd, nc.sync):
                        engine.nop()
                    ring = Ring(nc, "dense", raw_w, split_w, dense_units)
                    split_fm("x3_split", hT, hP, KD)
                    gated_hidden("dense", ring, 0, n_hidden, lambda n, t: rest[:, t, n // per:n // per + 1])
                    scaled_add("rest", 1.0)
                nc.end_ifs()
                layer_norm("ln2", "ln2_g_2", "ln2_b_2")
            with nc.Block() as block:
                @block.sync
                def _(sp):
                    stored = nc.alloc_semaphore("stored")
                    sp.dma_start(OUT.rearrange("o (t p) d -> p (o t) d", p=P), x[:, :, :]).then_inc(stored, 16)
                    sp.wait_ge(stored, 16)

        def scaled_add(tag, factor):
            step = Count(nc, f"{tag}_added")
            with nc.Block() as block:
                @block.vector
                def _(dve):
                    for q in range(4):
                        t, cut = q // 2, slice((q % 2) * 512, (q % 2) * 512 + 512)
                        signal(nc.vector.scalar_tensor_tensor(x[:, t, cut], x[:, t, cut], factor, ps[4 + q][:, :],
                                                              ALU.mult, ALU.add), step)

        def layer_norm(tag, gain_name, bias_name, load_ahead=None):
            with ExitStack() as st:
                rows = sb(f"{tag}_rows", [P, 2, D], st)
                junk = sb(f"{tag}_junk", [P, TILES, D], st)
                loaded = nc.alloc_semaphore(f"{tag}_rows_loaded")
                step, squared, rooted = (Count(nc, f"{tag}_{n}") for n in ("step", "squared", "rooted"))
                with nc.Block() as block:
                    @block.sync
                    def _(sp):
                        for i, name in enumerate((gain_name, bias_name)):
                            sp.dma_start(rows[:, i, :], A[name].broadcast_to([P, D])).then_inc(loaded, 16)
                        if load_ahead is not None:
                            load_ahead(sp)

                    @block.vector
                    def _(dve):
                        v = nc.vector
                        done(dve, v.tensor_reduce(rstat[:, 0:2], x[:, :, :], AX, ALU.add), step)
                        done(dve, v.tensor_scalar(rstat[:, 0:2], rstat[:, 0:2], 1.0 / D, None, ALU.mult), step)
                        for t in range(TILES):
                            done(dve, v.tensor_scalar(x[:, t, :], x[:, t, :], rstat[:, t:t + 1], None, ALU.subtract), step)
                        dve.wait_ge(rooted.sem, 2)
                        dve.wait_ge(loaded, 32)
                        for t in range(TILES):
                            done(dve, v.scalar_tensor_tensor(x[:, t, :], x[:, t, :], rstat[:, 4 + t:5 + t], rows[:, 0, :],
                                                             ALU.mult, ALU.mult), step)
                            done(dve, v.tensor_tensor(x[:, t, :], x[:, t, :], rows[:, 1, :], ALU.add), step)

                    @block.scalar
                    def _(act):
                        for t in range(TILES):
                            act.wait_ge(step.sem, 3 + t)
                            signal(nc.scalar.activation(junk[:, t, :], x[:, t, :], ACT.Square,
                                                        accum_out=rstat[:, 2 + t:3 + t]), squared)

                    @block.gpsimd
                    def _(pool):
                        pool.wait_ge(squared.sem, 2)
                        rsqrt_on_pool(pool, rstat[:, 4:6], rstat[:, 2:4], 2, rooted, 1.0 / D, LN_EPS)

        def router(w, bias, loaded, comb, chosen):
            with ExitStack() as st:
                sc = sb("router_scores", [P, TILES, 16], st)
                bi = sb("router_biased", [P, TILES, 16], st)
                t1 = sb("router_t1", [P, TILES, 16], st)
                t2 = sb("router_t2", [P, TILES, 16], st)
                gs = sb("router_groups", [P, TILES, 4], st)
                g1 = sb("router_g1", [P, TILES, 4], st)
                g2 = sb("router_g2", [P, TILES, 4], st)
                m = sb("router_max", [P, TILES, 1], st)
                scored, squashed, step = (Count(nc, f"router_{n}") for n in ("scored", "squashed", "step"))
                with nc.Block() as block:
                    @block.tensor
                    def _(pe):
                        pe.wait_ge(loaded, 32)
                        for t in range(TILES):
                            for k in range(KD):
                                ins = nc.tensor.matmul(ps[t][:, 0:16], hT[:, k, t * P:(t + 1) * P], w[:, k, :],
                                                       start=k == 0, stop=k == KD - 1)
                            ins.then_inc(scored.sem, 1)

                    @block.scalar
                    def _(act):
                        for t in range(TILES):
                            act.wait_ge(scored.sem, t + 1)
                            nc.scalar.activation(sc[:, t, :], ps[t][:, 0:16], ACT.Sigmoid).then_inc(squashed.sem, 1)

                    @block.vector
                    def _(dve):
                        v = nc.vector

                        def do(ins):
                            done(dve, ins, step)

                        def first_max(onehot, values, key, rank, n):
                            bc = [P, TILES, n]
                            do(v.tensor_reduce(m[:, :, :], values, AX, ALU.max))
                            do(v.tensor_tensor(key, values, m[:, :, :].broadcast_to(bc), ALU.is_equal))
                            do(v.tensor_tensor(key, key, rank.unsqueeze(1).broadcast_to(bc), ALU.mult))
                            do(v.tensor_reduce(m[:, :, :], key, AX, ALU.max))
                            do(v.tensor_tensor(onehot, key, m[:, :, :].broadcast_to(bc), ALU.is_equal))

                        dve.wait_ge(loaded, 32)
                        dve.wait_ge(squashed.sem, 2)
                        S16, B16, T1, T2 = (a[:, :, :] for a in (sc, bi, t1, t2))
                        do(v.tensor_tensor(B16, S16, bias[:, :].unsqueeze(1).broadcast_to([P, TILES, 16]), ALU.add))
                        e = B16.rearrange("p t (g e) -> p t g e", e=4)
                        pairs = [(a, b) for a in range(4) for b in range(a + 1, 4)]
                        for i, (a, b) in enumerate(pairs):
                            dst = gs[:, :, :] if i == 0 else g1[:, :, :]
                            do(v.tensor_tensor(dst, e[:, :, :, a], e[:, :, :, b], ALU.add))
                            if i:
                                do(v.tensor_tensor(gs[:, :, :], gs[:, :, :], g1[:, :, :], ALU.max))
                        first_max(g2[:, :, :], gs[:, :, :], g1[:, :, :], const("rank4"), 4)
                        inside = g2[:, :, :].unsqueeze(3).broadcast_to([P, TILES, 4, 4])
                        do(v.tensor_tensor(e, e, inside, ALU.mult))
                        do(v.tensor_scalar(g1[:, :, :], g2[:, :, :], -1.0, -NEG, ALU.add, ALU.mult))
                        do(v.tensor_tensor(e, e, g1[:, :, :].unsqueeze(3).broadcast_to([P, TILES, 4, 4]), ALU.add))
                        first_max(T1, B16, T2, const("rank16"), 16)
                        do(v.scalar_tensor_tensor(B16.rearrange("p t e -> p (t e)"), T1.rearrange("p t e -> p (t e)"),
                                                  4 * NEG, B16.rearrange("p t e -> p (t e)"), ALU.mult, ALU.add))
                        first_max(comb[:, :, :], B16, T2, const("rank16"), 16)
                        do(v.tensor_tensor(comb[:, :, :], comb[:, :, :], T1, ALU.add))
                        do(v.tensor_copy(chosen[:, :, :], comb[:, :, :]))
                        do(v.tensor_tensor(comb[:, :, :], comb[:, :, :], S16, ALU.mult))
                        do(v.tensor_reduce(m[:, :, :], comb[:, :, :], AX, ALU.add))
                        do(v.reciprocal(m[:, :, :], m[:, :, :]))
                        do(v.tensor_tensor(comb[:, :, :], comb[:, :, :], m[:, :, :].broadcast_to([P, TILES, 16]), ALU.mult))

        def sparse_experts(ring, comb, chosen, key, rest, most, most_int, st):
            v, a = nc.vector, nc.scalar
            xP = sb("x3_pair", [P, 2, TILES, D], st, FR)
            other = sb("gathered_pair", [P, 2, KD, S], st, FR)
            gathered = (hP, other)
            G = sb("gather_table", [P, 2, TILES, S], st, FR)
            GT = sb("scatter_table", [P, 2, S], st, FR)
            w_slot = sb("slot_weights", [P, 2], st)
            sig = sb("expert_sig", [P, 2, 256], st)
            act_ = sb("expert_hidden", [P, 2, 256], st)
            aT = sb("expert_hidden_T", [P, 2, 4, P], st, FR)
            oP = sb("expert_out", [P, 2, D], st, FR)

            counted, x_hi, step = nc.alloc_semaphore("slots_counted"), nc.alloc_semaphore("x3_hi"), Count(nc, "slot_step")
            with nc.Block() as block:
                @block.tensor
                def _(pe):
                    before = const("sb_strict")
                    nc.tensor.matmul(ps[0][:, 0:16], before, chosen[:, 0, :], start=True, stop=True)
                    nc.tensor.matmul(ps[0][:, 16:32], ones, chosen[:, 0, :], start=True, stop=False)
                    nc.tensor.matmul(ps[0][:, 16:32], before, chosen[:, 1, :], start=False, stop=True)
                    for t in range(TILES):
                        ins = nc.tensor.matmul(ps[0][:, 32:48], ones, chosen[:, t, :], start=t == 0, stop=t == 1)
                    ins.then_inc(counted, 1)

                @block.scalar
                def _(act):
                    a.activation(xP[:, 0, :, :], x[:, :, :], ACT.Copy).then_inc(x_hi, 1)

                @block.vector
                def _(dve):
                    dve.wait_ge(counted, 1)
                    place = ps[0][:, 0:32].rearrange("p (t e) -> p t e", t=TILES)
                    done(dve, v.scalar_tensor_tensor(key[:, :, :], place, 1.0, chosen[:, :, :], ALU.add, ALU.mult), step)
                    done(dve, v.tensor_scalar(key[:, :, :], key[:, :, :], -1.0, None, ALU.add), step)
                    done(dve, v.tensor_scalar(rest[:, :, :], key[:, :, :], P - 0.5, None, ALU.is_gt), step)
                    done(dve, v.tensor_tensor(rest[:, :, :], rest[:, :, :], comb[:, :, :], ALU.mult), step)
                    done(dve, v.tensor_reduce(most[:, :], ps[0][:, 32:48], AX, ALU.max), step)
                    done(dve, v.tensor_copy(most_int[:, :], most[0:1, :]), step)
                    dve.wait_ge(x_hi, 1)
                    done(dve, v.tensor_tensor(xP[:, 1, :, :], x[:, :, :], xP[:, 0, :, :].bitcast(FP), ALU.subtract), step)

            placed, table_turned, table_out = (Count(nc, f"moe_{n}") for n in ("placed", "table_turned", "table_out"))
            picked, picked_act, picked_dve, sigd, acted, turned, a_hi, a_lo, o_hi, o_lo, scattered, chain = (
                nc.alloc_semaphore(f"moe_{n}") for n in ("picked", "picked_act", "picked_dve", "sig", "acted", "turned",
                                                         "a_hi", "a_lo", "o_hi", "o_lo", "scattered", "dve_step"))
            chain = Count(nc, "moe_step")
            N, PAIRS = N_EXPERTS, N_EXPERTS // 2

            with nc.Block() as block:
                @block.sync
                def _(sp):
                    ring.feed(sp, len(ring.units))

                @block.tensor
                def _(pe):
                    def pick(n):
                        pair, c = n // 8, n % 8
                        if pair >= PAIRS:
                            return
                        if c == 0:
                            pe.wait_ge(placed.sem, pair + 1)
                        if n >= 1:
                            pe.wait_ge(picked_dve if c % 2 == 0 else picked_act, (n + 1) // 2)
                        for part in range(2):
                            for t in range(TILES):
                                ins = nc.tensor.matmul(ps[3][:, part * S:(part + 1) * S], xP[:, part, t, c * P:(c + 1) * P],
                                                       G[:, pair % 2, t, :], start=t == 0, stop=t == 1)
                        ins.then_inc(picked, 1)

                    def hidden(e, n):
                        for up in range(2):
                            u = 6 * e + 2 * n + up
                            ring.arrived(pe, u)
                            for c in range(KD):
                                for tp, wp in ((0, 0), (0, 1), (1, 0)):
                                    ins = nc.tensor.matmul(ps[n][:, up * 256:(up + 1) * 256],
                                                           gathered[(e // 2) % 2][:, tp, c, (e % 2) * P:(e % 2 + 1) * P],
                                                           ring.view(u, wp, KD, UNIT_W)[:, c, :],
                                                           start=c + tp + wp == 0, stop=c == KD - 1 and tp == 1)
                            ins.then_inc(ring.used, 1)

                    def scatter(e):
                        pe.wait_ge(o_lo, 2 * e + 2)
                        for t in range(TILES):
                            for nb in range(2):
                                for part in range(2):
                                    ins = nc.tensor.matmul(ps[4 + 2 * t + nb][:, :], GT[:, e % 2, t * P:(t + 1) * P],
                                                           oP[:, part, nb * 512:(nb + 1) * 512],
                                                           start=e == 0 and part == 0, stop=e == N - 1 and part == 1)
                        ins.then_inc(scattered, 1)

                    for n in range(8):
                        pick(n)
                    for e in range(N):
                        table = [G[:, (e // 2) % 2, t, (e % 2) * P:(e % 2 + 1) * P].bitcast(FP) for t in range(TILES)]
                        for t in range(TILES):
                            nc.tensor.transpose(ps[2][:, t * P:(t + 1) * P], table[t], ident)
                        for t in range(TILES):
                            ins = nc.tensor.matmul(ps[2][:, S:S + 1], table[t], comb[:, t, e:e + 1], start=t == 0, stop=t == 1)
                        ins.then_inc(table_turned.sem, 1)
                        if e == 0:
                            pe.wait_ge(picked_dve, 4)
                        elif e % 2 == 0:
                            pe.wait_ge(picked_dve, 4 * (e // 2 + 1))
                        if e >= 1:
                            pe.wait_ge(o_lo, 2 * e - 1)
                        hidden(e, 0)
                        pick(4 * e + 8)
                        if e >= 1:
                            pe.wait_ge(o_lo, 2 * e)
                        hidden(e, 1)
                        pick(4 * e + 9)
                        if e >= 1:
                            scatter(e - 1)
                        pick(4 * e + 10)
                        pe.wait_ge(acted, 2 * e + 2)
                        pe.wait_ge(table_out.sem, e + 1)
                        for n in range(2):
                            for c in range(2):
                                ins = nc.tensor.transpose(ps[2][:, (2 * n + c) * P:(2 * n + c + 1) * P],
                                                          act_[:, n, c * P:(c + 1) * P], ident)
                        ins.then_inc(turned, 1)
                        pick(4 * e + 11)
                        pe.wait_ge(a_lo, e + 1)
                        for nb in range(2):
                            u = 6 * e + 4 + nb
                            ring.arrived(pe, u)
                            for c in range(4):
                                for tp, wp in ((0, 0), (0, 1), (1, 0)):
                                    ins = nc.tensor.matmul(ps[nb][:, :], aT[:, tp, c, :], ring.view(u, wp, 4, 512)[:, c, :],
                                                           start=c + tp + wp == 0, stop=c == 3 and tp == 1)
                            ins.then_inc(ring.used, 1)
                    scatter(N - 1)

                def picked_out(eng, n):
                    if n // 8 >= PAIRS:
                        return
                    eng.wait_ge(picked, n + 1)
                    dst, src = gathered[(n // 8) % 2][:, :, n % 8, :], ps[3][:, :].rearrange("p (h s) -> p h s", h=2)
                    if n % 2 == 0:
                        a.activation(dst, src, ACT.Copy).then_inc(picked_act, 1)
                    else:
                        v.tensor_copy(dst, src).then_inc(picked_dve, 1)

                def flat(ap):
                    return ap.rearrange("p c s -> p (c s)")

                @block.scalar
                def _(act):
                    ring.hi(act, 0)
                    for n in (0, 2, 4, 6):
                        picked_out(act, n)
                    ring.hi(act, 1)
                    for e in range(N):
                        u = 6 * e
                        act.wait_ge(table_turned.sem, e + 1)
                        a.activation(GT[:, e % 2, :], ps[2][:, 0:S], ACT.Copy)
                        a.activation(w_slot[:, e % 2:e % 2 + 1], ps[2][:, S:S + 1], ACT.Copy).then_inc(table_out.sem, 1)
                        ring.hi(act, u + 3)
                        act.wait_ge(ring.used, u + 2)
                        a.activation(sig[:, 0, :], ps[0][:, 0:256], ACT.Sigmoid).then_inc(sigd, 1)
                        picked_out(act, 4 * e + 8)
                        ring.hi(act, u + 5)
                        act.wait_ge(ring.used, u + 4)
                        a.activation(sig[:, 1, :], ps[1][:, 0:256], ACT.Sigmoid).then_inc(sigd, 1)
                        picked_out(act, 4 * e + 10)
                        act.wait_ge(turned, e + 1)
                        a.activation(flat(aT[:, 0, :, :]), ps[2][:, :], ACT.Copy).then_inc(a_hi, 1)
                        for nb in range(2):
                            ring.hi(act, u + 6 + nb)
                            act.wait_ge(ring.used, u + 5 + nb)
                            a.activation(oP[:, 0, nb * 512:(nb + 1) * 512], ps[nb][:, :], ACT.Copy).then_inc(o_hi, 1)

                @block.vector
                def _(dve):
                    def place(pair):
                        if pair >= PAIRS:
                            return
                        for t in range(TILES):
                            for i in range(2):
                                k = key[:, t, 2 * pair + i:2 * pair + i + 1]
                                ins = v.tensor_scalar(G[:, pair % 2, t, i * P:(i + 1) * P], const("slot"), k, None, ALU.is_equal)
                        ins.then_inc(placed.sem, 1)

                    def hidden_out(e, n):
                        dve.wait_ge(sigd, 2 * e + n + 1)
                        done(dve, v.tensor_tensor(sig[:, n, :], ps[n][:, 0:256], sig[:, n, :], ALU.mult), chain)
                        dve.wait_ge(table_out.sem, e + 1)
                        v.scalar_tensor_tensor(act_[:, n, :], ps[n][:, 256:512], w_slot[:, e % 2:e % 2 + 1], sig[:, n, :],
                                               ALU.mult, ALU.mult).then_inc(acted, 1)

                    place(0)
                    ring.lo(dve, 0)
                    for n in (1, 3, 5, 7):
                        picked_out(dve, n)
                    ring.lo(dve, 1)
                    for e in range(N):
                        u = 6 * e
                        if e % 2 == 0:
                            dve.wait_ge(table_turned.sem, max(e, 1))
                            place(e // 2 + 1)
                        ring.lo(dve, u + 3)
                        hidden_out(e, 0)
                        ring.lo(dve, u + 5)
                        picked_out(dve, 4 * e + 9)
                        hidden_out(e, 1)
                        dve.wait_ge(a_hi, e + 1)
                        v.tensor_tensor(flat(aT[:, 1, :, :]), ps[2][:, :], flat(aT[:, 0, :, :]).bitcast(FP),
                                        ALU.subtract).then_inc(a_lo, 1)
                        picked_out(dve, 4 * e + 11)
                        for nb in range(2):
                            ring.lo(dve, u + 6 + nb)
                            cut = slice(nb * 512, (nb + 1) * 512)
                            dve.wait_ge(o_hi, 2 * e + nb + 1)
                            v.tensor_tensor(oP[:, 1, cut], ps[nb][:, :], oP[:, 0, cut].bitcast(FP),
                                            ALU.subtract).then_inc(o_lo, 1)

        def mixer(ring, s1, U_A, U_QKV, U_GGATE, U_MERGE, U_SB, U_GLA, U_LGATE, U_BR, U_OUT):
            v, a = nc.vector, nc.scalar
            yT = [None] * 4
            yT[0] = sb("y_lru", [P, 4, S], s1)
            yT[1] = sb("y_gdn", [P, 4, S], s1)
            par = sb("mixer_columns", [P, 86], s1)
            CONV_A, CONV_B, B_A, B_X, LAM, CONV_G, GDN_N, GLA_B, GLA_N = 0, 16, 20, 24, 28, 32, 80, 81, 85
            merge_gates = sb("merge_gates", [P, TILES, 4 * D], s1)
            small = sb("small_w", [P, KD, 24], s1)
            w_up = sb("gla_up", [16, 512], s1)
            tok8 = sb("beta_decay", [P, TILES, 8], s1)
            hrow = sb("head_rows", [P, 8], s1)
            lrT = sb("low_rank_T", [16, S], s1)

            with ExitStack() as s2:
                raw = sb("raw_2", [P, P], s2)
                gain = sb("final_gain", [P, D], s2)
                raw_loaded, gain_loaded = nc.alloc_semaphore("raw_2_loaded"), nc.alloc_semaphore("final_gain_loaded")
                turned, out = nc.alloc_semaphore("raw_2_turned"), nc.alloc_semaphore("raw_2_out")
                with nc.Block() as block:
                    @block.sync
                    def _(sp):
                        sp.dma_start(gain[:, :], A["final_norm_g"].rearrange("(o n) -> o n", o=1).broadcast_to([P, D])) \
                            .then_inc(gain_loaded, 16)
                        n = 0
                        for name, at, rows in (("conv_a_w_2", CONV_A, 16), ("conv_a_b_2", CONV_B, 4), ("rg_b_a_2", B_A, 4),
                                               ("rg_b_x_2", B_X, 4), ("rg_lambda_2", LAM, 4), ("gdn_conv_w_2", CONV_G, 48),
                                               ("gdn_norm_w_2", GDN_N, 1), ("gla_b_gate_2", GLA_B, 4),
                                               ("gla_norm_w_2", GLA_N, 1)):
                            src = A[name]
                            src = src[0, :, :].rearrange("k (c p) -> (k c) p", p=P) if len(src.shape) == 3 else \
                                src.rearrange("o (c p) -> (o c) p", p=P)
                            sp.dma_start(raw[at:at + rows, :], src).then_inc(raw_loaded, 16)
                        sp.dma_start(small[:, :, 0:8], cols2("w_in_2", 2048, 2056)).then_inc(gain_loaded, 16)
                        sp.dma_start(small[:, :, 8:24], cols2("w_in_2", 5640, 5656)).then_inc(gain_loaded, 16)
                        sp.dma_start(w_up[:, :], A["gla_w_gate_up_2"][0, :, :]).then_inc(gain_loaded, 16)
                        sp.dma_start(hrow[:, 0:4], A["gdn_a_log_2"].broadcast_to([P, 4])).then_inc(gain_loaded, 16)
                        sp.dma_start(hrow[:, 4:8], A["gdn_dt_bias_2"].broadcast_to([P, 4])).then_inc(gain_loaded, 16)
                        ring.feed(sp, -1)
                        sp.wait_ge(gain_loaded, 16 * 6)

                    @block.tensor
                    def _(pe):
                        pe.wait_ge(raw_loaded, 16 * 9)
                        nc.tensor.transpose(ps[0][:, 0:86], raw[0:86, :], ident[0:86, 0:86]).then_inc(turned, 1)

                    @block.scalar
                    def _(act):
                        act.wait_ge(turned, 1)
                        a.activation(par[:, :], ps[0][:, 0:86], ACT.Copy).then_inc(out, 1)
                rms_norm_to_fm("final", row_gain=gain[:, :], keep=True)
                split_fm("final_split", hT, hP, KD)

            def fm_jobs(pair, dst, at=0, func=None):
                def out(b, act):
                    d = dst[:, at + b, :]
                    return copy_out(act, d) if func is None else (lambda src: a.activation(d, src, func))
                return [Job(pair[b // 2], "fm", b % 2, S, b % 2 == 0 or func is not None,
                            out(b, b % 2 == 0 or func is not None)) for b in range(4)]

            def tok_jobs(pair, dst):
                return [Job(pair[i], "tok", t, 256, t == 0, copy_out(t == 0, dst[:, t, 256 * i:256 * i + 256]))
                        for i in range(2) for t in range(TILES)]

            with ExitStack() as s2:
                qkv = sb("gdn_qkv", [P, 12, S], s2)
                ggate = sb("gdn_gate", [P, 4, S], s2)
                w_ax = sb("lru_w", [P, 2, 4, P], s2)
                work_ = sb("work", [P, 9, 4 * S], s2)
                work = [work_[:, i, :] for i in range(9)] + [hT[:, 4 * i:4 * i + 4, :].rearrange("p c s -> p (c s)")
                                                             for i in range(2)]
                ain = work[4].rearrange("p (c s) -> p c s", c=4)
                cleared, w_ax_loaded = nc.alloc_semaphore("lru_w_cleared"), nc.alloc_semaphore("lru_w_loaded")

                def clear(pool):
                    pool.memset(w_ax[:, :, :, :], 0.0).then_inc(cleared, 1)

                def load_lru(sp):
                    sp.wait_ge(cleared, 1)
                    for i, name in enumerate(("rg_w_a_2", "rg_w_x_2")):
                        for half in range(2):
                            src = A[name][0, half:8:2, :, :].rearrange("c i j -> i c j")
                            sp.dma_start(w_ax[64 * half:64 * half + 64, i, :, 64 * half:64 * half + 64], src) \
                                .then_inc(w_ax_loaded, 16)
                    sp.wait_ge(w_ax_loaded, 64)

                jobs = fm_jobs(U_A, ain)
                for i in range(3):
                    jobs += fm_jobs(U_QKV[i], qkv, 4 * i)
                jobs += fm_jobs(U_GGATE, ggate, 0, ACT.Silu)
                small_done, small_out = nc.alloc_semaphore("small_summed"), nc.alloc_semaphore("small_out")

                def small_copy(act):
                    act.wait_ge(small_done, 1)
                    a.activation(tok8[:, :, :].rearrange("p t c -> p (t c)"), ps[7][:, 0:16], ACT.Copy).then_inc(small_out, 1)
                    a.activation(lrT[:, :], ps[7][0:16, S:2 * S], ACT.Copy).then_inc(small_out, 1)

                def small_products(pe):
                    for t in range(TILES):
                        for k in range(KD):
                            nc.tensor.matmul(ps[7][:, 8 * t:8 * t + 8], hT[:, k, t * P:(t + 1) * P], small[:, k, 0:8],
                                             start=k == 0, stop=k == KD - 1)
                    for k in range(KD):
                        ins = nc.tensor.matmul(ps[7][0:16, S:2 * S], small[:, k, 8:24], hT[:, k, :],
                                               start=k == 0, stop=k == KD - 1)
                    ins.then_inc(small_done, 1)

                project("mix_in", ring, jobs, banks=7, extra={"tensor": small_products, "scalar": small_copy,
                                                              "gpsimd": clear, "sync": load_lru})

                def W(i):
                    return work[i]

                def blocks4(i):
                    return work[i].rearrange("p (c s) -> p c s", c=4)

                conv = Count(nc, "conv_step")
                xc = blocks4(0)
                silu_out = nc.alloc_semaphore("gdn_silu")
                gdn_conv = [blocks4(i) for i in (1, 2, 3)]

                def convolve(dve):
                    def one(dst, src, w_cols, bias):
                        w3 = par[:, w_cols[3]:w_cols[3] + 1]
                        if bias is None:
                            ins = v.tensor_scalar(dst, src, w3, None, ALU.mult)
                        else:
                            ins = v.tensor_scalar(dst, src, w3, bias, ALU.mult, ALU.add)
                        done(dve, ins, conv)
                        yield
                        for k in range(3):
                            back = 3 - k
                            done(dve, v.scalar_tensor_tensor(dst[:, back:S], src[:, 0:S - back],
                                                             par[:, w_cols[k]:w_cols[k] + 1], dst[:, back:S],
                                                             ALU.mult, ALU.add), conv)
                            yield
                    for c in range(4):
                        yield from one(xc[:, c, :], ain[:, c, :], [CONV_A + 4 * k + c for k in range(4)],
                            par[:, CONV_B + c:CONV_B + c + 1])
                    for c in range(12):
                        yield from one(gdn_conv[c // 4][:, c % 4, :], qkv[:, c, :], [CONV_G + 12 * k + c for k in range(4)], None)

                def silus(act):
                    for i in range(3):
                        act.wait_ge(conv.sem, 4 * 4 * (i + 2))
                        a.activation(qkv[:, 4 * i:4 * i + 4, :].rearrange("p c s -> p (c s)"), W(1 + i),
                                     ACT.Silu).then_inc(silu_out, 1)

                jobs = [Job(U_MERGE[b], "tok", t, 256, True,
                            (lambda dst: lambda src: a.activation(dst, src, ACT.Sigmoid))(
                                merge_gates[:, t, 256 * b:256 * b + 256])) for b in range(16) for t in range(TILES)]
                n_first = 2 * 6
                project("merge_gates", ring, jobs[0:n_first], extra={"vector": convolve, "scalar": silus}, pace=10)
                beside = Beside("late_gates", ring, jobs[n_first:], (0, 1))

                lru(xc, blocks4, W, par, w_ax, yT[0], B_A, B_X, LAM)
                gdn(ring, beside, qkv, ggate, blocks4, W, tok8, hrow, par[:, GDN_N:GDN_N + 1], yT[1])

            yT[2] = sb("y_sb", [P, 4, S], s1)
            yT[3] = sb("y_gla", [P, 4, S], s1)
            with ExitStack() as s2:
                q = sb("gla_q", [P, 4, S], s2)
                k = sb("gla_k", [P, 4, S], s2)
                vt = sb("gla_v", [P, TILES, 512], s2)
                lgate = sb("gla_gate", [P, 4, S], s2)
                with ExitStack() as s3:
                    sq = sb("sb_q", [P, 4, S], s3)
                    sk = sb("sb_k", [P, 4, S], s3)
                    sv = sb("sb_v", [P, TILES, 512], s3)
                    jobs = []
                    def qkv_jobs(units, q, k, v):
                        return fm_jobs(units[0], q) + fm_jobs(units[1], k) + tok_jobs(units[2], v)

                    project("mix_in_2", ring, qkv_jobs(U_SB, sq, sk, sv) + fm_jobs(U_LGATE, lgate, 0, ACT.Silu))
                    stick_breaking(sq, sk, sv, yT[2], s3, ring, Beside("gla_in", ring, qkv_jobs(U_GLA, q, k, vt), (6, 7)))
                gla(q, k, vt, lgate, lrT, w_up, par, GLA_B, par[:, GLA_N:GLA_N + 1], yT[3], s2)

            with ExitStack() as s2:
                m = sb("mixer_sum", [P, TILES, D], s2)
                part = sb("mixer_part", [P, 512], s2)
                step = Count(nc, "mixer_step")
                yP = sb("mixer_pair", [P, 4, 2, 4, S], s2, FR)
                for n in range(4):
                    split_fm(f"mixer_split{n}", yT[n], yP[:, n, :, :, :], 4)
                jobs = []
                for n in range(4):
                    for nb in range(2):
                        for t in range(TILES):
                            def out(src, n=n, nb=nb, t=t):
                                gate = merge_gates[:, t, n * D + nb * 512:n * D + nb * 512 + 512]
                                dst = m[:, t, nb * 512:nb * 512 + 512]
                                if n == 0:
                                    return v.tensor_tensor(dst, src, gate, ALU.mult)
                                done(v, v.tensor_tensor(part[:, :], src, gate, ALU.mult), step)
                                return v.tensor_tensor(dst, dst, part[:, :], ALU.add)

                            jobs.append(Job(U_BR + 2 * n + nb, "tok", t, 512, False, out, k=4, lhs=yP[:, n, :, :, :],
                                            unit_width=512))
                project("mixer_merge", ring, jobs)
                transpose_split("mixer_T", m, hP)
            jobs = []
            for nb in range(4):
                for t in range(TILES):
                    cut = slice(nb * 256, nb * 256 + 256)

                    def out(src, t=t, cut=cut):
                        return v.scalar_tensor_tensor(x[:, t, cut], x[:, t, cut], ALPHA, src, ALU.mult, ALU.add)

                    jobs.append(Job(U_OUT + nb, "tok", t, 256, False, out))
            project("mixer_out", ring, jobs)

        def cols2(name, c0, c1):
            return A[name][0, :, c0:c1].rearrange("(k p) n -> p k n", p=P)

        def lru(xc, blocks4, W, par, w_ax, y, B_A, B_X, LAM):
            v, a = nc.vector, nc.scalar
            R, I, T, M, N = 1, 2, 3, 4, 5
            summed, squashed, step, acted, coef_ready = (Count(nc, f"lru_{n}") for n in
                                                         ("summed", "squashed", "step", "acted", "coef"))
            with ExitStack() as st:
                cf = sb("lru_coef", [P, 4, 4], st)
                with nc.Block() as block:
                    @block.tensor
                    def _(pe):
                        for i in range(2):
                            for c in range(4):
                                ins = nc.tensor.matmul(ps[2 * i + c // 2][:, (c % 2) * S:(c % 2 + 1) * S],
                                                       w_ax[:, i, c, :], xc[:, c, :], start=True, stop=True)
                            ins.then_inc(summed.sem, 1)

                    @block.scalar
                    def _(act):
                        for i, (B, dst) in enumerate(((B_A, R), (B_X, I))):
                            act.wait_ge(summed.sem, i + 1)
                            for c in range(4):
                                ins = a.activation(blocks4(dst)[:, c, :], ps[2 * i + c // 2][:, (c % 2) * S:(c % 2 + 1) * S],
                                                   ACT.Sigmoid, bias=par[:, B + c:B + c + 1])
                                ins.then_inc(squashed.sem, 1)
                        act.wait_ge(step.sem, 1)
                        done(act, a.activation(cf[:, 1, :], cf[:, 0, :], ACT.Exp), coef_ready)
                        done(act, a.activation(cf[:, 2, :], cf[:, 1, :], ACT.Ln, bias=1.0), coef_ready)
                        act.wait_ge(step.sem, 8)
                        done(act, a.activation(W(M), W(T), ACT.Tanh), acted)
                        done(act, a.activation(W(R), W(T), ACT.Exp), acted)
                        act.wait_ge(step.sem, 11)
                        done(act, a.activation(W(N), W(T), ACT.Sqrt), acted)

                    @block.vector
                    def _(dve):
                        def do(ins):
                            done(dve, ins, step)
                        lam = par[:, LAM:LAM + 4]
                        do(v.scalar_tensor_tensor(cf[:, 0, :], lam, -1.0, lam, ALU.mult, ALU.min))
                        do(v.tensor_scalar(cf[:, 3, :], lam, -1.0, 0.0, ALU.mult, ALU.max))
                        dve.wait_ge(coef_ready.sem, 2)
                        do(v.tensor_tensor(cf[:, 3, :], cf[:, 3, :], cf[:, 2, :], ALU.add))
                        do(v.tensor_scalar(cf[:, 3, :], cf[:, 3, :], -8.0, None, ALU.mult))
                        dve.wait_ge(squashed.sem, 8)
                        for c in range(4):
                            do(v.tensor_scalar(blocks4(T)[:, c, :], blocks4(R)[:, c, :], cf[:, 3, c:c + 1], None, ALU.mult))
                        dve.wait_ge(acted.sem, 2)
                        do(v.tensor_scalar(W(T), W(M), -1.0, 1.0, ALU.mult, ALU.add))
                        do(v.reciprocal(W(N), W(T)))
                        do(v.scalar_tensor_tensor(W(T), W(M), -2.0, W(N), ALU.mult, ALU.mult))
                        dve.wait_ge(acted.sem, 3)
                        do(v.memset(blocks4(N)[:, :, 0:1], 1.0))
                        do(v.tensor_tensor(W(N), W(N), W(I), ALU.mult))
                        do(v.tensor_tensor(W(N), W(N), W(0), ALU.mult))
                        for c in range(4):
                            do(v.tensor_tensor_scan(y[:, c, :], blocks4(R)[:, c, :], blocks4(N)[:, c, :], 0.0,
                                                    ALU.mult, ALU.add))

        def head_norm(tag, oT, sqT, rsT, gain, gate, y):
            v, a = nc.vector, nc.scalar
            squared, summed, rooted, step = (Count(nc, f"{tag}_{n}") for n in ("squared", "summed", "rooted", "step"))
            with nc.Block() as block:
                @block.vector
                def _(dve):
                    done(dve, v.tensor_tensor(sqT, oT, oT, ALU.mult), squared)
                    for b in range(2):
                        cut = slice(512 * b, 512 * b + 512)
                        dve.wait_ge(summed.sem, b + 1)
                        done(dve, v.tensor_scalar(rsT[:, cut], ps[b][:, :], 1.0 / P, EPS, ALU.mult, ALU.add), step)
                    dve.wait_ge(rooted.sem, 1)
                    done(dve, v.reciprocal(rsT, rsT), step)
                    done(dve, v.scalar_tensor_tensor(y, oT, gain, gate, ALU.mult, ALU.mult), step)
                    done(dve, v.tensor_tensor(y, y, rsT, ALU.mult), step)

                @block.tensor
                def _(pe):
                    pe.wait_ge(squared.sem, 1)
                    for b in range(2):
                        nc.tensor.matmul(ps[b][:, :], ones, sqT[:, 512 * b:512 * b + 512], start=True,
                                         stop=True).then_inc(summed.sem, 1)

                @block.scalar
                def _(act):
                    act.wait_ge(step.sem, 2)
                    a.activation(rsT, rsT, ACT.Sqrt).then_inc(rooted.sem, 1)

        def gdn(ring, beside, qkv, ggate, blocks4, W, tok8, hrow, gain, y):
            v, a = nc.vector, nc.scalar
            qT = qkv[:, 0:4, :].rearrange("p c s -> p (c s)")
            kT = qkv[:, 4:8, :].rearrange("p c s -> p (c s)")
            vT = qkv[:, 8:12, :].rearrange("p c s -> p (c s)")
            SQ, RS = 0, 1
            ROW, BROW, DT, AT, ATT, AN, AM, U, TN, Y = 0, 1, 2, 3, 4, 5, 6, 7, 8, 9

            def g8(flat):
                return flat.rearrange("p (g s) -> p g s", g=8)

            with ExitStack() as st:
                tg = sb("gdn_tok", [P, 8, 8], st)
                BETA, G, GC, GL, BE, KD_, T1, T2 = range(8)
                tq = {i: tg[:, i, :] for i in range(8)}

                def by_tile(i):
                    return tg[:, i, :].rearrange("p (h t) -> p t h", t=2)

                step, squared, summed, rooted = (Count(nc, f"gdn_l2_{n}") for n in ("step", "squared", "summed", "rooted"))
                with nc.Block() as block:
                    @block.vector
                    def _(dve):
                        done(dve, v.tensor_tensor(W(SQ), qT, qT, ALU.mult), squared)
                        done(dve, v.tensor_tensor(W(2), kT, kT, ALU.mult), squared)
                        for i in range(2):
                            rs = W(1 + 2 * i)
                            for b in range(2):
                                dve.wait_ge(summed.sem, 2 * i + b + 1)
                                done(dve, v.tensor_scalar(rs[:, 512 * b:512 * b + 512], ps[2 * i + b][:, :], EPS, None,
                                                          ALU.add), step)
                        dve.wait_ge(rooted.sem, 2)
                        for i, z in enumerate((qT, kT)):
                            rs = W(1 + 2 * i)
                            done(dve, v.reciprocal(rs, rs), step)
                            done(dve, v.scalar_tensor_tensor(z, z, P ** -0.5 if i == 0 else 1.0, rs, ALU.mult, ALU.mult), step)
                        d = by_tile(T1)
                        bc = [P, TILES, 4]
                        done(dve, v.tensor_tensor(d, tok8[:, :, 4:8], hrow[:, 4:8].unsqueeze(1).broadcast_to(bc), ALU.add), step)
                        done(dve, v.tensor_scalar(tq[G], tq[T1], 0.0, None, ALU.max), step)
                        done(dve, v.scalar_tensor_tensor(tq[T1], tq[T1], -1.0, tq[T1], ALU.mult, ALU.min), step)
                        dve.wait_ge(rooted.sem, 6)
                        done(dve, v.tensor_tensor(tq[G], tq[G], tq[T2], ALU.add), step)
                        done(dve, v.tensor_tensor(by_tile(G), by_tile(G), hrow[:, 0:4].unsqueeze(1).broadcast_to(bc), ALU.mult), step)
                        done(dve, v.tensor_scalar(tq[G], tq[G], -1.0, None, ALU.mult), step)

                    @block.tensor
                    def _(pe):
                        for i in range(2):
                            pe.wait_ge(squared.sem, i + 1)
                            for b in range(2):
                                nc.tensor.matmul(ps[2 * i + b][:, :], ones, W(2 * i)[:, 512 * b:512 * b + 512],
                                                 start=True, stop=True).then_inc(summed.sem, 1)

                    @block.scalar
                    def _(act):
                        for i in range(2):
                            act.wait_ge(step.sem, 2 * i + 2)
                            done(act, a.activation(W(1 + 2 * i), W(1 + 2 * i), ACT.Sqrt), rooted)
                        done(act, a.activation(by_tile(BETA), tok8[:, :, 0:4], ACT.Sigmoid), rooted)
                        act.wait_ge(step.sem, 11)
                        done(act, a.activation(hrow[:, 0:4], hrow[:, 0:4], ACT.Exp), rooted)
                        done(act, a.activation(tq[T2], tq[T1], ACT.Exp), rooted)
                        done(act, a.activation(tq[T2], tq[T2], ACT.Ln, bias=1.0), rooted)

                mm = Count(nc, "gdn_a_mm")
                step, acted = Count(nc, "gdn_a_step"), Count(nc, "gdn_a_act")
                with nc.Block() as block:
                    @block.tensor
                    def _(pe):
                        nc.tensor.matmul(ps[0][:, 0:8], const("cum64"), tq[G], start=True, stop=True)
                        nc.tensor.matmul(ps[0][:, 8:16], const("blk64"), tq[G], start=True, stop=True).then_inc(mm.sem, 1)
                        pe.wait_ge(step.sem, 2)
                        for g in range(8):
                            ins = nc.tensor.matmul(ps[1 + g // 4][:, (g % 4) * P:(g % 4 + 1) * P], g8(W(AM))[:, g, :],
                                                   const("cum64"), start=True, stop=True)
                        ins.then_inc(mm.sem, 1)
                        for g in range(8):
                            ins = nc.tensor.matmul(ps[3 + g // 4][:, (g % 4) * P:(g % 4 + 1) * P], g8(W(U))[:, g, :],
                                                   ident, start=True, stop=True)
                        ins.then_inc(mm.sem, 1)
                        for g in range(8):
                            ins = nc.tensor.matmul(ps[5 + g // 4][:, (g % 4) * P:(g % 4 + 1) * P], g8(kT)[:, g, :],
                                                   g8(kT)[:, g, :], start=True, stop=True)
                        ins.then_inc(mm.sem, 1)
                        pe.wait_ge(acted.sem, 2)
                        for g in range(8):
                            ins = nc.tensor.matmul(ps[1 + g // 4][:, (g % 4) * P:(g % 4 + 1) * P], g8(kT)[:, g, :],
                                                   g8(qT)[:, g, :], start=True, stop=True)
                        ins.then_inc(mm.sem, 1)

                    @block.scalar
                    def _(act):
                        act.wait_ge(mm.sem, 2)
                        for b in range(2):
                            done(act, a.activation(W(ROW)[:, 512 * b:512 * b + 512], ps[1 + b][:, :], ACT.Copy), acted)
                        act.wait_ge(mm.sem, 3)
                        for b in range(2):
                            done(act, a.activation(W(BROW)[:, 512 * b:512 * b + 512], ps[3 + b][:, :], ACT.Copy), acted)
                        act.wait_ge(step.sem, 12)
                        done(act, a.activation(W(DT), W(DT), ACT.Exp), acted)
                        done(act, a.activation(W(ROW), W(ROW), ACT.Exp), acted)
                        done(act, a.activation(tq[BE], tq[GC], ACT.Exp), acted)
                        done(act, a.activation(tq[KD_], tq[KD_], ACT.Exp), acted)

                    @block.vector
                    def _(dve):
                        def do(ins):
                            done(dve, ins, step)
                        bc = [P, 8, P]
                        do(v.tensor_copy(g8(W(AM)), tq[G].unsqueeze(2).broadcast_to(bc)))
                        do(v.tensor_copy(g8(W(U)), tq[BETA].unsqueeze(2).broadcast_to(bc)))
                        dve.wait_ge(mm.sem, 1)
                        do(v.tensor_copy(tq[GC], ps[0][:, 0:8]))
                        do(v.tensor_tensor(tq[KD_], ps[0][:, 8:16], tq[GC], ALU.subtract))
                        dve.wait_ge(acted.sem, 2)
                        for g in range(8):
                            do(v.tensor_scalar(g8(W(DT))[:, g, :], g8(W(ROW))[:, g, :], tq[GC][:, g:g + 1], 0.0,
                                               ALU.subtract, ALU.min))
                        dve.wait_ge(acted.sem, 7)
                        do(v.tensor_tensor(tq[BE], tq[BE], tq[BETA], ALU.mult))
                        do(v.tensor_tensor(g8(W(AN)), g8(W(DT)), const("strict64").unsqueeze(1).broadcast_to(bc), ALU.mult))
                        do(v.tensor_tensor(W(AN), W(AN), W(BROW), ALU.mult))
                        do(v.tensor_tensor(g8(W(DT)), g8(W(DT)), const("cum64").unsqueeze(1).broadcast_to(bc), ALU.mult))
                        dve.wait_ge(mm.sem, 5)
                        for b in range(2):
                            cut = slice(512 * b, 512 * b + 512)
                            do(v.tensor_tensor(W(AT)[:, cut], W(AN)[:, cut], ps[5 + b][:, :], ALU.mult))
                            do(v.tensor_tensor(W(ATT)[:, cut], W(DT)[:, cut], ps[1 + b][:, :], ALU.mult))

                step, mm, yout = Count(nc, "gdn_inv_step"), Count(nc, "gdn_inv_mm"), Count(nc, "gdn_inv_y")
                levels = (2, 4, 8, 16, 32)
                first = beside.jobs[0].unit
                with nc.Block() as block:
                    bc = [P, 8, P]

                    @block.sync
                    def _(sp):
                        ring.feed(sp, first + 10)

                    @block.vector
                    def _(dve):
                        def do(ins):
                            done(dve, ins, step)
                        dve.wait_ge(mm.sem, 1)
                        for b in range(2):
                            do(v.tensor_copy(W(AN)[:, 512 * b:512 * b + 512], ps[b][:, :]))
                        for dst, src, mask in ((U, AT, "level1_t"), (TN, AN, "level1")):
                            do(v.tensor_tensor(g8(W(dst)), g8(W(src)), const(mask).unsqueeze(1).broadcast_to(bc), ALU.mult))
                            do(v.tensor_tensor(g8(W(dst)), ident.unsqueeze(1).broadcast_to(bc), g8(W(dst)), ALU.subtract))
                        for n, s in enumerate(levels):
                            do(v.tensor_tensor(g8(W(AM)), g8(W(AN)), const(f"level{s}").unsqueeze(1).broadcast_to(bc), ALU.mult))
                            ring.lo(dve, first + 2 * n + 2)
                            dve.wait_ge(mm.sem, 3 + 2 * n)
                            for b in range(2):
                                cut = slice(512 * b, 512 * b + 512)
                                do(v.tensor_tensor(W(U)[:, cut], W(U)[:, cut], ps[4 + b][:, :], ALU.subtract))
                                if n < 4:
                                    do(v.tensor_tensor(W(TN)[:, cut], W(TN)[:, cut], ps[6 + b][:, :], ALU.subtract))

                    @block.tensor
                    def _(pe):
                        for g in range(8):
                            ins = nc.tensor.transpose(ps[g // 4][:, (g % 4) * P:(g % 4 + 1) * P], g8(W(AT))[:, g, :], ident)
                        ins.then_inc(mm.sem, 1)
                        for n in range(5):
                            pe.wait_ge(step.sem, 7 + 5 * n)
                            for g in range(8):
                                ins = nc.tensor.matmul(ps[2 + g // 4][:, (g % 4) * P:(g % 4 + 1) * P], g8(W(AM))[:, g, :],
                                                       g8(W(U))[:, g, :], start=True, stop=True)
                            ins.then_inc(mm.sem, 1)
                            beside.multiply(pe, 2)
                            pe.wait_ge(yout.sem, 2 * n + 2)
                            for g in range(8):
                                ins = nc.tensor.matmul(ps[4 + g // 4][:, (g % 4) * P:(g % 4 + 1) * P], g8(W(TN))[:, g, :],
                                                       g8(W(Y))[:, g, :], start=True, stop=True)
                            for g in range(8 if n < 4 else 0):
                                ins = nc.tensor.matmul(ps[6 + g // 4][:, (g % 4) * P:(g % 4 + 1) * P], g8(W(Y))[:, g, :],
                                                       g8(W(TN))[:, g, :], start=True, stop=True)
                            ins.then_inc(mm.sem, 1)
                            beside.multiply(pe, 2)

                    @block.scalar
                    def _(act):
                        for n in range(5):
                            act.wait_ge(mm.sem, 2 + 2 * n)
                            for b in range(2):
                                done(act, a.activation(W(Y)[:, 512 * b:512 * b + 512], ps[2 + b][:, :], ACT.Copy), yout)
                            ring.hi(act, first + 2 * n + 1)
                            beside.leave(act, True, 4 * n + 2)
                            ring.hi(act, first + 2 * n + 2)
                            beside.leave(act, True, 4 * n + 4)

                KBE, KDEC, VB, WT, UU, QD = 5, 6, 2, 8, 9, 3
                step, mm, acted = Count(nc, "gdn_w_step"), Count(nc, "gdn_w_mm"), Count(nc, "gdn_w_act")
                with nc.Block() as block:
                    @block.tensor
                    def _(pe):
                        for i, z in enumerate((kT, vT)):
                            for g in range(8):
                                ins = nc.tensor.transpose(ps[2 * i + g // 4][:, (g % 4) * P:(g % 4 + 1) * P], g8(z)[:, g, :], ident)
                            ins.then_inc(mm.sem, 1)
                        pe.wait_ge(acted.sem, 16)
                        for g in range(8):
                            ins = nc.tensor.matmul(ps[4 + g // 4][:, (g % 4) * P:(g % 4 + 1) * P], g8(W(KBE))[:, g, :],
                                                   g8(W(U))[:, g, :], start=True, stop=True)
                        ins.then_inc(mm.sem, 1)
                        for g in range(8):
                            ins = nc.tensor.matmul(ps[6 + g // 4][:, (g % 4) * P:(g % 4 + 1) * P], g8(W(U))[:, g, :],
                                                   g8(W(VB))[:, g, :], start=True, stop=True)
                        ins.then_inc(mm.sem, 1)

                    @block.scalar
                    def _(act):
                        for n, (dst, bank, colq) in enumerate(((KBE, 0, BE), (VB, 2, BETA))):
                            act.wait_ge(mm.sem, n + 1)
                            for g in range(8):
                                done(act, a.activation(g8(W(dst))[:, g, :], ps[bank + g // 4][:, (g % 4) * P:(g % 4 + 1) * P],
                                                       ACT.Copy, scale=tq[colq][:, g:g + 1]), acted)
                        act.wait_ge(mm.sem, 3)
                        for b in range(2):
                            done(act, a.activation(W(WT)[:, 512 * b:512 * b + 512], ps[4 + b][:, :], ACT.Copy), acted)

                    @block.vector
                    def _(dve):
                        def do(ins):
                            done(dve, ins, step)
                        do(v.tensor_tensor(W(QD), qT, W(ROW), ALU.mult))
                        dve.wait_ge(acted.sem, 8)
                        for g in range(8):
                            do(v.tensor_scalar(g8(W(KDEC))[:, g, :], ps[g // 4][:, (g % 4) * P:(g % 4 + 1) * P],
                                               tq[KD_][:, g:g + 1], None, ALU.mult))
                        dve.wait_ge(mm.sem, 4)
                        for b in range(2):
                            do(v.tensor_copy(W(UU)[:, 512 * b:512 * b + 512], ps[6 + b][:, :]))

                step, mm = Count(nc, "gdn_scan_step"), Count(nc, "gdn_scan_mm")
                oT = W(5)
                with ExitStack() as s5:
                    state = W(10)[:, 0:512].rearrange("p (h d) -> p h d", h=4)
                    new = W(10)[:, 512:1024].rearrange("p (h d) -> p h d", h=4)
                    with nc.Block() as block:
                        @block.vector
                        def _(dve):
                            def do(ins):
                                done(dve, ins, step)
                            do(v.memset(state, 0.0))
                            uu = W(UU).rearrange("p (h t d) -> p h t d", h=4, t=2)
                            for n in range(4):
                                t, b0 = n // 2, 64 * (n % 2)
                                dve.wait_ge(mm.sem, 2 * n + 1)
                                do(v.tensor_tensor(new[b0:b0 + 64, :, :], uu[b0:b0 + 64, :, t, :],
                                                   ps[0][b0:b0 + 64, :].rearrange("p (h d) -> p h d", h=4), ALU.subtract))
                                dve.wait_ge(mm.sem, 2 * n + 2)
                                for h in range(4):
                                    do(v.scalar_tensor_tensor(state[:, h, :], state[:, h, :],
                                                              blocks4(ROW)[:, h, 64 * n + 63:64 * n + 64],
                                                              ps[1][:, h * P:(h + 1) * P], ALU.mult, ALU.add))

                        @block.tensor
                        def _(pe):
                            for n in range(4):
                                t, b0 = n // 2, 64 * (n % 2)
                                cut = slice(64 * n, 64 * n + 64)
                                pe.wait_ge(step.sem, 1 + 5 * n)
                                for h in range(4):
                                    ins = nc.tensor.matmul(ps[0][b0:b0 + 64, h * P:(h + 1) * P], blocks4(WT)[:, h, cut],
                                                           state[:, h, :], start=True, stop=True)
                                ins.then_inc(mm.sem, 1)
                                pe.wait_ge(step.sem, 2 + 5 * n)
                                for h in range(4):
                                    g = 2 * h + t
                                    out = ps[2 + h][:, cut]
                                    nc.tensor.matmul(out, state[:, h, :], blocks4(QD)[:, h, cut], start=True, stop=False)
                                    nc.tensor.matmul(out, new[b0:b0 + 64, h, :],
                                                     g8(W(ATT))[b0:b0 + 64, g, b0:b0 + 64], start=False, stop=True)
                                for h in range(4):
                                    g = 2 * h + t
                                    ins = nc.tensor.matmul(ps[1][:, h * P:(h + 1) * P], g8(W(KDEC))[b0:b0 + 64, g, :],
                                                           new[b0:b0 + 64, h, :], start=True, stop=True)
                                ins.then_inc(mm.sem, 1)
                    o_out = Count(nc, "gdn_o_out")
                    with nc.Block() as block:
                        @block.scalar
                        def _(act):
                            for h in range(4):
                                done(act, a.activation(blocks4(5)[:, h, :], ps[2 + h][:, 0:S], ACT.Copy), o_out)
            head_norm("gdn_norm", W(5), W(6), W(7), gain, ggate[:, :, :].rearrange("p c s -> p (c s)"),
                      y[:, :, :].rearrange("p c s -> p (c s)"))

        def stick_breaking(q, k, sv, y, s3, ring, beside):
            v, a = nc.vector, nc.scalar
            scale = 64 ** -0.5
            Wd = S + P
            with ExitStack() as st:
                ab = sb("sb_abs", [P, 2, Wd], st)
                score = sb("sb_score", [P, 2, Wd], st)
                keep = sb("sb_keep", [P, 2, Wd], st)
                wt = sb("sb_weights", [P, 2, Wd], st)
                scored, prepped, logged, kept, cumed, added, expd, masked, mixed, out, step = (
                    Count(nc, f"sb_{n}") for n in ("scored", "prepped", "logged", "kept", "cumed", "added", "expd",
                                                   "masked", "mixed", "out", "step"))
                exped = Count(nc, "sb_exped")
                strict = const("sb_strict")
                H = 8
                first = beside.jobs[0].unit
                n_beside = len(beside.jobs) // 2
                with nc.Block() as block:
                    @block.sync
                    def _(sp):
                        ring.feed(sp, first + n_beside)

                    @block.tensor
                    def _(pe):
                        for i in range(H + 2):
                            if i < H:
                                b0, c = 64 * (i % 2), i // 2
                                if i >= 2:
                                    pe.wait_ge(added.sem, i - 1)
                                kk, qq = k[b0:b0 + 64, c, :], q[b0:b0 + 64, c, :]
                                nc.tensor.matmul(ps[i % 2][:, 0:S], kk[:, 0:P], qq, start=True, stop=True)
                                nc.tensor.matmul(ps[i % 2][:, S:Wd], kk[:, P:S], qq[:, P:S], start=True,
                                                 stop=True).then_inc(scored.sem, 1)
                            beside.multiply(pe, 1)
                            if 1 <= i <= H:
                                n = i - 1
                                pe.wait_ge(kept.sem, n + 1)
                                if n >= 2:
                                    pe.wait_ge(added.sem, n - 1)
                                kp = keep[:, n % 2, :]
                                bank = ps[2 + n % 2]
                                nc.tensor.matmul(bank[:, 0:S], const("sb_incl"), kp[:, 0:S], start=True, stop=False)
                                nc.tensor.matmul(bank[:, P:S], ones, kp[:, S:Wd], start=False, stop=True)
                                nc.tensor.matmul(bank[:, S:Wd], const("sb_incl"), kp[:, S:Wd], start=True,
                                                 stop=True).then_inc(cumed.sem, 1)
                            if i >= 2:
                                n = i - 2
                                pe.wait_ge(masked.sem, n + 1)
                                if n >= 2:
                                    pe.wait_ge(out.sem, n - 1)
                                b0 = 64 * (n % 2)
                                o = ps[4 + n % 2][b0:b0 + 64, :]
                                nc.tensor.matmul(o[:, 0:S], sv[:, 0, 64 * n:64 * n + 64], wt[:, n % 2, 0:S], start=True, stop=False)
                                nc.tensor.matmul(o[:, P:S], sv[:, 1, 64 * n:64 * n + 64], wt[:, n % 2, S:Wd], start=False,
                                                 stop=True).then_inc(mixed.sem, 1)
                            beside.multiply(pe, 1)

                    @block.vector
                    def _(dve):
                        for i in range(H + 2):
                            beside.leave(dve, False, 2 * i)
                            if i < H:
                                dve.wait_ge(scored.sem, i + 1)
                                z = ps[i % 2][:, 0:Wd]
                                if i >= 2:
                                    dve.wait_ge(cumed.sem, i - 1)
                                zs = score[:, i % 2, :]
                                done(dve, v.tensor_scalar(zs, z, scale, None, ALU.mult), step)
                                v.scalar_tensor_tensor(ab[:, i % 2, :], zs, -1.0, zs, ALU.mult, ALU.min) \
                                    .then_inc(prepped.sem, 1)
                            if 1 <= i <= H:
                                n = i - 1
                                dve.wait_ge(cumed.sem, n + 1)
                                if n >= 2:
                                    dve.wait_ge(mixed.sem, n - 1)
                                v.tensor_tensor(wt[:, n % 2, :], score[:, n % 2, :], ps[2 + n % 2][:, 0:Wd],
                                                ALU.add).then_inc(added.sem, 1)
                            if i < H:
                                dve.wait_ge(logged.sem, i + 1)
                                kp, lg = keep[:, i % 2, :], ab[:, i % 2, :]
                                done(dve, v.scalar_tensor_tensor(lg, score[:, i % 2, :], 0.0, lg, ALU.max, ALU.add), step)
                                v3 = v.scalar_tensor_tensor
                                done(dve, v3(kp[:, 0:P], lg[:, 0:P], -1.0, strict, ALU.mult, ALU.mult), step)
                                done(dve, v.tensor_scalar(kp[:, P:S], lg[:, P:S], -1.0, None, ALU.mult), step)
                                v3(kp[:, S:Wd], lg[:, S:Wd], -1.0, strict, ALU.mult, ALU.mult).then_inc(kept.sem, 1)
                            if 1 <= i <= H:
                                n = i - 1
                                dve.wait_ge(expd.sem, n + 1)
                                done(dve, v.tensor_tensor(wt[:, n % 2, 0:P], wt[:, n % 2, 0:P], strict, ALU.mult), step)
                                v.tensor_tensor(wt[:, n % 2, S:Wd], wt[:, n % 2, S:Wd], strict, ALU.mult).then_inc(masked.sem, 1)
                            if i >= 2:
                                n = i - 2
                                b0 = 64 * (n % 2)
                                dve.wait_ge(mixed.sem, n + 1)
                                v.tensor_copy(y[b0:b0 + 64, n // 2, :], ps[4 + n % 2][b0:b0 + 64, 0:S]).then_inc(out.sem, 1)
                            ring.lo(dve, min(first + i + 1, first + n_beside))
                            beside.leave(dve, False, 2 * i + 1)

                    @block.scalar
                    def _(act):
                        for i in range(H + 1):
                            beside.leave(act, True, 2 * i)
                            if i < H:
                                act.wait_ge(prepped.sem, i + 1)
                                z = ab[:, i % 2, :]
                                done(act, a.activation(z, z, ACT.Exp), exped)
                                a.activation(z, z, ACT.Ln, bias=1.0).then_inc(logged.sem, 1)
                            if i >= 1:
                                n = i - 1
                                act.wait_ge(added.sem, n + 1)
                                w = wt[:, n % 2, :]
                                a.activation(w, w, ACT.Exp).then_inc(expd.sem, 1)
                            ring.hi(act, min(first + i + 1, first + n_beside))
                            beside.leave(act, True, 2 * i + 1)

        def gla(q, k, vt, lgate, lrT, w_up, par, GLA_B, gain, y, s2):
            v, a = nc.vector, nc.scalar
            with ExitStack() as st:
                bc_ = sb("gla_bcum", [P, 4 * S], st)
                eb = sb("gla_exp", [P, 4 * S], st)
                kd = sb("gla_kdT", [P, 4 * S], st)
                at = hT[:, 0:4, :].rearrange("p c (t s) -> p (c t) s", t=2)
                kt = hT[:, 4:8, :].rearrange("p c (t s) -> p (c t) s", t=2)
                vx = sb("gla_v_pairs", [P, TILES, 4, 2, P], st)
                states = sb("gla_states", [P, 2, 16, P], st)
                flat = "p c s -> p (c s)"
                qf, kf = q[:, :, :].rearrange(flat), k[:, :, :].rearrange(flat)
                mm, step, acted = (Count(nc, f"gla_{n}") for n in ("mm", "step", "acted"))
                with nc.Block() as block:
                    @block.tensor
                    def _(pe):
                        for c in range(4):
                            ins = nc.tensor.matmul(ps[c // 2][:, (c % 2) * S:(c % 2 + 1) * S], w_up[:, c * P:(c + 1) * P],
                                                   lrT[:, :], start=True, stop=True)
                        ins.then_inc(mm.sem, 1)
                        pe.wait_ge(step.sem, 9)
                        for g in range(8):
                            ins = nc.tensor.matmul(ps[2 + g // 4][:, (g % 4) * P:(g % 4 + 1) * P], kf[:, g * P:(g + 1) * P],
                                                   qf[:, g * P:(g + 1) * P], start=True, stop=True)
                        ins.then_inc(mm.sem, 1)
                        for g in range(8):
                            ins = nc.tensor.transpose(ps[4 + g // 4][:, (g % 4) * P:(g % 4 + 1) * P], kd[:, g * P:(g + 1) * P], ident)
                        ins.then_inc(mm.sem, 1)

                    @block.scalar
                    def _(act):
                        act.wait_ge(mm.sem, 1)
                        for c in range(4):
                            done(act, a.activation(bc_[:, c * S:(c + 1) * S], ps[c // 2][:, (c % 2) * S:(c % 2 + 1) * S],
                                                   ACT.Identity, bias=par[:, GLA_B + c:GLA_B + c + 1]), acted)
                        act.wait_ge(step.sem, 2)
                        done(act, a.activation(eb[:, :], eb[:, :], ACT.Exp), acted)
                        done(act, a.activation(eb[:, :], eb[:, :], ACT.Ln, bias=1.0), acted)
                        act.wait_ge(step.sem, 4)
                        done(act, a.activation(eb[:, :], bc_[:, :], ACT.Exp, scale=1.0 / 16), acted)
                        act.wait_ge(step.sem, 5)
                        done(act, a.activation(kd[:, :], kd[:, :], ACT.Exp, scale=1.0 / 16), acted)
                        done(act, a.activation(bc_[:, :], bc_[:, :], ACT.Exp, scale=-1.0 / 16), acted)
                        act.wait_ge(mm.sem, 3)
                        for b in range(2):
                            done(act, a.activation(kt[:, 4 * b:4 * b + 4, :].rearrange("p g d -> p (g d)"), ps[4 + b][:, :],
                                                   ACT.Copy), acted)

                    @block.vector
                    def _(dve):
                        def do(ins):
                            done(dve, ins, step)
                        dve.wait_ge(acted.sem, 4)
                        do(v.scalar_tensor_tensor(eb[:, :], bc_[:, :], -1.0, bc_[:, :], ALU.mult, ALU.min))
                        do(v.tensor_scalar(bc_[:, :], bc_[:, :], 0.0, None, ALU.min))
                        dve.wait_ge(acted.sem, 6)
                        do(v.tensor_tensor(bc_[:, :], bc_[:, :], eb[:, :], ALU.subtract))
                        do(v.tensor_tensor_scan(bc_[:, :], const("restart16"), bc_[:, :], 0.0, ALU.mult, ALU.add))
                        b3 = bc_[:, :].rearrange("p (n s) -> p n s", s=16)
                        do(v.tensor_tensor(kd[:, :].rearrange("p (n s) -> p n s", s=16),
                                           b3[:, :, 15:16].broadcast_to([P, 64, 16]), b3, ALU.subtract))
                        dve.wait_ge(acted.sem, 9)
                        do(v.scalar_tensor_tensor(qf, qf, P ** -0.5, eb[:, :], ALU.mult, ALU.mult))
                        do(v.tensor_tensor(kd[:, :], kd[:, :], kf, ALU.mult))
                        do(v.tensor_tensor(kf, kf, bc_[:, :], ALU.mult))
                        for par_ in range(2):
                            last = v.tensor_scalar(vx[:, :, :, par_, :], vt[:, :, :].rearrange("p t (h d) -> p t h d", h=4),
                                                   const("parity")[:, par_:par_ + 1], None, ALU.mult)
                            do(last)
                        dve.wait_ge(mm.sem, 2)
                        for b in range(2):
                            do(v.tensor_tensor(at[:, 4 * b:4 * b + 4, :], ps[2 + b][:, :].rearrange("p (g s) -> p g s", g=4),
                                               const("causal16").unsqueeze(1).broadcast_to([P, 4, P]), ALU.mult))
                mm, step, acted = (Count(nc, f"gla_scan_{n}") for n in ("mm", "step", "acted"))
                oT = kd[:, :]
                with nc.Block() as block:
                    @block.tensor
                    def _(pe):
                        def updates(h):
                            if h >= 1:
                                pe.wait_ge(step.sem, 16 * h)
                            for pr in range(8):
                                t, b0 = pr // 4, 32 * (pr % 4)
                                ins = nc.tensor.matmul(ps[pr % 4][:, t * S:(t + 1) * S], kt[b0:b0 + 32, 2 * h + t, :],
                                                       vx[b0:b0 + 32, t, h, :, :].rearrange("p a d -> p (a d)"),
                                                       start=True, stop=True, tile_position=(b0, 0))
                            ins.then_inc(mm.sem, 1)

                        def outputs(h):
                            if h >= 2:
                                pe.wait_ge(acted.sem, h - 1)
                            bank = ps[4 + h % 2]
                            for t in range(TILES):
                                nc.tensor.matmul(bank[:, t * P:(t + 1) * P], vt[:, t, h * P:(h + 1) * P], at[:, 2 * h + t, :],
                                                 start=t == 0, stop=False, skip_group_check=True)
                            pe.wait_ge(step.sem, 16 * (h + 1))
                            for n in range(1, 16):
                                ins = nc.tensor.matmul(bank[:, 16 * n:16 * n + 16], states[:, h % 2, n, :],
                                                       q[:, h, 16 * n:16 * n + 16], start=False, stop=n == 15,
                                                       skip_group_check=True)
                            ins.then_inc(mm.sem, 1)

                        for h in range(5):
                            if h < 4:
                                updates(h)
                            if h >= 1:
                                outputs(h - 1)

                    @block.vector
                    def _(dve):
                        def do(ins):
                            done(dve, ins, step)
                        e4 = eb[:, :].rearrange("p (h s) -> p h s", h=4)
                        for h in range(4):
                            if h >= 2:
                                dve.wait_ge(mm.sem, 2 * h - 1)
                            dve.wait_ge(mm.sem, max(2 * h, 1))
                            for n in range(16):
                                pr = n // 2
                                kv = ps[pr % 4][:, (pr // 4) * S + (n % 2) * P:(pr // 4) * S + (n % 2 + 1) * P]
                                if n == 15:
                                    do(v.memset(states[:, h % 2, 0, 0:1], 0.0))
                                elif n == 0:
                                    do(v.tensor_copy(states[:, h % 2, 1, :], kv))
                                else:
                                    do(v.scalar_tensor_tensor(states[:, h % 2, n + 1, :], states[:, h % 2, n, :],
                                                              e4[:, h, 16 * n + 15:16 * n + 16], kv, ALU.mult, ALU.add))

                    @block.scalar
                    def _(act):
                        for h in range(4):
                            act.wait_ge(mm.sem, 2 * h + 3 if h < 3 else 8)
                            a.activation(oT[:, h * S:(h + 1) * S], ps[4 + h % 2][:, 0:S], ACT.Copy).then_inc(acted.sem, 1)
                head_norm("gla_norm", oT, bc_[:, :], eb[:, :], gain, lgate[:, :, :].rearrange(flat),
                          y[:, :, :].rearrange(flat))

        def clear_semaphores(first, last):
            with nc.Block() as block:
                @block.gpsimd
                def _(pool):
                    pool.sem_clear(range(first.num, last.num))
            nc.prepend_free_semaphores(list(range(first.num, last.num)))

        first_sem = nc.alloc_semaphore("layer_sems_from")
        with nc.Fori(0, DEPTH) as l:
            layer(l)
            last_sem = nc.alloc_semaphore("layer_sems_to")
            clear_semaphores(first_sem, last_sem)
        second_part()


NAMES = ("x", "c", "ada_w", "ada_b", "norm_mix_g", "norm_ffn_g", "w_in", "na_rpb", "mla_q_norm_g", "mla_kv_norm_g",
         "mla_w_uq", "mla_w_ukv", "gqa_q_norm_g", "gqa_k_norm_g", "w_br_na", "w_br_mla", "w_br_gqa", "w_out",
         "ffn_w_gate_up", "ffn_w_down", "final_norm_g", "w_in_2", "conv_a_w_2", "conv_a_b_2", "rg_w_a_2", "rg_b_a_2",
         "rg_w_x_2", "rg_b_x_2", "rg_lambda_2", "gdn_conv_w_2", "gdn_a_log_2", "gdn_dt_bias_2", "gdn_norm_w_2",
         "gla_w_gate_up_2", "gla_b_gate_2", "gla_norm_w_2", "w_branch_2", "w_out_2", "ln1_g_2", "ln1_b_2",
         "w_router_2", "router_bias_2", "w_gate_2", "w_up_2", "w_down_2", "ln2_g_2", "ln2_b_2")


def kernel(**inputs):
    import concourse.bacc as bacc
    from concourse.bass_utils import run_bass_kernel_spmd

    nc = bacc.Bacc("TRN2", target_bir_lowering=False, num_devices=1)
    arrays = {f"in_{name}": np.ascontiguousarray(inputs[name]) for name in NAMES}
    arrays["in_constants"] = np.ascontiguousarray(np.concatenate(list(constants().values()), axis=1))
    args = {k[3:]: nc.dram_tensor(k, a.shape, mybir.dt.from_np(a.dtype), kind="ExternalInput").ap()
            for k, a in arrays.items()}
    out = nc.dram_tensor("out", (1, S, D), FP, kind="ExternalOutput").ap()
    program(nc, args, out)
    result = run_bass_kernel_spmd(nc, [arrays], core_ids=[0])
    return result.results[0]["out"]
```
